# Optimizing a Trainium2 kernel written in Bass

```python
import jax, jax.numpy as jnp
from jax import lax
import numpy as np

D_MODEL = 1024
BATCH = 1
SEQ = 256
DEPTH = 1

GRID_W = 64
CTX_LEN = 256
HGRN_HEADS = 8
HGRN_EXPAND = 128
HGRN_DIM = HGRN_HEADS * HGRN_EXPAND
HGRN_HEAD_V = HGRN_DIM // HGRN_HEADS
CONV_DIM = D_MODEL
CONV_WIDTH = 31
FFN_DIM = 2816
N_MOD = 9
IN_COLS = 5 * HGRN_DIM + 2 * CONV_DIM
EPS = 1e-6

kernel_name = "hybrid_hgrn2_conformer_dit_block"

def rms_norm(x, gain):
    x32 = x.astype(jnp.float32)
    y = x32 * lax.rsqrt(jnp.mean(x32 * x32, axis=-1, keepdims=True) + EPS)
    return y.astype(x.dtype) * gain

def layer_norm(x, gain, bias):
    x32 = x.astype(jnp.float32)
    mu = jnp.mean(x32, axis=-1, keepdims=True)
    var = jnp.mean(jnp.square(x32 - mu), axis=-1, keepdims=True)
    y = (x32 - mu) * lax.rsqrt(var + EPS)
    return y.astype(x.dtype) * gain + bias

def modulate(x, shift, scale):
    return x * (1.0 + scale) + shift

def swiglu(u, w_up, w_down):
    a, b = jnp.split(u @ w_up, 2, axis=-1)
    return (jax.nn.silu(a) * b) @ w_down

def ffn_sublayer(h, gain, w_up, w_down, shift, scale, gate):
    return h + 0.5 * gate * swiglu(modulate(rms_norm(h, gain), shift, scale), w_up, w_down)

def to_heads(t):
    b, n, _ = t.shape
    return t.reshape(b, n, HGRN_HEADS, -1).transpose(0, 2, 1, 3)

def chunk_scan(q, f, v, s0):
    b, nh, n, dk = q.shape
    dv = v.shape[-1]
    rows = n // GRID_W
    k = 1.0 - f
    g = jnp.log(f)

    def chunks(t):
        return jnp.moveaxis(t.reshape(b, nh, rows, GRID_W, t.shape[-1]), 2, 0)

    causal = jnp.tril(jnp.ones((GRID_W, GRID_W), dtype=bool))[:, :, None]

    def step(S, inp):
        qc, kc, vc, gc = inp
        G = jnp.cumsum(gc, axis=-2)
        diff = G[..., :, None, :] - G[..., None, :, :]
        decay = jnp.exp(jnp.where(causal, diff, -jnp.inf))
        A = jnp.einsum('bhtd,bhsd,bhtsd->bhts', qc, kc, decay)
        o = jnp.einsum('bhts,bhse->bhte', A, vc) + jnp.einsum('bhtd,bhde->bhte', qc * jnp.exp(G), S)
        G_end = G[..., -1, :]
        S = jnp.exp(G_end)[..., :, None] * S + jnp.einsum(
            'bhsd,bhse->bhde', kc * jnp.exp(G_end[..., None, :] - G), vc)
        return S, o

    S_fin, o = lax.scan(step, s0, (chunks(q), chunks(k), chunks(v), chunks(g)))
    o = jnp.moveaxis(o, 0, 2).reshape(b, nh, n, dv)
    return o, S_fin

def hgrn2_bidir(q, zf, zb, v, lb_f, lb_b, sf0, sb0):
    qh = to_heads(jax.nn.silu(q)).astype(jnp.float32)
    vh = to_heads(v).astype(jnp.float32)
    lbf = lb_f.reshape(HGRN_HEADS, 1, HGRN_EXPAND)
    lbb = lb_b.reshape(HGRN_HEADS, 1, HGRN_EXPAND)
    ff = lbf + (1.0 - lbf) * jax.nn.sigmoid(to_heads(zf).astype(jnp.float32))
    fb = lbb + (1.0 - lbb) * jax.nn.sigmoid(to_heads(zb).astype(jnp.float32))
    o_f, sf = chunk_scan(qh, ff, vh, sf0)
    flip = lambda t: jnp.flip(t, axis=2)
    o_b, sb = chunk_scan(flip(qh), flip(fb), flip(vh), sb0)
    return o_f + flip(o_b), sf, sb

def mixer_scan(u, w_in, lb_f, lb_b, sf0, sb0):
    proj = u @ w_in
    q, zf, zb, v, gout, glu = jnp.split(
        proj, [HGRN_DIM, 2 * HGRN_DIM, 3 * HGRN_DIM, 4 * HGRN_DIM, 5 * HGRN_DIM], axis=-1)
    o, sf, sb = hgrn2_bidir(q, zf, zb, v, lb_f, lb_b, sf0, sb0)
    return o, gout, glu, sf, sb

def depthwise_conv(x, w, bias):
    pad = CONV_WIDTH // 2
    y = lax.conv_general_dilated(
        x, w[:, None, :].astype(x.dtype), window_strides=(1,), padding=[(pad, pad)],
        dimension_numbers=('NWC', 'WIO', 'NWC'), feature_group_count=x.shape[-1])
    return y + bias

def mixer_merge(u, o, gout, glu, hgrn_norm, w_proj_a, w_dw, b_dw, ln_g, ln_b, w_proj_b, w_gate, b_gate, w_o):
    b, n, _ = u.shape
    oa = rms_norm(o, hgrn_norm).transpose(0, 2, 1, 3).reshape(b, n, HGRN_DIM).astype(u.dtype)
    y_a = (oa * jax.nn.silu(gout)) @ w_proj_a
    ga, gb = jnp.split(glu, 2, axis=-1)
    hb = depthwise_conv(ga * jax.nn.sigmoid(gb), w_dw, b_dw)
    y_b = jax.nn.silu(layer_norm(hb, ln_g, ln_b)) @ w_proj_b
    gate_a, gate_b = jnp.split(jax.nn.sigmoid(u @ w_gate + b_gate), 2, axis=-1)
    return (gate_a * y_a + gate_b * y_b) @ w_o

def setup_inputs(seed: int = 0) -> dict:
    key = jax.random.key(seed)
    ks = jax.random.split(key, 32)
    nrm = lambda k, shape, s: jax.random.normal(k, shape, jnp.float32) * s
    D, L = D_MODEL, DEPTH
    lb_base = jnp.linspace(-1.0, 1.0, L + 1, dtype=jnp.float32)[:, None, None]
    return {
        "x": nrm(ks[0], (BATCH, SEQ, D), 1.0),
        "c": nrm(ks[1], (BATCH, D), 1.0),
        "ctx": nrm(ks[2], (BATCH, CTX_LEN, D), 1.0),
        "c_ctx": nrm(ks[3], (D,), 1.0),
        "w_ada": nrm(ks[4], (L, D, N_MOD * D), D ** -0.5),
        "b_ada": nrm(ks[5], (L, N_MOD * D), 0.02),
        "norm_ffn1": 1.0 + nrm(ks[6], (L, D), 0.05),
        "w_ffn1_up": nrm(ks[7], (L, D, 2 * FFN_DIM), D ** -0.5),
        "w_ffn1_down": nrm(ks[8], (L, FFN_DIM, D), FFN_DIM ** -0.5),
        "norm_mix": 1.0 + nrm(ks[9], (L, D), 0.05),
        "w_in": nrm(ks[10], (L, D, IN_COLS), D ** -0.5),
        "lb_logits": lb_base + nrm(ks[11], (L + 1, 2, HGRN_DIM), 0.1),
        "hgrn_norm": 1.0 + nrm(ks[12], (L, HGRN_HEAD_V), 0.05),
        "w_dw": nrm(ks[13], (L, CONV_WIDTH, CONV_DIM), CONV_WIDTH ** -0.5),
        "b_dw": nrm(ks[14], (L, CONV_DIM), 0.02),
        "conv_ln_g": 1.0 + nrm(ks[15], (L, CONV_DIM), 0.05),
        "conv_ln_b": nrm(ks[16], (L, CONV_DIM), 0.02),
        "w_proj_a": nrm(ks[17], (L, HGRN_DIM, D), HGRN_DIM ** -0.5),
        "w_proj_b": nrm(ks[18], (L, CONV_DIM, D), CONV_DIM ** -0.5),
        "w_gate": nrm(ks[19], (L, D, 2 * D), D ** -0.5),
        "b_gate": nrm(ks[20], (L, 2 * D), 0.02),
        "w_o": nrm(ks[21], (L, D, D), D ** -0.5),
        "norm_ffn2": 1.0 + nrm(ks[22], (L, D), 0.05),
        "w_ffn2_up": nrm(ks[23], (L, D, 2 * FFN_DIM), D ** -0.5),
        "w_ffn2_down": nrm(ks[24], (L, FFN_DIM, D), FFN_DIM ** -0.5),
        "final_norm": 1.0 + nrm(ks[25], (D,), 0.05),
    }

def reference(x, c, ctx, c_ctx, w_ada, b_ada, norm_ffn1, w_ffn1_up, w_ffn1_down, norm_mix, w_in,
              lb_logits, hgrn_norm, w_dw, b_dw, conv_ln_g, conv_ln_b, w_proj_a, w_proj_b, w_gate,
              b_gate, w_o, norm_ffn2, w_ffn2_up, w_ffn2_down, final_norm):
    b = x.shape[0]
    lb_all = jnp.cumsum(jax.nn.softmax(lb_logits.astype(jnp.float32), axis=0), axis=0)
    h, hc = x, ctx
    for l in range(DEPTH):
        last = l == DEPTH - 1
        m = jnp.split((jax.nn.silu(c) @ w_ada[l] + b_ada[l])[:, None, :], N_MOD, axis=-1)
        mc = jnp.split((jax.nn.silu(c_ctx) @ w_ada[l] + b_ada[l])[None, None, :], N_MOD, axis=-1)
        lb_f, lb_b = lb_all[l, 0], lb_all[l, 1]
        mix_w = (hgrn_norm[l], w_proj_a[l], w_dw[l], b_dw[l], conv_ln_g[l], conv_ln_b[l],
                 w_proj_b[l], w_gate[l], b_gate[l], w_o[l])
        h = ffn_sublayer(h, norm_ffn1[l], w_ffn1_up[l], w_ffn1_down[l], m[0], m[1], m[2])
        hc = ffn_sublayer(hc, norm_ffn1[l], w_ffn1_up[l], w_ffn1_down[l], mc[0], mc[1], mc[2])
        u = modulate(rms_norm(h, norm_mix[l]), m[3], m[4])
        uc = modulate(rms_norm(hc, norm_mix[l]), mc[3], mc[4])
        zeros = jnp.zeros((b, HGRN_HEADS, HGRN_EXPAND, HGRN_HEAD_V), jnp.float32)
        oc, goc, gluc, sf, sb = mixer_scan(uc, w_in[l], lb_f, lb_b, zeros, zeros)
        o, go, glu, _, _ = mixer_scan(u, w_in[l], lb_f, lb_b, sf, sb)
        h = h + m[5] * mixer_merge(u, o, go, glu, *mix_w)
        h = ffn_sublayer(h, norm_ffn2[l], w_ffn2_up[l], w_ffn2_down[l], m[6], m[7], m[8])
        if not last:
            hc = hc + mc[5] * mixer_merge(uc, oc, goc, gluc, *mix_w)
            hc = ffn_sublayer(hc, norm_ffn2[l], w_ffn2_up[l], w_ffn2_down[l], mc[6], mc[7], mc[8])
    return rms_norm(h, final_norm)


_drawn_inputs = setup_inputs


def setup_inputs(seed=0):
    import zlib

    import numpy as np

    out = dict(_drawn_inputs(seed))
    spreads = {}
    factors = {'ctx': 8.0,
     'c_ctx': 8.0,
     'norm_mix': 2.928,
     'hgrn_norm': 4.674,
     'b_dw': 8.0,
     'conv_ln_g': 16.849,
     'conv_ln_b': 42.33,
     'b_gate': 8.0,
     'norm_ffn2': 3.007}
    for name, (base, spread) in spreads.items():
        noise = np.random.default_rng([zlib.crc32(name.encode()), seed]).standard_normal(out[name].shape)
        drawn = base * np.exp(spread * noise) if base else spread * noise
        out[name] = __import__('jax').numpy.asarray(drawn.astype(out[name].dtype))
    for name, factor in factors.items():
        out[name] = (out[name] * factor).astype(out[name].dtype)
    return out
```

```python
from contextlib import ExitStack

import numpy as np

import concourse.bass as bass
from concourse import mybir

F32 = mybir.dt.float32
F32R = mybir.dt.float32r
U8 = mybir.dt.uint8
ACT = mybir.ActivationFunctionType
ALU = mybir.AluOpType
AX = mybir.AxisListType

P = 128
D = 1024
KC = D // P
T = 256
F = 2816
FC = F // P
HEADS = 8
TAPS = 31
PAD = TAPS // 2
GLUW = T + 2 * PAD
ADA = 72
EPS = 1e-6
HG = 4

V_N1, V_NM, V_N2, V_NF = 0, 8, 16, 24
V_BADA, V_BGATE, V_LB, V_HN = 32, 104, 120, 152
V_BDW, V_LNG, V_LNB, V_END = 153, 161, 169, 177

UP1, DOWN1, GLU, VV, ZZ, QQ, GO, PB, PA, WO, UP2, DOWN2, UNITS = (
    0, 44, 68, 84, 92, 108, 116, 124, 140, 156, 164, 208, 232)
(G_UP1, G_DOWN1, G_GLU, G_V, G_Z, G_Q, G_GO, G_PB, G_PA, G_WO, G_UP2, G_DOWN2) = (
    0, 22, 30, 38, 40, 56, 64, 72, 80, 88, 96, 118)
DOWN_K = (8, 8, 6)
ADA_FIRST = 16
ADA_UP = 44
SPLIT_POOL = (VV, QQ)


def layer(nc, d):
    with ExitStack() as ctx:
        def sem(name):
            return ctx.enter_context(nc.semaphore(name))

        base = (nc.sbuf_base + 31) // 32 * 32
        slab = ctx.enter_context(nc.sbuf_tensor("slab", [P, (nc.sbuf_usable_end - base) // 4 - 16], F32))

        def at(name, shape, offset, dt=F32):
            return nc.alloc_sbuf_tensor_at(name, [P, *shape], dt, offset=base + offset)

        KB = 1024
        h = at("h", [2, KC, T], 0)
        uh = at("uh", [2, KC, T], 16 * KB, F32R)
        ul = at("ul", [2, KC, T], 32 * KB, F32R)
        raw = at("raw", [4, 8, P], 48 * KB)
        wh = at("wh", [4, 8, P], 64 * KB, F32R)
        wl = at("wl", [4, 8, P], 80 * KB, F32R)
        M = 96 * KB
        ada_first = at("ada_first", [ADA_FIRST, KC, P], M)
        act_h = at("act_h", [FC, 2, T], M, F32R)
        act_l = at("act_l", [FC, 2, T], M + 44 * KB, F32R)
        act2_h = at("act2_h", [FC, T], M, F32R)
        act2_l = at("act2_l", [FC, T], M + 22 * KB, F32R)
        ada_ring = at("ada_ring", [2, KC, P], M + 88 * KB)
        q = at("q", [HEADS, T], M)
        khat = at("khat", [2, HG, T], M)
        kdec = at("kdec", [2, HEADS, T], M + 8 * KB)
        Q = at("Q", [2, HEADS, T], M + 8 * KB)
        K = at("K", [2, HEADS, T], M + 24 * KB)
        tot1 = [at(f"tot1_{g}", [2, HG, T], M + (40 + 8 * g) * KB) for g in range(2)]
        v = at("v", [4, D], M + 56 * KB)
        state = at("state", [HEADS, 2, P], M + 72 * KB)
        glu = at("glu", [KC, GLUW], M + 72 * KB)
        gout = at("gout", [HEADS, T], M + 80 * KB)
        lnsq = at("lnsq", [KC, T], M + 80 * KB)
        tot2 = at("tot2", [2, 2, HG, T // 2], M + 88 * KB)
        dec = at("dec", [2, 2, T], M + 88 * KB)
        ident = at("ident", [P], M + 92 * KB)
        masks_f = at("masks_f", [7, P], M + 92 * KB + 512)
        zh = at("zh", [KC, T], M + 40 * KB, F32R)
        zl = at("zl", [KC, T], M + 48 * KB, F32R)
        ozh = at("ozh", [HEADS, T], M, F32R)
        ozl = at("ozl", [HEADS, T], M + 88 * KB, F32R)
        yh = at("yh", [KC, T], M + 24 * KB, F32R)
        yl = at("yl", [KC, T], M + 32 * KB, F32R)
        orms = at("orms", [HG, T], M + 24 * KB)
        onorm = at("onorm", [HG, T], M + 28 * KB)
        A = [at("A0", [HG, 2, T], 16 * KB), at("A1", [HG, 2, T], 32 * KB)]
        hb = at("hb", [KC, T], 0)
        yb = at("yb", [KC, T], 0)
        ta = at("ta", [2, 512], M + 96 * KB)
        tb = at("tb", [2, 512], M + 100 * KB)
        ssq = at("ssq", [512], M + 104 * KB)
        rstd = at("rstd", [512], M + 106 * KB)
        tot4 = at("tot4", [2, 2, HG, T // 4], M + 104 * KB)
        osq = at("osq", [HG, T], M + 104 * KB)
        S0 = M + 108 * KB
        vecs = at("vecs", [V_END], S0)
        wdw = at("wdw", [TAPS, KC], S0 + 736)
        masks = at("masks", [7, P], S0 + 736, U8)
        mod = at("mod", [ADA, 2], S0 + 1760)
        ones = at("ones", [P], S0 + 2336)
        cvec = at("cvec", [KC, 2], S0 + 2848)
        csil = at("csil", [KC, 2], S0 + 2912)
        scale = at("scale", [3, KC, 2], S0 + 2976)
        half_gate = at("half_gate", [2, KC, 2], S0 + 3168)
        lbt = at("lbt", [6, 16], S0 + 3296)
        eps = at("eps", [1], S0 + 3680)
        ps = ctx.enter_context(nc.psum_tensor("ps", [P, 8, 512], F32))
        dummy = slab

        raw_in = [sem(f"raw_in{i}") for i in range(4)]
        ada_in = [sem(f"ada_in{i}") for i in range(2)]
        ada_first_in = [sem(f"ada_first_in{i}") for i in range(ADA_FIRST // 2)]
        small_in = sem("small_in")
        x_in = sem("x_in")
        ident_in, masks_in, masks_made = sem("ident_in"), sem("masks_in"), sem("masks_made")
        out_sent = sem("out_sent")
        hi_made = sem("hi_made")
        lo_dve, lo_pool = sem("lo_dve"), sem("lo_pool")
        unit_done = sem("unit_done")
        ada_done = sem("ada_done")
        bank_read = sem("bank_read")
        act_made = sem("act_made")
        acth_made, actl_made = sem("acth_made"), sem("actl_made")
        ready = sem("ready")
        csil_made = sem("csil_made")
        exp_made = sem("exp_made")
        chain = sem("chain")
        mod_made = sem("mod_made")
        sq_made, ssq_made = sem("sq_made"), sem("ssq_made")
        stat_made, rms_made, rstd_made = sem("stat_made"), sem("rms_made"), sem("rstd_made")
        t_made = sem("t_made")
        uf_made, uh_made, ul_made = sem("uf_made"), sem("uh_made"), sem("ul_made")
        out_made = sem("out_made")
        conv_step = sem("conv_step")
        z_step = sem("z_step")
        v_copied = sem("v_copied")
        turned, turned_read = sem("turned"), sem("turned_read")
        state_ps, state_made = sem("state_ps"), sem("state_made")
        ln_dve, ln_ps, ln_act = sem("ln_dve"), sem("ln_ps"), sem("ln_act")
        q_first = sem("q_first")
        level_ps = [sem(f"level_ps{g}") for g in range(2)]
        a_act = [sem(f"a_act{g}") for g in range(2)]
        a_dve = [sem(f"a_dve{g}") for g in range(2)]
        khat_made = [sem(f"khat_made{g}") for g in range(2)]
        q_up = [sem(f"q_up{g}") for g in range(2)]
        k_up = [sem(f"k_up{g}") for g in range(2)]
        tot_up = [sem(f"tot_up{g}") for g in range(2)]
        zs_made, zf_made, zh_made, zl_made = sem("zs_made"), sem("zf_made"), sem("zh_made"), sem("zl_made")
        o_ps, osq_made, ostat_ps, orms_made, of_made, ozh_made, ozl_made = (
            sem("o_ps"), sem("osq_made"), sem("ostat_ps"), sem("orms_made"), sem("of_made"),
            sem("ozh_made"), sem("ozl_made"))
        ya_made, yf_made, yh_made, yl_made = sem("ya_made"), sem("yf_made"), sem("yh_made"), sem("yl_made")

        block = ctx.enter_context(nc.Block())

        def lo_wait(eng, n, i=0, per=0):
            a, b = SPLIT_POOL
            if n < a:
                eng.wait_ge(lo_dve, n + 1 + per * i)
            elif n < b:
                eng.wait_ge(lo_pool, n + 1 - a + per * i)
            else:
                eng.wait_ge(lo_dve, n + 1 - (b - a) + per * i)

        def bank(g):
            return 2 * (g % 2)

        def acts(g):
            if g < G_DOWN1:
                return g + 1
            if g < G_GLU:
                return 22
            if g < G_WO:
                return g + 1 - 8
            return g + 1 - 16

        def tot_view(gr, m):
            if m == 1:
                return tot1[gr], 0, HG * T, 2 * HG * T
            t, w = (tot2, HG * T) if m.bit_length() % 2 == 0 else (tot4, HG * T // 2)
            return t, gr * w, HG * T // m, 2 * w

        def tot_halves(gr, m):
            t, o, pl, row = tot_view(gr, m)
            n = HG * T // (2 * m)
            t2, o2, pl2, row2 = tot_view(gr, 2 * m)
            return (bass.AP(t, o, [[row, P], [pl, 2], [2, n]]),
                    bass.AP(t, o + 1, [[row, P], [pl, 2], [2, n]]),
                    bass.AP(t2, o2, [[row2, P], [pl2, 2], [1, n]]))

        def tot_pairs(gr, m, swap):
            t, o, pl, row = tot_view(gr, m)
            n = HG * T // (2 * m)
            if swap:
                return bass.AP(t, o + pl + 1, [[row, P], [2, n], [-pl - 1, 2], [0, m]])
            return bass.AP(t, o + 1, [[row, P], [2, n], [pl - 1, 2], [0, m]])

        def pairs(t, gr, m):
            return bass.AP(t, gr * HG * T, [[2 * HEADS * T, P], [2 * m, HG * T // (2 * m)], [HEADS * T + m, 2], [1, m]])

        def q_pairs(gr, m):
            return pairs(Q, gr, m)

        def k_pairs(gr, m):
            return pairs(K, gr, m)

        def operand(t, head, blk, m):
            o = head * T + blk * P
            return bass.AP(t, o, [[2 * HEADS * T, P], [2 * m, P // (2 * m)], [HEADS * T + m, 2], [1, m]])

        @block.sync
        def _(sp):
            def load(n, src, k=8, i=0, per=0, shape=None):
                if n >= 4:
                    lo_wait(sp, n - 4, i, per)
                dst = raw[:, n % 4, 0:k]
                if shape:
                    dst = dst.rearrange("p k c -> p (k c)").rearrange("p (a b) -> p a b", a=shape)
                sp.dma_start(dst, src).then_inc(raw_in[n % 4], 16)

            def ada(a, i=0, per=0):
                if a >= 2:
                    sp.wait_ge(ada_done, ADA_FIRST + a - 1 + per * i)
                sp.dma_start(ada_ring[:, a % 2], d["ada"][ADA_FIRST + a + per * i] if per == 0 else
                             d["ada"][bass.ds(ADA_FIRST + a + per * i, 1)].rearrange("o p k c -> (o p) k c")
                             ).then_inc(ada_in[a % 2], 16)

            sp.dma_start(cvec[:], d["cvec"]).then_inc(small_in, 16)
            sp.dma_start(vecs[:], d["vecs"]).then_inc(small_in, 16)
            sp.dma_start(wdw[:], d["wdw"]).then_inc(small_in, 16)
            sp.dma_start(h[:, 0], d["ctx"]).then_inc(x_in, 16)
            sp.dma_start(h[:, 1], d["x"]).then_inc(x_in, 16)
            for a in range(0, ADA_FIRST, 2):
                sp.dma_start(ada_first[:, a:a + 2], d["ada"][a:a + 2].rearrange("a p k c -> p a k c")
                             ).then_inc(ada_first_in[a // 2], 16)

            up1 = d["up1"]
            for s in range(4):
                load(s, up1[s])
                ada(s)
            with sp.Fori(0, 10) as i:
                for s in range(4):
                    load(4 + s, up1[bass.ds(4 * i + (4 + s), 1)].rearrange("o p k c -> (o p) k c"), i=i, per=4)
                    ada(4 + s, i, 4)

            def down(first, src, with_ada):
                n, a = first, ADA_UP
                for c in range(KC):
                    k0 = 0
                    for k in DOWN_K:
                        load(n, src[c, :, k0:k0 + k], k)
                        n, k0 = n + 1, k0 + k
                    if with_ada:
                        for _ in range(2 if c % 2 else 1):
                            ada(a)
                            a += 1

            down(DOWN1, d["down1"], True)
            w_in = d["w_in"]
            for c in range(KC):
                load(GLU + 2 * c, w_in[40 + c])
                load(GLU + 2 * c + 1, w_in[48 + c])
            for j in range(8):
                load(VV + j, d["w_v"][j // 4, j % 4], 8, shape=2)
            sp.wait_ge(ada_done, ADA)
            sp.dma_start(ident[:], d["ident"]).then_inc(ident_in, 16)
            sp.dma_start(masks_f[:], d["masks"]).then_inc(masks_in, 16)
            for j in range(16):
                load(ZZ + j, w_in[8 + j])
            for j in range(8):
                load(QQ + j, w_in[j])
            for j in range(8):
                load(GO + j, w_in[32 + j])
            for c in range(KC):
                load(PB + 2 * c, d["gate"][8 + c])
                load(PB + 2 * c + 1, d["proj_b"][c])
            for c in range(KC):
                load(PA + 2 * c, d["gate"][c])
                load(PA + 2 * c + 1, d["proj_a"][c])
            for c in range(KC):
                load(WO + c, d["w_o"][c])
            up2 = d["up2"]
            with sp.Fori(0, 11) as i:
                for s in range(4):
                    load(UP2 + s, up2[bass.ds(4 * i + s, 1)].rearrange("o p k c -> (o p) k c"), i=i, per=4)
            down(DOWN2, d["down2"], False)
            for c in range(KC):
                sp.wait_ge(out_made, c + 1)
                sp.dma_start(d["out"][c], h[:, 1, c]).then_inc(out_sent, 16)
            sp.wait_ge(out_sent, 16 * KC)

        @block.scalar
        def _(act):
            def hi(n, k=8, i=0, per=0):
                act.wait_ge(raw_in[n % 4], 16 * (n // 4 + 1) + 4 * per * i)
                if n >= 4:
                    act.wait_ge(unit_done, n - 3 + per * i)
                nc.scalar.activation(wh[:, n % 4, 0:k], raw[:, n % 4, 0:k], ACT.Copy).then_inc(hi_made, 1)

            def func(g, dst, src, f, i=0, per=0, unit=0, uper=0, sig=act_made, **kw):
                act.wait_ge(unit_done, unit + 1 + uper * i)
                if g >= 2:
                    act.wait_ge(bank_read, g - 1 + per * i)
                nc.scalar.activation(dst, src, f, **kw).then_inc(sig, 1)

            def squares(which, halves, before):
                for c in range(KC):
                    before(c)
                    n = 8 * which + c
                    if c >= 2:
                        act.wait_ge(ssq_made, n - 1)
                    src = h[:, halves, c]
                    dst = ta[:, c % 2, 0:src.shape[1] * T].rearrange("p (a t) -> p a t", t=T)
                    nc.scalar.activation(dst, src, ACT.Square).then_inc(sq_made, 1)
                    yield

            def root(which, w):
                act.wait_ge(stat_made, which + 1)
                nc.scalar.activation(rstd[:, 0:w], ps[:, 7, 0:w], ACT.Sqrt, scale=1.0 / D,
                                     bias=eps[:]).then_inc(rms_made, 1)

            def u_hi(which, halves, w):
                for c in range(KC):
                    act.wait_ge(uf_made, 8 * which + c + 1)
                    nc.scalar.activation(uh[:, halves, c], tb[:, c % 2, 0:w].rearrange("p (a t) -> p a t", t=T),
                                         ACT.Copy).then_inc(uh_made, 1)

            both, lat = slice(0, 2), slice(1, 2)
            act.wait_ge(small_in, 48)
            act.wait_ge(chain, 2)
            nc.scalar.activation(lbt[:, 1:3], lbt[:, 1:3], ACT.Exp).then_inc(exp_made, 1)
            nc.scalar.activation(csil[:], cvec[:], ACT.Silu).then_inc(csil_made, 1)
            act.wait_ge(x_in, 32)
            for _ in squares(0, both, lambda c: None):
                pass
            root(0, 512)
            hi(0)
            hi(1)
            u_hi(0, both, 512)

            nc.scalar.preload_act_table(ACT.Silu)

            def up_body(first, g0, i, per, w, last=False):
                for s in range(2):
                    hi(first + 2 * s + 2, i=i, per=per)
                    hi(first + 2 * s + 3, i=i, per=per)
                    func(g0 + s, ta[:, s, 0:w], ps[:, 2 * s, 0:w], ACT.Silu, i, per // 2,
                         first + 2 * s + 1, per)

            up_body(UP1, G_UP1, 0, 0, 512)
            with act.Fori(0, 10) as i:
                up_body(UP1 + 4, G_UP1 + 2, i, 4, 512)

            def down_body(first, g0, which, halves, ahead):
                n = first + 2
                gen = squares(which, halves, lambda c: act.wait_ge(bank_read, g0 + c + 1))
                for c in range(KC):
                    for k in range(3):
                        if n < ahead:
                            hi(n, DOWN_K[(n - first) % 3] if n < first + 24 else 8)
                            n += 1
                    next(gen)

            down_body(DOWN1, G_DOWN1, 1, both, DOWN1 + 26)
            root(1, 512)
            u_hi(1, both, 512)
            for c in range(KC):
                hi(GLU + 2 * c + 2)
                hi(GLU + 2 * c + 3)
                g = G_GLU + c
                func(g, ta[:, c % 2, 0:T], ps[:, bank(g) + 1, 0:T], ACT.Sigmoid, unit=GLU + 2 * c + 1)
            for c in range(2):
                for j in range(4):
                    hi(VV + 4 * c + j + 2)
                act.wait_ge(unit_done, VV + 4 * c + 4)
                for b in (0, 1):
                    x = nc.scalar.activation(v[:, b, 512 * c:512 * c + 512], ps[:, (4 - 4 * c) + b], ACT.Copy)
                x.then_inc(act_made, 1)
            for j in range(16):
                hi(ZZ + j + 2)
                g = G_Z + j
                func(g, ta[:, j % 2], ps[:, bank(g)], ACT.Sigmoid, unit=ZZ + j)
            for j in range(8):
                hi(QQ + j + 2)
                g = G_Q + j
                func(g, ta[:, j % 2, 0:T], ps[:, bank(g), 0:T], ACT.Sigmoid, unit=QQ + j)
                act.wait_ge(turned, j + 1)
                if j >= 2:
                    act.wait_ge(state_ps, j - 1)
                nc.scalar.activation(tb[:, j % 2], ps[:, 4], ACT.Copy).then_inc(turned_read, 1)
                act.wait_ge(state_ps, j + 1)
                nc.scalar.activation(state[:, j], ps[:, 5, 0:2 * P].rearrange("p (a e) -> p a e", a=2), ACT.Copy,
                                     scale=-1.0).then_inc(state_made, 1)
                if j == 3:
                    act.wait_ge(ln_dve, 3)
                    nc.scalar.activation(lnsq[:], hb[:], ACT.Square).then_inc(ln_act, 1)
                if j == 6:
                    act.wait_ge(ln_ps, 2)
                    nc.scalar.activation(rstd[:, T:2 * T], ps[:, 7, 0:T], ACT.Sqrt, scale=1.0 / D,
                                         bias=eps[:]).then_inc(ln_act, 1)

            def a_copy(gr, level):
                act.wait_ge(level_ps[gr], level + 1)
                x = ps[:, 4 + 2 * gr:6 + 2 * gr].rearrange("p a (h b t) -> p (a h) b t", h=2, b=2)
                for b in range(2):
                    c = b if level == 0 else 1 - b
                    y = nc.scalar.activation(A[gr][:, :, b, P * c:P * c + P], x[:, :, b], ACT.Copy)
                y.then_inc(a_act[gr], 1)

            def keys(gr, level):
                m = 1 << (level - 1)
                act.wait_ge(level_ps[gr], level)
                if level > 1:
                    act.wait_ge(k_up[gr], level - 1)
                nc.scalar.activation(khat[:, gr].rearrange("p h t -> p (h t)").rearrange(
                    "p (n a m) -> p n a m", a=2, m=m), k_pairs(gr, m), ACT.Copy).then_inc(khat_made[gr], 1)

            def scan_step(gr, level):
                if level == 0:
                    a_copy(gr, 0)
                if level < 7:
                    keys(gr, level + 1)
                if level == 8:
                    a_copy(gr, 8)

            def z_act(c):
                act.wait_ge(ln_dve, 8)
                if c >= 2:
                    act.wait_ge(zl_made, c - 1)
                nc.scalar.activation(tb[:, c % 2, 0:T], hb[:, c], ACT.Sigmoid, scale=vecs[:, V_LNG + c:V_LNG + c + 1],
                                     bias=vecs[:, V_LNB + c:V_LNB + c + 1]).then_inc(zs_made, 1)
                act.wait_ge(zf_made, c + 1)
                nc.scalar.activation(zh[:, c], tb[:, c % 2, T:2 * T], ACT.Copy).then_inc(zh_made, 1)

            queue = [(gr, level) for level in range(9) for gr in range(2)]
            for j in range(8):
                hi(GO + j + 2)
                g = G_GO + j
                func(g, ta[:, j % 2, 0:T], ps[:, bank(g), 0:T], ACT.Sigmoid, unit=GO + j)
                scan_step(*queue.pop(0))
                if j >= 4:
                    z_act(2 * j - 8)
                    z_act(2 * j - 7)
            def pair(first, g0, c, bias):
                hi(first + 2 * c + 2)
                hi(first + 2 * c + 3)
                g = g0 + c
                func(g, ta[:, c % 2, 0:T], ps[:, bank(g), 0:T], ACT.Sigmoid, unit=first + 2 * c + 1,
                     bias=vecs[:, bias + c:bias + c + 1])

            for c in range(KC):
                pair(PB, G_PB, c, V_BGATE + 8)
                for _ in range(2):
                    if queue:
                        scan_step(*queue.pop(0))
            for b in range(2):
                act.wait_ge(o_ps, b + 1)
                if b:
                    act.wait_ge(ostat_ps, b)
                nc.scalar.activation(osq[:].rearrange("p (a h) t -> p a (h t)", a=2), ps[:, 4 + 2 * b:6 + 2 * b],
                                     ACT.Square).then_inc(osq_made, 1)
                act.wait_ge(ostat_ps, b + 1)
                if b:
                    act.wait_ge(ozl_made, b)
                nc.scalar.activation(orms[:].rearrange("p (a h) t -> p a (h t)", a=2),
                                     ps[:, 6 - 2 * b:8 - 2 * b], ACT.Sqrt, scale=1.0 / P,
                                     bias=eps[:]).then_inc(orms_made, 1)
                act.wait_ge(of_made, b + 1)
                nc.scalar.activation(ozh[:, HG * b:HG * b + HG], onorm[:], ACT.Copy).then_inc(ozh_made, 1)
            for c in range(KC):
                pair(PA, G_PA, c, V_BGATE)
                act.wait_ge(yf_made, c + 1)
                nc.scalar.activation(yh[:, c], tb[:, c % 2, 0:T], ACT.Copy).then_inc(yh_made, 1)
            gen = squares(2, lat, lambda c: act.wait_ge(bank_read, G_WO + c + 1))
            for c in range(KC):
                hi(WO + c + 2)
                next(gen)
            root(2, T)
            u_hi(2, lat, T)
            nc.scalar.preload_act_table(ACT.Silu)
            with act.Fori(0, 11) as i:
                up_body(UP2, G_UP2, i, 4, T)
            down_body(DOWN2, G_DOWN2, 3, lat, UNITS)
            root(3, T)

        @block.gpsimd
        def _(pool):
            nc.gpsimd.memset(ones[:], 1.0).then_inc(ready, 1)
            nc.gpsimd.memset(eps[:], EPS).then_inc(ready, 1)

            def sums(which, w):
                for c in range(KC):
                    n = 8 * which + c
                    pool.wait_ge(sq_made, n + 1)
                    if c:
                        pool.wait_ge(ssq_made, n)
                        nc.gpsimd.tensor_tensor(ssq[:, 0:w], ssq[:, 0:w], ta[:, c % 2, 0:w],
                                                ALU.add).then_inc(ssq_made, 1)
                    else:
                        nc.gpsimd.tensor_copy(ssq[:, 0:w], ta[:, 0, 0:w]).then_inc(ssq_made, 1)

            def u_lo(which, halves, w):
                for c in range(KC):
                    pool.wait_ge(uh_made, 8 * which + c + 1)
                    nc.gpsimd.tensor_tensor(ul[:, halves, c], tb[:, c % 2, 0:w].rearrange("p (a t) -> p a t", t=T),
                                            uh[:, halves, c].bitcast(F32), ALU.subtract).then_inc(ul_made, 1)

            both, lat = slice(0, 2), slice(1, 2)
            sums(0, 512)
            u_lo(0, both, 512)
            sums(1, 512)
            u_lo(1, both, 512)
            pool.wait_ge(unit_done, DOWN1 + 24)
            nc.gpsimd.memset(glu[:, :, 0:PAD], 0.0)
            nc.gpsimd.memset(glu[:, :, PAD + T:GLUW], 0.0).then_inc(ready, 1)
            pool.wait_ge(ada_done, ADA)
            nc.gpsimd.memset(dec[:, 0, :, T - 1:T], 1.0)
            nc.gpsimd.memset(dec[:, 1, :, 0:1], 1.0).then_inc(ready, 1)
            for n in range(*SPLIT_POOL):
                pool.wait_ge(hi_made, n + 1)
                nc.gpsimd.tensor_tensor(wl[:, n % 4], raw[:, n % 4], wh[:, n % 4].bitcast(F32),
                                        ALU.subtract).then_inc(lo_pool, 1)

            pool.wait_ge(conv_step, KC * TAPS)
            pool.wait_ge(masks_in, 16)
            nc.gpsimd.tensor_copy(masks[:], masks_f[:]).then_inc(masks_made, 1)
            pool.wait_ge(masks_made, 1)
            for level in range(1, 8):
                m = 1 << (level - 1)
                for gr in range(2):
                    if level == 1:
                        pool.wait_ge(q_first, gr + 1)
                    pool.wait_ge(khat_made[gr], level)
                    if level > 1:
                        pool.wait_ge(tot_up[gr], level - 1)
                        pool.wait_ge(k_up[gr], level - 1)
                        pool.wait_ge(q_up[gr], level - 1)
                    tk = tot_pairs(gr, m, swap=True)
                    x = k_pairs(gr, m)
                    nc.gpsimd.tensor_tensor(x, x, tk, ALU.mult).then_inc(k_up[gr], 1)
                    even, odd, dst = tot_halves(gr, m)
                    nc.gpsimd.tensor_tensor(dst, even, odd, ALU.mult).then_inc(tot_up[gr], 1)
            sums(2, T)
            u_lo(2, lat, T)
            sums(3, T)

        @block.vector
        def _(dve):
            links = [0]

            def link(ins):
                links[0] += 1
                ins.then_inc(chain, 1)
                dve.wait_ge(chain, links[0])

            def lo(n, k=8, i=0, per=0):
                dve.wait_ge(hi_made, n + 1 + per * i)
                nc.vector.tensor_tensor(wl[:, n % 4, 0:k], raw[:, n % 4, 0:k], wh[:, n % 4, 0:k].bitcast(F32),
                                        ALU.subtract).then_inc(lo_dve, 1)

            def col(o):
                return vecs[:, o:o + 1]

            dve.wait_ge(small_in, 48)
            l0, l1 = vecs[:, V_LB:V_LB + 16], vecs[:, V_LB + 16:V_LB + 32]
            link(nc.vector.tensor_tensor(lbt[:, 0], l0, l1, ALU.max))
            nc.vector.tensor_tensor(lbt[:, 1], l0, lbt[:, 0], ALU.subtract)
            link(nc.vector.tensor_tensor(lbt[:, 2], l1, lbt[:, 0], ALU.subtract))
            dve.wait_ge(exp_made, 1)
            link(nc.vector.tensor_tensor(lbt[:, 3], lbt[:, 1], lbt[:, 2], ALU.add))
            link(nc.vector.reciprocal(lbt[:, 0], lbt[:, 3]))
            link(nc.vector.tensor_tensor(lbt[:, 4], lbt[:, 1], lbt[:, 0], ALU.mult))
            link(nc.vector.tensor_scalar(lbt[:, 5], lbt[:, 4], -1.0, 1.0, ALU.mult, ALU.add))

            def modulation(a, b, bk):
                src = ps[:, bk, 0:2 * (b - a)].rearrange("p (a t) -> p a t", t=2)
                bias = vecs[:, V_BADA + a:V_BADA + b].unsqueeze(2).to_broadcast([P, b - a, 2])
                link(nc.vector.tensor_tensor(mod[:, a:b], src, bias, ALU.add))

            def gain(which, m, norm):
                g = vecs[:, norm:norm + 8].unsqueeze(2).to_broadcast([P, KC, 2])
                link(nc.vector.scalar_tensor_tensor(scale[:, which], mod[:, 8 * m:8 * m + 8], 1.0, g, ALU.add, ALU.mult))

            def half(which, m):
                link(nc.vector.tensor_scalar(half_gate[:, which], mod[:, 8 * m:8 * m + 8], 0.5, None, ALU.mult))

            def normed(which, halves, w, shift):
                dve.wait_ge(rms_made, which + 1)
                nc.vector.reciprocal(rstd[:, 0:w], rstd[:, 0:w]).then_inc(rstd_made, 1)
                dve.wait_ge(rstd_made, which + 1)
                hv = range(*halves.indices(2))
                for c in range(KC):
                    n = 8 * which + c
                    if c >= 2:
                        dve.wait_ge(ul_made, n - 1)
                    nc.vector.tensor_tensor(ta[:, c % 2, 0:w].rearrange("p (a t) -> p a t", t=T), h[:, halves, c],
                                            rstd[:, 0:w].rearrange("p (a t) -> p a t", t=T), ALU.mult
                                            ).then_inc(t_made, 1)
                    dve.wait_ge(t_made, n + 1)
                    for j, s in enumerate(hv):
                        x = nc.vector.tensor_scalar(tb[:, c % 2, j * T:j * T + T], ta[:, c % 2, j * T:j * T + T],
                                                    scale[:, which, c, s:s + 1],
                                                    mod[:, 8 * shift + c, s:s + 1], ALU.mult, ALU.add)
                    x.then_inc(uf_made, 1)

            both, lat = slice(0, 2), slice(1, 2)
            dve.wait_ge(ada_done, ADA_FIRST)
            modulation(0, ADA_FIRST, 4)
            gain(0, 1, V_N1)
            normed(0, both, 512, 0)
            lo(0)
            lo(1)

            def up_body(first, g0, j0, i, per, w, ah, al, js):
                gp = per // 2
                for s in range(2):
                    lo(first + 2 * s + 2, i=i, per=per)
                    lo(first + 2 * s + 3, i=i, per=per)
                    g = g0 + s
                    dve.wait_ge(act_made, acts(g) + gp * i)
                    nc.vector.tensor_tensor(tb[:, s, 0:w], ta[:, s, 0:w], ps[:, 2 * s + 1, 0:w],
                                            ALU.mult).then_inc(bank_read, 1)
                    dve.wait_ge(bank_read, g + 1 + gp * i)
                    j = js + j0 + s
                    at_j = j0 + s + gp * i
                    hj = ah[:, bass.ds(at_j, 1)] if per else ah[:, at_j:at_j + 1]
                    lj = al[:, bass.ds(at_j, 1)] if per else al[:, at_j:at_j + 1]
                    f = tb[:, s, 0:w].unsqueeze(1)
                    nc.vector.tensor_copy(hj, f).then_inc(acth_made, 1)
                    dve.wait_ge(acth_made, j + 1 + gp * i)
                    nc.vector.tensor_tensor(lj, f, hj.bitcast(F32), ALU.subtract).then_inc(actl_made, 1)

            ah, al = (x[:].rearrange("p f a t -> p f (a t)") for x in (act_h, act_l))
            up_body(UP1, G_UP1, 0, 0, 0, 512, ah, al, 0)
            with dve.Fori(0, 10) as i:
                up_body(UP1 + 4, G_UP1 + 2, 2, i, 4, 512, ah, al, 0)

            dve.wait_ge(ada_done, ADA_FIRST + ADA_UP)
            modulation(ADA_FIRST, ADA_FIRST + ADA_UP, 5)
            half(0, 2)
            gain(1, 4, V_NM)

            def down_body(first, g0, which, halves, ahead):
                n = first + 2
                for c in range(KC):
                    for k in range(3):
                        if n < ahead:
                            lo(n, DOWN_K[(n - first) % 3] if n < first + 24 else 8)
                            n += 1
                    g = g0 + c
                    dve.wait_ge(unit_done, first + 3 * c + 3)
                    for j, s in enumerate(range(*halves.indices(2))):
                        x = nc.vector.scalar_tensor_tensor(h[:, s, c], ps[:, bank(g), j * T:j * T + T],
                                                           half_gate[:, which, c, s:s + 1], h[:, s, c],
                                                           ALU.mult, ALU.add)
                    x.then_inc(bank_read, 1)

            down_body(DOWN1, G_DOWN1, 0, both, DOWN1 + 26)
            dve.wait_ge(ada_done, ADA)
            modulation(ADA_FIRST + ADA_UP, ADA, 6)
            gain(2, 7, V_N2)
            half(1, 8)
            normed(1, both, 512, 3)

            dve.wait_ge(ready, 4)
            for c in range(KC):
                if c < 7:
                    lo(GLU + 2 * c + 2)
                    lo(GLU + 2 * c + 3)
                g = G_GLU + c
                dve.wait_ge(act_made, acts(g))
                nc.vector.tensor_tensor(glu[:, c, PAD:PAD + T], ps[:, bank(g), 0:T], ta[:, c % 2, 0:T],
                                        ALU.mult).then_inc(bank_read, 1)

            steps = [(c, tap) for c0 in range(0, KC, 2) for tap in range(TAPS) for c in (c0, c0 + 1)]
            done = [0]

            def convolve(count):
                for _ in range(count):
                    if done[0] == len(steps):
                        return
                    c, tap = steps[done[0]]
                    src = glu[:, c, tap:tap + T]
                    w = wdw[:, tap, c:c + 1]
                    if tap == 0:
                        if done[0] == 0:
                            dve.wait_ge(bank_read, G_V)
                        x = nc.vector.tensor_scalar(hb[:, c], src, w, col(V_BDW + c), ALU.mult, ALU.add)
                    else:
                        dve.wait_ge(conv_step, done[0] - 1)
                        x = nc.vector.scalar_tensor_tensor(hb[:, c], src, w, hb[:, c], ALU.mult, ALU.add)
                    x.then_inc(conv_step, 1)
                    done[0] += 1

            for c in range(2):
                convolve(58)
                dve.wait_ge(act_made, acts(G_V + c))
                for b in (2, 3):
                    x = nc.vector.tensor_copy(v[:, b, 512 * c:512 * c + 512], ps[:, (4 - 4 * c) + b])
                x.then_inc(bank_read, 1)

            for j in range(16):
                way, hd = divmod(j, HEADS)
                gr, hl = divmod(hd, HG)
                g = G_Z + j
                lb, oml = lbt[:, 4, j:j + 1], lbt[:, 5, j:j + 1]
                dve.wait_ge(act_made, acts(g))
                f = kdec[:, way, hd]
                nc.vector.tensor_scalar(f, ta[:, j % 2, 0:T], oml, lb, ALU.mult, ALU.add).then_inc(z_step, 1)
                fl = tot1[gr][:, 1 - way, hl]
                nc.vector.tensor_scalar(fl, ta[:, j % 2, T:2 * T], oml, lb, ALU.mult, ALU.add).then_inc(bank_read, 1)
                dve.wait_ge(z_step, 3 * j + 1)
                if way == 0:
                    dst, src = dec[:, 0, j % 2, T - 2::-1], f[:, T - 1:0:-1]
                else:
                    dst, src = dec[:, 1, j % 2, 1:T], f[:, 0:T - 1]
                nc.vector.tensor_tensor_scan(dst, src, src, 1.0, ALU.mult, ALU.bypass).then_inc(z_step, 1)
                dve.wait_ge(bank_read, g + 1)
                nc.vector.tensor_scalar(K[:, way, hd], fl, -1.0, 1.0, ALU.mult, ALU.add)
                dve.wait_ge(z_step, 3 * j + 2)
                nc.vector.scalar_tensor_tensor(f, f, -1.0, dec[:, way, j % 2], ALU.add, ALU.mult).then_inc(z_step, 1)
                convolve(9)
                if j >= 14:
                    lo(QQ + j - 14)
            convolve(KC * TAPS)

            per_token = hb[:].rearrange("p c t -> p t c")
            bcast = lambda x: x.unsqueeze(1).to_broadcast([P, KC, T])
            dve.wait_ge(conv_step, KC * TAPS)
            for j in range(8):
                lo(QQ + j + 2)
                g = G_Q + j
                dve.wait_ge(act_made, acts(g))
                nc.vector.tensor_tensor(q[:, j], ps[:, bank(g), 0:T], ta[:, j % 2, 0:T], ALU.mult).then_inc(bank_read, 1)
                if j == 0:
                    nc.vector.tensor_reduce(ssq[:, 0:T], per_token, AX.X, ALU.add).then_inc(ln_dve, 1)
                if j == 2:
                    dve.wait_ge(ln_ps, 1)
                    nc.vector.tensor_scalar(rstd[:, 0:T], ps[:, 6, 0:T], 1.0 / D, None, ALU.mult).then_inc(ln_dve, 1)
                    dve.wait_ge(ln_dve, 2)
                    nc.vector.tensor_tensor(hb[:], hb[:], bcast(rstd[:, 0:T]), ALU.subtract).then_inc(ln_dve, 1)
                if j == 4:
                    dve.wait_ge(ln_act, 1)
                    nc.vector.tensor_reduce(ssq[:, T:2 * T], lnsq[:].rearrange("p c t -> p t c"), AX.X,
                                            ALU.add).then_inc(ln_dve, 1)
                if j == 6:
                    dve.wait_ge(ln_act, 2)
                    nc.vector.reciprocal(rstd[:, T:2 * T], rstd[:, T:2 * T]).then_inc(ln_dve, 1)
                    dve.wait_ge(ln_dve, 5)
                    nc.vector.tensor_tensor(hb[:], hb[:], bcast(rstd[:, T:2 * T]), ALU.mult).then_inc(ln_dve, 1)

            dve.wait_ge(bank_read, G_GO)
            dve.wait_ge(turned, HEADS)
            for gr in range(2):
                qv = q[:, HG * gr:HG * gr + HG].rearrange("p h t -> p (h t)").unsqueeze(1).to_broadcast([P, 2, HG * T])
                nc.vector.tensor_tensor(Q[:, :, HG * gr:HG * gr + HG].rearrange("p a h t -> p a (h t)"),
                                        tot1[gr][:].rearrange("p a h t -> p a (h t)"), qv,
                                        ALU.mult).then_inc(q_first, 1)
            nc.vector.tensor_copy(lbt[:, 0], lbt[:, 1]).then_inc(ln_dve, 1)
            dve.wait_ge(ln_dve, 7)
            nc.vector.tensor_copy(lbt[:, 0], lbt[:, 1]).then_inc(ln_dve, 1)

            def level_dve(gr, level):
                m = 1 << (level - 1)
                dve.wait_ge(level_ps[gr], level + 1)
                if level <= 7:
                    if level == 1:
                        dve.wait_ge(masks_made, 1)
                        dve.wait_ge(a_act[gr], 1)
                    else:
                        dve.wait_ge(a_dve[gr], level - 1)
                    diag = bass.AP(A[gr], 0, [[HG * 2 * T, P], [2 * T, HG], [T + P, 2], [1, P]])
                    x = ps[:, 4 + 2 * gr:6 + 2 * gr].rearrange("p a (h b t) -> p (a h) b t", h=2, b=2)
                    mk = bass.AP(masks, (level - 1) * P, [[7 * P, P], [0, HG], [0, 2], [1, P]])
                    nc.vector.copy_predicated(diag, mask=mk, data=x).then_inc(a_dve[gr], 1)
                    if level > 1:
                        dve.wait_ge(tot_up[gr], level - 1)
                        dve.wait_ge(q_up[gr], level - 1)
                    x = q_pairs(gr, m)
                    nc.vector.tensor_tensor(x, x, tot_pairs(gr, m, swap=False), ALU.mult).then_inc(q_up[gr], 1)
                else:
                    dve.wait_ge(tot_up[gr], 7)
                    dve.wait_ge(q_up[gr], 7)
                    x = q_pairs(gr, m)
                    nc.vector.tensor_tensor(x, x, tot_pairs(gr, m, swap=False), ALU.mult).then_inc(q_up[gr], 1)

            def z_dve(c):
                if c == 0:
                    for gr in range(2):
                        dve.wait_ge(k_up[gr], 1)
                        dve.wait_ge(tot_up[gr], 1)
                        dve.wait_ge(q_up[gr], 1)
                nc.vector.tensor_scalar(tb[:, c % 2, T:2 * T], hb[:, c], col(V_LNG + c), col(V_LNB + c),
                                        ALU.mult, ALU.add).then_inc(chain, 1)
                links[0] += 1
                dve.wait_ge(chain, links[0])
                dve.wait_ge(zs_made, c + 1)
                nc.vector.tensor_tensor(tb[:, c % 2, T:2 * T], tb[:, c % 2, T:2 * T], tb[:, c % 2, 0:T],
                                        ALU.mult).then_inc(zf_made, 1)
                dve.wait_ge(zh_made, c + 1)
                nc.vector.tensor_tensor(zl[:, c], tb[:, c % 2, T:2 * T], zh[:, c].bitcast(F32),
                                        ALU.subtract).then_inc(zl_made, 1)

            queue = [(gr, level) for level in range(9) for gr in range(2)]
            for j in range(8):
                lo(GO + j + 2)
                g = G_GO + j
                dve.wait_ge(act_made, acts(g))
                nc.vector.tensor_tensor(gout[:, j], ps[:, bank(g), 0:T], ta[:, j % 2, 0:T], ALU.mult).then_inc(bank_read, 1)
                gr, level = queue.pop(0)
                if level:
                    level_dve(gr, level)
                if j >= 4:
                    z_dve(2 * j - 8)
                    z_dve(2 * j - 7)
            for c in range(KC):
                lo(PB + 2 * c + 2)
                lo(PB + 2 * c + 3)
                g = G_PB + c
                dve.wait_ge(act_made, acts(g))
                nc.vector.tensor_tensor(yb[:, c], ps[:, bank(g) + 1, 0:T], ta[:, c % 2, 0:T], ALU.mult).then_inc(bank_read, 1)
                for _ in range(2):
                    if queue:
                        gr, level = queue.pop(0)
                        level_dve(gr, level)
            assert not queue
            for b in range(2):
                dve.wait_ge(orms_made, b + 1)
                link(nc.vector.reciprocal(orms[:], orms[:]))
                link(nc.vector.tensor_tensor(onorm[:].rearrange("p (a h) t -> p a (h t)", a=2),
                                             ps[:, 4 + 2 * b:6 + 2 * b],
                                             orms[:].rearrange("p (a h) t -> p a (h t)", a=2), ALU.mult))
                nc.vector.scalar_tensor_tensor(onorm[:], onorm[:], col(V_HN), gout[:, HG * b:HG * b + HG],
                                               ALU.mult, ALU.mult).then_inc(of_made, 1)
                dve.wait_ge(ozh_made, b + 1)
                nc.vector.tensor_tensor(ozl[:, HG * b:HG * b + HG], onorm[:],
                                        ozh[:, HG * b:HG * b + HG].bitcast(F32), ALU.subtract).then_inc(ozl_made, 1)
            for c in range(KC):
                lo(PA + 2 * c + 2)
                lo(PA + 2 * c + 3)
                g = G_PA + c
                dve.wait_ge(act_made, acts(g))
                if c >= 2:
                    dve.wait_ge(yh_made, c - 1)
                nc.vector.tensor_tensor(tb[:, c % 2, 0:T], ps[:, bank(g) + 1, 0:T], ta[:, c % 2, 0:T],
                                        ALU.mult).then_inc(bank_read, 1)
                dve.wait_ge(bank_read, g + 1)
                nc.vector.tensor_tensor(tb[:, c % 2, 0:T], tb[:, c % 2, 0:T], yb[:, c], ALU.add).then_inc(yf_made, 1)
                dve.wait_ge(yh_made, c + 1)
                nc.vector.tensor_tensor(yl[:, c], tb[:, c % 2, 0:T], yh[:, c].bitcast(F32),
                                        ALU.subtract).then_inc(yl_made, 1)
            for c in range(KC):
                lo(WO + c + 2)
                g = G_WO + c
                dve.wait_ge(unit_done, WO + c + 1)
                nc.vector.scalar_tensor_tensor(h[:, 1, c], ps[:, bank(g), 0:T], mod[:, 40 + c, 1:2], h[:, 1, c],
                                               ALU.mult, ALU.add).then_inc(bank_read, 1)
            normed(2, lat, T, 6)
            with dve.Fori(0, 11) as i:
                up_body(UP2, G_UP2, 0, i, 4, T, act2_h, act2_l, 22)
            down_body(DOWN2, G_DOWN2, 1, lat, UNITS)
            dve.wait_ge(rms_made, 4)
            nc.vector.reciprocal(rstd[:, 0:T], rstd[:, 0:T]).then_inc(rstd_made, 1)
            dve.wait_ge(rstd_made, 4)
            for c in range(KC):
                nc.vector.scalar_tensor_tensor(h[:, 1, c], h[:, 1, c], col(V_NF + c), rstd[:, 0:T],
                                               ALU.mult, ALU.mult).then_inc(out_made, 1)

        @block.tensor
        def _(pe):
            def three(out, w_hi, w_lo, x_hi, x_lo, start, stop):
                nc.tensor.matmul(out, w_hi, x_hi, start=start, stop=False)
                nc.tensor.matmul(out, w_hi, x_lo, start=False, stop=False)
                return nc.tensor.matmul(out, w_lo, x_hi, start=False, stop=stop)

            def unit(n, out, xs, k0=0, k=8, start=True, stop=True, i=0, per=0):
                lo_wait(pe, n, i, per)
                for j in range(k):
                    x = three(out, wh[:, n % 4, j], wl[:, n % 4, j], *xs(k0 + j),
                              start=start and j == 0, stop=stop and j == k - 1)
                x.then_inc(unit_done, 1)

            def free(g, i=0, per=0):
                if g >= 2:
                    pe.wait_ge(bank_read, g - 1 + per * i)

            def out512(b):
                return ps[:, b].rearrange("p (a t) -> p a t", a=2)

            u_both = lambda k: (uh[:, :, k], ul[:, :, k])
            u_lat = lambda k: (uh[:, 1, k], ul[:, 1, k])

            def ada(w, bk, c, cdyn=None):
                out = ps[:, bk, 2 * c:2 * c + 2] if cdyn is None else ps[:, bk, bass.ds(cdyn, 2)]
                for k in range(KC):
                    x = nc.tensor.matmul(out, w[:, k], csil[:, k], start=(k == 0), stop=(k == KC - 1))
                x.then_inc(ada_done, 1)

            def statistics(which, w):
                pe.wait_ge(ssq_made, 8 * which + 8)
                nc.tensor.matmul(ps[:, 7, 0:w], ones[:], ssq[:, 0:w], start=True, stop=True).then_inc(stat_made, 1)

            pe.wait_ge(csil_made, 1)
            pe.wait_ge(ready, 1)
            for a in range(ADA_FIRST):
                if a % 2 == 0:
                    pe.wait_ge(ada_first_in[a // 2], 16)
                if a == 6:
                    statistics(0, 512)
                ada(ada_first[:, a], 4, a)
            pe.wait_ge(ul_made, 8)

            def up_body(first, g0, i, per, w, with_ada, xs):
                for s in range(2):
                    g = g0 + s
                    free(g, i, per // 2)
                    for e in range(2):
                        b = 2 * s + e
                        unit(first + b, out512(b) if w == 512 else ps[:, b, 0:w], xs, i=i, per=per)
                        if with_ada:
                            a = first + b
                            pe.wait_ge(ada_in[a % 2], 16 * (a // 2 + 1) + 8 * per * i)
                            ada(ada_ring[:, a % 2], 5, a, 2 * a + 2 * per * i if per else None)

            up_body(UP1, G_UP1, 0, 0, 512, True, u_both)
            with pe.Fori(0, 10) as i:
                up_body(UP1 + 4, G_UP1 + 2, i, 4, 512, True, u_both)

            def down_body(first, g0, js, w, xs, with_ada, view):
                n, a = first, ADA_UP
                for c in range(KC):
                    g = g0 + c
                    free(g)
                    if c == 0:
                        pe.wait_ge(actl_made, js)
                    k0 = 0
                    for e, k in enumerate(DOWN_K):
                        unit(n, view(bank(g)), xs, k0, k, start=(e == 0), stop=(e == 2))
                        n, k0 = n + 1, k0 + k
                    if with_ada:
                        for _ in range(2 if c % 2 else 1):
                            pe.wait_ge(ada_in[a % 2], 16 * (a // 2 + 1))
                            ada(ada_ring[:, a % 2], 6, a - ADA_UP)
                            a += 1

            down_body(DOWN1, G_DOWN1, 22, 512, lambda k: (act_h[:, k], act_l[:, k]), True, out512)
            statistics(1, 512)
            pe.wait_ge(ul_made, 16)
            for c in range(KC):
                g = G_GLU + c
                free(g)
                unit(GLU + 2 * c, ps[:, bank(g), 0:T], u_lat)
                unit(GLU + 2 * c + 1, ps[:, bank(g) + 1, 0:T], u_lat)
            for c in range(2):
                pe.wait_ge(bank_read, G_GLU if c == 0 else G_V)
                for j in range(4):
                    n = VV + 4 * c + j
                    lo_wait(pe, n)
                    w_hi = wh[:, n % 4].rearrange("p k c -> p (k c)")
                    w_lo = wl[:, n % 4].rearrange("p k c -> p (k c)")
                    for e in range(2):
                        k = 2 * j + e
                        for b in range(4):
                            uhb = uh[:, b // 2, k, P * (b % 2):P * (b % 2) + P]
                            ulb = ul[:, b // 2, k, P * (b % 2):P * (b % 2) + P]
                            x = three(ps[:, (4 - 4 * c) + b], uhb, ulb, w_hi[:, 512 * e:512 * e + 512],
                                      w_lo[:, 512 * e:512 * e + 512], start=(k == 0), stop=(k == KC - 1))
                    x.then_inc(unit_done, 1)
            for j in range(16):
                g = G_Z + j
                if j < 2:
                    pe.wait_ge(bank_read, G_Z)
                else:
                    free(g)
                unit(ZZ + j, out512(bank(g)), u_both)
            pe.wait_ge(ident_in, 16)
            for j in range(8):
                g = G_Q + j
                free(g)
                unit(QQ + j, ps[:, bank(g), 0:T], u_lat)
                if j == 0:
                    pe.wait_ge(z_step, 48)
                else:
                    pe.wait_ge(turned_read, j)
                for way in range(2):
                    for b in range(2):
                        x = nc.tensor.transpose(ps[:, 4, (2 * way + b) * P:(2 * way + b) * P + P],
                                                kdec[:, way, j, P * b:P * b + P], ident[:])
                x.then_inc(turned, 1)
                pe.wait_ge(turned_read, j + 1)
                if j:
                    pe.wait_ge(state_made, j)
                for way in range(2):
                    for b in range(2):
                        x = nc.tensor.matmul(ps[:, 5, way * P:way * P + P], tb[:, j % 2, (2 * way + b) * P:(2 * way + b) * P + P],
                                             v[:, b, P * j:P * j + P], start=(b == 0), stop=(b == 1))
                x.then_inc(state_ps, 1)
                if j == 1:
                    pe.wait_ge(ln_dve, 1)
                    nc.tensor.matmul(ps[:, 6, 0:T], ones[:], ssq[:, 0:T], start=True, stop=True).then_inc(ln_ps, 1)
                if j == 5:
                    pe.wait_ge(ln_dve, 4)
                    nc.tensor.matmul(ps[:, 7, 0:T], ones[:], ssq[:, T:2 * T], start=True, stop=True).then_inc(ln_ps, 1)

            def level_mm(gr, level):
                m = 1 << max(level - 1, 0)
                if level == 0:
                    pe.wait_ge(q_first, gr + 1)
                    if gr == 0:
                        pe.wait_ge(state_made, HEADS)
                else:
                    if level == 1:
                        pe.wait_ge(a_act[gr], 1)
                    else:
                        pe.wait_ge(a_dve[gr], level - 1)
                        pe.wait_ge(q_up[gr], level - 1)
                    if level < 8:
                        pe.wait_ge(khat_made[gr], level)
                    else:
                        pe.wait_ge(k_up[gr], 7)
                for hl in range(HG):
                    hd = HG * gr + hl
                    for b in range(2):
                        out = ps[:, 4 + 2 * gr + hl // 2, (hl % 2) * T + b * P:(hl % 2) * T + b * P + P]
                        if level == 0:
                            for way in range(2):
                                x = nc.tensor.matmul(out, K[:, way, hd, P * b:P * b + P], q[:, hd, P * b:P * b + P],
                                                     start=(way == 0), stop=(way == 1))
                        elif level < 8:
                            o3 = out.rearrange("p (n a m) -> p n a m", a=2, m=m)
                            x = nc.tensor.matmul(out, khat[:, gr, hl, P * b:P * b + P], operand(Q, hd, b, m), start=True, stop=True)
                        else:
                            x = nc.tensor.matmul(out, K[:, b, hd, P * b:P * b + P],
                                                 Q[:, 1 - b, hd, P * (1 - b):P * (1 - b) + P], start=True, stop=True)
                x.then_inc(level_ps[gr], 1)

            queue = [(gr, level) for level in range(9) for gr in range(2)]
            for j in range(8):
                g = G_GO + j
                free(g)
                unit(GO + j, ps[:, bank(g), 0:T], u_lat)
                level_mm(*queue.pop(0))
            for c in range(KC):
                g = G_PB + c
                free(g)
                unit(PB + 2 * c, ps[:, bank(g), 0:T], u_lat)
                if c == 0:
                    pe.wait_ge(zl_made, 8)
                unit(PB + 2 * c + 1, ps[:, bank(g) + 1, 0:T], lambda k: (zh[:, k], zl[:, k]))
                for _ in range(2):
                    if queue:
                        level_mm(*queue.pop(0))
            for b in range(2):
                if b == 0:
                    for gr in range(2):
                        pe.wait_ge(a_act[gr], 2)
                        pe.wait_ge(q_up[gr], 8)
                else:
                    pe.wait_ge(orms_made, 1)
                for hl in range(HG):
                    hd = HG * b + hl
                    out = ps[:, 4 + 2 * b + hl // 2, (hl % 2) * T:(hl % 2) * T + T]
                    for s in range(2):
                        nc.tensor.matmul(out, v[:, 2 + s, P * hd:P * hd + P], A[b][:, hl, s], start=(s == 0), stop=False)
                    nc.tensor.matmul(out, state[:, hd, 0], Q[:, 1, hd], start=False, stop=False)
                    x = nc.tensor.matmul(out, state[:, hd, 1], Q[:, 0, hd], start=False, stop=True)
                x.then_inc(o_ps, 1)
                pe.wait_ge(osq_made, b + 1)
                if b:
                    pe.wait_ge(ozl_made, 1)
                for e in range(2):
                    x = nc.tensor.matmul(ps[:, 6 - 2 * b + e], ones[:], osq[:, 2 * e:2 * e + 2].rearrange("p h t -> p (h t)"),
                                         start=True, stop=True)
                x.then_inc(ostat_ps, 1)
            pe.wait_ge(ozl_made, 2)
            for c in range(KC):
                g = G_PA + c
                free(g)
                unit(PA + 2 * c, ps[:, bank(g), 0:T], u_lat)
                unit(PA + 2 * c + 1, ps[:, bank(g) + 1, 0:T], lambda k: (ozh[:, k], ozl[:, k]))
            pe.wait_ge(yl_made, 8)
            for c in range(KC):
                g = G_WO + c
                free(g)
                unit(WO + c, ps[:, bank(g), 0:T], lambda k: (yh[:, k], yl[:, k]))
            statistics(2, T)
            pe.wait_ge(ul_made, 24)
            with pe.Fori(0, 11) as i:
                up_body(UP2, G_UP2, i, 4, T, False, u_lat)
            down_body(DOWN2, G_DOWN2, 44, T, lambda k: (act2_h[:, k], act2_l[:, k]), False,
                      lambda b: ps[:, b, 0:T])
            statistics(3, T)


def _units(w):
    k, n = w.shape
    return np.ascontiguousarray(w.reshape(k // P, P, n // P, P).transpose(2, 1, 0, 3))


def _columns(x):
    return x.reshape(-1, P).T


def kernel(**inputs):
    import concourse.bacc as _bacc
    from concourse.bass_utils import run_bass_kernel_spmd as _run

    a = {k: np.asarray(x) for k, x in inputs.items()}
    nc = _bacc.Bacc("TRN2", target_bir_lowering=False, num_devices=1)

    def tokens(x):
        return x.reshape(T, KC, P).transpose(2, 1, 0)

    def pairs(w):
        u = _units(w)
        return u.reshape(2, FC, P, KC, P).transpose(1, 0, 2, 3, 4).reshape(2 * FC, P, KC, P)

    w_in = a["w_in"][0]
    level = np.arange(P)
    masks = np.zeros((P, 7, P), np.float32)
    for i in range(7):
        m = 1 << i
        same = (level[:, None] // (2 * m)) == (level[None, :] // (2 * m))
        masks[:, i] = same & ((level[:, None] // m) != (level[None, :] // m))
    arrays = {
        "x": tokens(a["x"][0]),
        "ctx": tokens(a["ctx"][0]),
        "cvec": np.stack([_columns(a["c_ctx"]), _columns(a["c"][0])], axis=2),
        "vecs": np.concatenate(
            [_columns(a[n].reshape(-1)) for n in ("norm_ffn1", "norm_mix", "norm_ffn2", "final_norm", "b_ada",
                                                  "b_gate", "lb_logits", "hgrn_norm", "b_dw", "conv_ln_g",
                                                  "conv_ln_b")], axis=1),
        "wdw": a["w_dw"][0].reshape(TAPS, KC, P).transpose(2, 0, 1),
        "masks": masks,
        "ident": np.eye(P, dtype=np.float32),
        "ada": _units(a["w_ada"][0]),
        "up1": pairs(a["w_ffn1_up"][0]),
        "down1": _units(a["w_ffn1_down"][0]),
        "w_in": _units(w_in),
        "w_v": w_in[:, 3 * D:4 * D].reshape(4, 2, P, 2, 512).transpose(3, 0, 2, 1, 4),
        "gate": _units(a["w_gate"][0]),
        "proj_a": _units(a["w_proj_a"][0]),
        "proj_b": _units(a["w_proj_b"][0]),
        "w_o": _units(a["w_o"][0]),
        "up2": pairs(a["w_ffn2_up"][0]),
        "down2": _units(a["w_ffn2_down"][0]),
    }
    arrays = {f"{k}_dram": np.ascontiguousarray(x) for k, x in arrays.items()}
    d = {k[:-5]: nc.dram_tensor(k, x.shape, mybir.dt.from_np(x.dtype), kind="ExternalInput").ap()
         for k, x in arrays.items()}
    d["out"] = nc.dram_tensor("out_dram", (KC, P, T), F32, kind="ExternalOutput").ap()
    layer(nc, d)
    r = _run(nc, [arrays], core_ids=[0])
    return r.results[0]["out_dram"].transpose(2, 0, 1).reshape(1, T, D)
```

```python
from contextlib import ExitStack

import numpy as np

import concourse.bass as bass
from concourse import mybir

F32 = mybir.dt.float32
F32R = mybir.dt.float32r
U8 = mybir.dt.uint8
ACT = mybir.ActivationFunctionType
ALU = mybir.AluOpType
AX = mybir.AxisListType

P = 128
D = 1024
KC = D // P
T = 256
F = 2816
FC = F // P
HEADS = 8
TAPS = 31
PAD = TAPS // 2
GLUW = T + 2 * PAD
ADA = 72
EPS = 1e-6
HG = 4
SUMS = (0, 1, 3, 4)

V_N1, V_NM, V_N2, V_NF = 0, 8, 16, 24
V_BADA, V_BGATE, V_LB, V_HN = 32, 104, 120, 152
V_BDW, V_LNG, V_LNB, V_END = 153, 161, 169, 177

UP1, DOWN1, GLU, VV, ZZ, QQ, GO, GA, PB, PA, WO, UP2, DOWN2, UNITS = (
    0, 44, 68, 84, 92, 108, 116, 124, 132, 148, 156, 164, 208, 232)
(G_UP1, G_DOWN1, G_GLU, G_V, G_Z, G_Q, G_GO, G_GA, G_PB, G_PA, G_WO, G_UP2, G_DOWN2) = (
    0, 22, 30, 38, 40, 56, 64, 72, 80, 88, 96, 104, 126)
DOWN_K = (8, 8, 6)
ADA_FIRST = 16
ADA_PE = 12
ADA_GROUPS = ADA_PE // 4
ADA_UP = 44
ADA_BOTH = 24


def down_units():
    for c in range(KC):
        k0 = 0
        for k in DOWN_K:
            yield c, k0, k
            k0 += k


def ada_beside(c):
    a = ADA_FIRST + ADA_UP + c + c // 2
    return range(a, a + 1 + c % 2)


def ahead(units, after):
    ks = [k for _, _, k in units] + after
    return ks[2:len(units) + 2]


GLU_STEPS, V_STEPS, Z_STEPS = 5, (48, 32), 9
MOD_FIRST = 2
SPLIT_POOL = (VV, QQ)


def layer(nc, d):
    with ExitStack() as ctx:
        def sem(name):
            return ctx.enter_context(nc.semaphore(name))

        base = (nc.sbuf_base + 31) // 32 * 32
        slab = ctx.enter_context(nc.sbuf_tensor("slab", [P, (nc.sbuf_usable_end - base) // 4 - 16], F32))

        def at(name, shape, offset, dt=F32):
            return nc.alloc_sbuf_tensor_at(name, [P, *shape], dt, offset=base + offset)

        KB = 1024
        h = at("h", [2, KC, T], 0)
        uh = at("uh", [2, KC, T], 16 * KB, F32R)
        ul = at("ul", [2, KC, T], 32 * KB, F32R)
        raw = at("raw", [4, 8, P], 48 * KB)
        wh = at("wh", [4, 8, P], 64 * KB, F32R)
        wl = at("wl", [4, 8, P], 80 * KB, F32R)
        M = 96 * KB
        junk0 = at("junk0", [D], M + 16 * KB)
        c_row = at("c_row", [2, D], M + 72 * KB)
        mrow = at("mrow", [ADA_GROUPS, 4 * P], M + 80 * KB)
        ada0 = at("ada0", [ADA_GROUPS, KC, 4 * P], M + 24 * KB)
        ada_raw = at("ada_raw", [2, D], M + 88 * KB)
        t_first = at("t_first", [2, KC, T], M)
        act_h = at("act_h", [FC, 2, T], M, F32R)
        act_l = at("act_l", [FC, 2, T], M + 44 * KB, F32R)
        act2_h = at("act2_h", [FC, T], M, F32R)
        act2_l = at("act2_l", [FC, T], M + 22 * KB, F32R)
        q = at("q", [HEADS, T], M)
        khat = at("khat", [2, HG, T], M)
        kdec = at("kdec", [2, HEADS, T], M + 8 * KB)
        Q = at("Q", [2, HEADS, T], M + 8 * KB)
        K = at("K", [2, HEADS, T], M + 24 * KB)
        tot1 = [at(f"tot1_{g}", [2, HG, T], M + (40 + 8 * g) * KB) for g in range(2)]
        v = at("v", [4, D], M + 56 * KB)
        state = at("state", [HEADS, 2, P], M + 72 * KB)
        glu = at("glu", [KC, GLUW], M + 72 * KB)
        gout = at("gout", [HEADS, T], M + 80 * KB)
        lnsq = at("lnsq", [KC, T], M + 80 * KB)
        tot2 = at("tot2", [2, 2, HG, T // 2], M + 88 * KB)
        dec = at("dec", [2, 2, T], M + 88 * KB)
        ident = at("ident", [P], M + 92 * KB)
        masks_f = at("masks_f", [7, P], M + 92 * KB + 512)
        zh = at("zh", [KC, T], M + 40 * KB, F32R)
        zl = at("zl", [KC, T], M + 48 * KB, F32R)
        ozh = at("ozh", [HEADS, T], M, F32R)
        ozl = at("ozl", [HEADS, T], M + 88 * KB, F32R)
        yh = at("yh", [KC, T], M + 24 * KB, F32R)
        yl = at("yl", [KC, T], M + 32 * KB, F32R)
        orms = at("orms", [HG, T], M + 24 * KB)
        onorm = at("onorm", [HG, T], M + 28 * KB)
        A = [at("A0", [HG, 2, T], 16 * KB), at("A1", [HG, 2, T], 32 * KB)]
        hb = at("hb", [KC, T], 0)
        yb = at("yb", [KC, T], 0)
        ga = at("ga", [KC, T], M + 56 * KB)
        ta = at("ta", [2, 512], M + 96 * KB)
        tb = at("tb", [2, 512], M + 100 * KB)
        ssq = at("ssq", [512], M + 104 * KB)
        rstd = at("rstd", [512], M + 106 * KB)
        junk = at("junk", [D], M + 104 * KB)
        tot4 = at("tot4", [2, 2, HG, T // 4], M + 104 * KB)
        osq = at("osq", [HG, T], M + 104 * KB)
        S0 = M + 108 * KB
        vecs = at("vecs", [V_END], S0)
        wdw = at("wdw", [TAPS, KC], S0 + 736)
        masks = at("masks", [7, P], S0 + 736, U8)
        mod = at("mod", [ADA, 2], S0 + 1760)
        ones = at("ones", [P], S0 + 2336)
        cvec = at("cvec", [KC, 2], S0 + 2848)
        csil = at("csil", [KC, 2], S0 + 2912)
        ident0 = at("ident0", [2], S0 + 3808)
        dots = at("dots", [12, 2], S0 + 3712)
        scale = at("scale", [3, KC, 2], S0 + 2976)
        half_gate = at("half_gate", [2, KC, 2], S0 + 3168)
        lbt = at("lbt", [6, 16], S0 + 3296)
        eps = at("eps", [1], S0 + 3680)
        ps = ctx.enter_context(nc.psum_tensor("ps", [P, 8, 512], F32))
        csil_all = ps[:, 4:8].rearrange("p (x k) n -> p x (k n)", x=2)

        raw_in = [sem(f"raw_in{i}") for i in range(4)]
        small_in = sem("small_in")
        x_in = sem("x_in")
        ident_in, masks_in, masks_made = sem("ident_in"), sem("masks_in"), sem("masks_made")
        out_sent = sem("out_sent")
        hi_made = sem("hi_made")
        lo_dve, lo_pool = sem("lo_dve"), sem("lo_pool")
        unit_done = sem("unit_done")
        cvec_in = sem("cvec_in")
        ada0_in = [sem(f"ada0_in{a}") for a in range(2 * ADA_GROUPS)]
        ada_in = [sem("ada_in0"), sem("ada_in1")]
        ada0_done = sem("ada0_done")
        dot_both, dot_made = sem("dot_both"), sem("dot_made")
        dots_read = sem("dots_read")
        c_row_in, c_row_made, csil_ps = sem("c_row_in"), sem("c_row_made"), sem("csil_ps")
        ada0_ps, mrow_made = sem("ada0_ps"), sem("mrow_made")
        bank_read = sem("bank_read")
        act_made = sem("act_made")
        acth_made, actl_made = sem("acth_made"), sem("actl_made")
        ready = sem("ready")
        csil_made = sem("csil_made")
        logits_made, exp_made = sem("logits_made"), sem("exp_made")
        chain = sem("chain")
        sq_made, ssq_made = sem("sq_made"), sem("ssq_made")
        stat_made, rms_made, rstd_made = sem("stat_made"), sem("rms_made"), sem("rstd_made")
        tf_made = sem("tf_made")
        uf_act = sem("uf_act")
        uf_made, uh_made, ul_made = sem("uf_made"), sem("uh_made"), sem("ul_made")
        lat_ps, lat_added = sem("lat_ps"), sem("lat_added")
        con_square, con_ssq = sem("con_square"), sem("con_ssq")
        out_made = sem("out_made")
        conv_step = sem("conv_step")
        z_step = sem("z_step")
        v_copied = sem("v_copied")
        turned, turned_read = sem("turned"), sem("turned_read")
        state_ps, state_made = sem("state_ps"), sem("state_made")
        ln_dve, ln_ps, ln_act = sem("ln_dve"), sem("ln_ps"), sem("ln_act")
        q_first = sem("q_first")
        level_ps = [sem(f"level_ps{g}") for g in range(2)]
        a_act = [sem(f"a_act{g}") for g in range(2)]
        a_dve = [sem(f"a_dve{g}") for g in range(2)]
        khat_made = [sem(f"khat_made{g}") for g in range(2)]
        q_up = [sem(f"q_up{g}") for g in range(2)]
        k_up = [sem(f"k_up{g}") for g in range(2)]
        tot_up = [sem(f"tot_up{g}") for g in range(2)]
        zs_made, zf_made, zh_made, zl_made = sem("zs_made"), sem("zf_made"), sem("zh_made"), sem("zl_made")
        o_ps, osq_made, ostat_ps, orms_made, of_made, ozh_made, ozl_made = (
            sem("o_ps"), sem("osq_made"), sem("ostat_ps"), sem("orms_made"), sem("of_made"),
            sem("ozh_made"), sem("ozl_made"))
        ya_made, yf_made, yh_made, yl_made = sem("ya_made"), sem("yf_made"), sem("yh_made"), sem("yl_made")

        block = ctx.enter_context(nc.Block())

        def lo_wait(eng, n, i=0, per=0):
            a, b = SPLIT_POOL
            if n < a:
                eng.wait_ge(lo_dve, n + 1 + per * i)
            elif n < b:
                eng.wait_ge(lo_pool, n + 1 - a + per * i)
            else:
                eng.wait_ge(lo_dve, n + 1 - (b - a) + per * i)

        def bank(g):
            return 2 * (g % 2)

        def acts(g):
            if g < G_DOWN1:
                return g + 1
            if g < G_GLU:
                return 22
            if g < G_PA:
                return g + 1 - 8
            return g + 1 - 24

        def tot_view(gr, m):
            if m == 1:
                return tot1[gr], 0, HG * T, 2 * HG * T
            t, w = (tot2, HG * T) if m.bit_length() % 2 == 0 else (tot4, HG * T // 2)
            return t, gr * w, HG * T // m, 2 * w

        def tot_halves(gr, m):
            t, o, pl, row = tot_view(gr, m)
            n = HG * T // (2 * m)
            t2, o2, pl2, row2 = tot_view(gr, 2 * m)
            return (bass.AP(t, o, [[row, P], [pl, 2], [2, n]]),
                    bass.AP(t, o + 1, [[row, P], [pl, 2], [2, n]]),
                    bass.AP(t2, o2, [[row2, P], [pl2, 2], [1, n]]))

        def tot_pairs(gr, m, swap):
            t, o, pl, row = tot_view(gr, m)
            n = HG * T // (2 * m)
            if swap:
                return bass.AP(t, o + pl + 1, [[row, P], [2, n], [-pl - 1, 2], [0, m]])
            return bass.AP(t, o + 1, [[row, P], [2, n], [pl - 1, 2], [0, m]])

        def pairs(t, gr, m):
            return bass.AP(t, gr * HG * T, [[2 * HEADS * T, P], [2 * m, HG * T // (2 * m)], [HEADS * T + m, 2], [1, m]])

        def q_pairs(gr, m):
            return pairs(Q, gr, m)

        def k_pairs(gr, m):
            return pairs(K, gr, m)

        def operand(t, head, blk, m):
            o = head * T + blk * P
            return bass.AP(t, o, [[2 * HEADS * T, P], [2 * m, P // (2 * m)], [HEADS * T + m, 2], [1, m]])

        @block.sync
        def _(sp):
            def load(n, src, k=8, i=0, per=0, shape=None):
                if n >= 4:
                    lo_wait(sp, n - 4, i, per)
                dst = raw[:, n % 4, 0:k]
                if shape:
                    dst = dst.rearrange("p k c -> p (k c)").rearrange("p (a b) -> p a b", a=shape)
                sp.dma_start(dst, src).then_inc(raw_in[n % 4], 16)

            def load_first(g, half):
                k = slice(4 * half, 4 * half + 4)
                sp.dma_start(ada0[:, g, k], d["ada0"][:, g, k]).then_inc(ada0_in[2 * g + half], 16)

            def load_ada(a, src, i=0, per=0):
                if a >= 2:
                    sp.wait_ge(dot_made, a - 1 + per * i)
                sp.dma_start(ada_raw[:, a % 2], src).then_inc(ada_in[a % 2], 16)

            sp.dma_start(c_row[0:1], d["c_rows"]).then_inc(c_row_in, 16)
            sp.dma_start(cvec[:], d["cvec"]).then_inc(cvec_in, 16)
            sp.dma_start(ident0[0:2], d["ident0"]).then_inc(cvec_in, 16)
            sp.dma_start(h[:, 0], d["ctx"]).then_inc(x_in, 16)
            sp.dma_start(h[:, 1], d["x"]).then_inc(x_in, 16)
            load_first(0, 0)
            load_first(0, 1)
            load_ada(0, d["ada"][0])
            load_first(1, 0)
            load_ada(1, d["ada"][1])
            load_first(1, 1)
            load_first(2, 0)
            load_ada(2, d["ada"][2])
            load_first(2, 1)
            load_ada(3, d["ada"][3])
            sp.dma_start(vecs[:], d["vecs"]).then_inc(small_in, 16)
            sp.dma_start(wdw[:], d["wdw"]).then_inc(small_in, 16)
            for s in range(4):
                load(UP1 + s, d["up1"][s])

            def one(t, at):
                return t[bass.ds(at, 1)].rearrange("o p k c -> (o p) k c")

            for a in (4, 5):
                load_ada(a, d["ada"][a])
            with sp.Fori(0, 10) as i:
                for s in (0, 2):
                    for e in (s, s + 1):
                        load(UP1 + 4 + e, one(d["up1"], 4 * i + (4 + e)), i=i, per=4)
                    for e in (s, s + 1):
                        load_ada(6 + e, d["ada"][bass.ds(4 * i + (6 + e), 1)].rearrange("o p n -> (o p) n"), i, 4)
            for a in (ADA_UP + 2, ADA_UP + 3):
                load_ada(a, d["ada"][a])
            for n, (c, k0, k) in enumerate(down_units(), DOWN1):
                load(n, d["down1"][c, :, k0:k0 + k], k)
                if k0 + k == FC:
                    last = ada_beside(c).start - ADA_PE + 2
                    for a in range(ada_beside(c - 1).start - ADA_PE + 2 if c else last - 2, last):
                        load_ada(a, d["ada"][a])
            w_in = d["w_in"]
            for c in range(KC):
                load(GLU + 2 * c, w_in[40 + c])
                load(GLU + 2 * c + 1, w_in[48 + c])
            for j in range(8):
                load(VV + j, d["w_v"][j // 4, j % 4], 8, shape=2)
            sp.dma_start(ident[:], d["ident"]).then_inc(ident_in, 16)
            sp.dma_start(masks_f[:], d["masks"]).then_inc(masks_in, 16)
            for j in range(16):
                load(ZZ + j, w_in[8 + j])
            for j in range(8):
                load(QQ + j, w_in[j])
            for j in range(8):
                load(GO + j, w_in[32 + j])
            for c in range(KC):
                load(GA + c, d["gate"][c])
            for c in range(KC):
                load(PB + 2 * c, d["gate"][8 + c])
                load(PB + 2 * c + 1, d["proj_b"][c])
            for c in range(KC):
                load(PA + c, d["proj_a"][c])
            for c in range(KC):
                load(WO + c, d["w_o"][c])
            with sp.Fori(0, 11) as i:
                for s in range(4):
                    load(UP2 + s, one(d["up2"], 4 * i + s), i=i, per=4)
            for n, (c, k0, k) in enumerate(down_units(), DOWN2):
                load(n, d["down2"][c, :, k0:k0 + k], k)
            for c in range(KC):
                sp.wait_ge(out_made, c + 1)
                sp.dma_start(d["out"][c], h[:, 1, c]).then_inc(out_sent, 16)
            sp.wait_ge(out_sent, 16 * KC)

        @block.scalar
        def _(act):
            def hi(n, k=8, i=0, per=0):
                act.wait_ge(raw_in[n % 4], 16 * (n // 4 + 1) + 4 * per * i)
                if n >= 4:
                    act.wait_ge(unit_done, n - 3 + per * i)
                nc.scalar.activation(wh[:, n % 4, 0:k], raw[:, n % 4, 0:k], ACT.Copy).then_inc(hi_made, 1)

            def func(g, dst, src, f, i=0, per=0, unit=0, uper=0, sig=act_made, **kw):
                act.wait_ge(unit_done, unit + 1 + uper * i)
                if g >= 2:
                    act.wait_ge(bank_read, g - 1 + per * i)
                nc.scalar.activation(dst, src, f, **kw).then_inc(sig, 1)

            def square(which, halves, c):
                n = 8 * SUMS.index(which) + c
                if c >= 2:
                    act.wait_ge(ssq_made, n - 1)
                w = T * (halves.stop - halves.start)
                src = h[:, halves, c]
                dst = ta[:, c % 2, 2 * T - w:2 * T].rearrange("p (a t) -> p a t", t=T)
                nc.scalar.activation(dst, src, ACT.Square).then_inc(sq_made, 1)

            def root(which, a, b, bk=7):
                act.wait_ge(stat_made, which + 1)
                nc.scalar.activation(rstd[:, a:b], ps[:, bk, a:b], ACT.Sqrt, scale=1.0 / D,
                                     bias=eps[:]).then_inc(rms_made, 1)

            def u_hi(which, s, c, shift=0):
                act.wait_ge(uf_made, 8 * which + c + 1)
                if which == 0:
                    act.wait_ge(uf_act, c + 1)
                    nc.scalar.activation(uh[:, :, c], tb[:, c % 2].rearrange("p (a t) -> p a t", t=T),
                                         ACT.Copy).then_inc(uh_made, 1)
                else:
                    nc.scalar.activation(uh[:, s, c], tb[:, c % 2, T:2 * T], ACT.Identity,
                                         bias=mod[:, 8 * shift + c, s:s + 1]).then_inc(uh_made, 1)

            both, con, lat = slice(0, 2), slice(0, 1), slice(1, 2)
            def rows(g):
                act.wait_ge(ada0_ps, g + 1)
                nc.scalar.activation(mrow[0:2, g], ps[0:2, g % 2], ACT.Copy).then_inc(mrow_made, 1)

            nc.scalar.preload_act_table(ACT.Silu)
            act.wait_ge(c_row_in, 16)
            nc.scalar.activation(c_row[0:1], c_row[0:1], ACT.Silu).then_inc(c_row_made, 1)
            act.wait_ge(cvec_in, 32)
            nc.scalar.activation(csil[:], cvec[:], ACT.Silu).then_inc(csil_made, 1)
            nc.scalar.preload_act_table(ACT.Sqrt)
            act.wait_ge(ready, 2)
            act.wait_ge(x_in, 32)
            for c in range(KC):
                square(0, both, c)
            root(0, 0, 2 * T, 3)
            rows(0)
            rows(1)
            nc.scalar.preload_act_table(ACT.Silu)
            hi(UP1)
            rows(2)
            hi(UP1 + 1)
            for c in range(KC):
                if c == 0:
                    act.wait_ge(chain, MOD_FIRST)
                else:
                    u_hi(0, None, c - 1)
                if c >= 2:
                    act.wait_ge(ul_made, c - 1)
                nc.scalar.activation(tb[:, c % 2, 0:T], t_first[:, 0, c], ACT.Identity, scale=scale[:, 0, c, 0:1],
                                     bias=mod[:, c, 0:1]).then_inc(uf_act, 1)
            u_hi(0, None, KC - 1)

            def up_body(first, g0, i, per, w):
                for s in range(2):
                    for e in range(2):
                        hi(first + 2 * s + e + 2, i=i, per=per)
                    func(g0 + s, ta[:, s, 0:w], ps[:, 2 * s, 0:w], ACT.Silu, i, 2, first + 2 * s + 1, per)

            up_body(UP1, G_UP1, 0, 0, 512)
            with act.Fori(0, 10) as i:
                up_body(UP1 + 4, G_UP1 + 2, i, 4, 512)
            act.wait_ge(logits_made, 1)
            nc.scalar.activation(lbt[:, 1:3], lbt[:, 1:3], ACT.Exp).then_inc(exp_made, 1)
            nc.scalar.preload_act_table(ACT.Sqrt)

            def down_body(first, units, after, g0, which, halves):
                units = list(units)
                ks = ahead(units, after)
                split = which == 1
                for e, (c, k0, k) in enumerate(units):
                    if split and e == len(units) - 1:
                        act.wait_ge(lat_added, 1)
                        square(which, lat, c)
                    if e < len(ks):
                        hi(first + e + 2, ks[e])
                    if k0 + k == FC and not (split and c == KC - 1):
                        act.wait_ge(bank_read, g0 + c + 1)
                        square(which, halves, c)

            down_body(DOWN1, down_units(), [8, 8], G_DOWN1, 1, both)
            root(1, T, 2 * T, 1)
            for c in range(KC):
                u_hi(1, 1, c, 3)
                if c == 3:
                    act.wait_ge(bank_read, G_GLU)
                    nc.scalar.activation(ta[:, 1, 0:T], h[:, 0, KC - 1], ACT.Square).then_inc(con_square, 1)
            root(2, 0, T, 5)
            for c in range(KC):
                hi(GLU + 2 * c + 2)
                hi(GLU + 2 * c + 3)
                g = G_GLU + c
                func(g, ta[:, c % 2, 0:T], ps[:, bank(g) + 1, 0:T], ACT.Sigmoid, unit=GLU + 2 * c + 1)
                u_hi(2, 0, c, 3)
            for c in range(2):
                for j in range(4):
                    hi(VV + 4 * c + j + 2)
                act.wait_ge(unit_done, VV + 4 * c + 4)
                for b in (0, 1):
                    x = nc.scalar.activation(v[:, b, 512 * c:512 * c + 512], ps[:, (4 - 4 * c) + b], ACT.Copy)
                x.then_inc(act_made, 1)
            for j in range(16):
                hi(ZZ + j + 2)
                g = G_Z + j
                func(g, ta[:, j % 2], ps[:, bank(g)], ACT.Sigmoid, unit=ZZ + j)

            def state_copy(j):
                act.wait_ge(state_ps, j + 1)
                nc.scalar.activation(state[:, j], ps[:, 5, 0:2 * P].rearrange("p (a e) -> p a e", a=2), ACT.Copy,
                                     scale=-1.0).then_inc(state_made, 1)

            for j in range(8):
                hi(QQ + j + 2)
                g = G_Q + j
                func(g, ta[:, j % 2, 0:T], ps[:, bank(g), 0:T], ACT.Sigmoid, unit=QQ + j)
                act.wait_ge(turned, j + 1)
                if j >= 2:
                    act.wait_ge(state_ps, j - 1)
                nc.scalar.activation(tb[:, j % 2], ps[:, 4], ACT.Copy).then_inc(turned_read, 1)
                if j:
                    state_copy(j - 1)
                if j == 3:
                    act.wait_ge(ln_dve, 3)
                    nc.scalar.activation(lnsq[:], hb[:], ACT.Square).then_inc(ln_act, 1)
                if j == 6:
                    act.wait_ge(ln_ps, 2)
                    nc.scalar.activation(rstd[:, T:2 * T], ps[:, 7, 0:T], ACT.Sqrt, scale=1.0 / D,
                                         bias=eps[:]).then_inc(ln_act, 1)
            state_copy(7)

            def a_copy(gr, level):
                act.wait_ge(level_ps[gr], level + 1)
                x = ps[:, 4 + 2 * gr:6 + 2 * gr].rearrange("p a (h b t) -> p (a h) b t", h=2, b=2)
                for b in range(2):
                    c = b if level == 0 else 1 - b
                    y = nc.scalar.activation(A[gr][:, :, b, P * c:P * c + P], x[:, :, b], ACT.Copy)
                y.then_inc(a_act[gr], 1)

            def keys(gr, level):
                m = 1 << (level - 1)
                act.wait_ge(level_ps[gr], level)
                if level > 1:
                    act.wait_ge(k_up[gr], level - 1)
                nc.scalar.activation(khat[:, gr].rearrange("p h t -> p (h t)").rearrange(
                    "p (n a m) -> p n a m", a=2, m=m), k_pairs(gr, m), ACT.Copy).then_inc(khat_made[gr], 1)

            def scan_step(gr, level):
                if level == 0:
                    a_copy(gr, 0)
                if level < 7:
                    keys(gr, level + 1)
                if level == 8:
                    a_copy(gr, 8)

            def z_act(c):
                act.wait_ge(ln_dve, 8)
                if c >= 2:
                    act.wait_ge(zl_made, c - 1)
                nc.scalar.activation(tb[:, c % 2, 0:T], hb[:, c], ACT.Sigmoid, scale=vecs[:, V_LNG + c:V_LNG + c + 1],
                                     bias=vecs[:, V_LNB + c:V_LNB + c + 1]).then_inc(zs_made, 1)
                act.wait_ge(zf_made, c + 1)
                nc.scalar.activation(zh[:, c], tb[:, c % 2, T:2 * T], ACT.Copy).then_inc(zh_made, 1)

            queue = [(gr, level) for level in range(9) for gr in range(2)]
            for j in range(8):
                hi(GO + j + 2)
                g = G_GO + j
                func(g, ta[:, j % 2, 0:T], ps[:, bank(g), 0:T], ACT.Sigmoid, unit=GO + j)
                scan_step(*queue.pop(0))
                if j >= 4:
                    z_act(j - 4)
            for j in range(8):
                hi(GA + j + 2)
                g = G_GA + j
                func(g, ta[:, j % 2, 0:T], ps[:, bank(g), 0:T], ACT.Sigmoid, unit=GA + j,
                     bias=vecs[:, V_BGATE + j:V_BGATE + j + 1])
                scan_step(*queue.pop(0))
                if j < 4:
                    z_act(j + 4)

            def o_square(b):
                act.wait_ge(o_ps, b + 1)
                if b:
                    act.wait_ge(ostat_ps, b)
                nc.scalar.activation(osq[:].rearrange("p (a h) t -> p a (h t)", a=2), ps[:, 4 + 2 * b:6 + 2 * b],
                                     ACT.Square).then_inc(osq_made, 1)

            def o_root(b):
                act.wait_ge(ostat_ps, b + 1)
                if b:
                    act.wait_ge(ozl_made, b)
                nc.scalar.activation(orms[:].rearrange("p (a h) t -> p a (h t)", a=2),
                                     ps[:, 6 - 2 * b:8 - 2 * b], ACT.Sqrt, scale=1.0 / P,
                                     bias=eps[:]).then_inc(orms_made, 1)

            def o_hi(b):
                act.wait_ge(of_made, b + 1)
                nc.scalar.activation(ozh[:, HG * b:HG * b + HG], onorm[:], ACT.Copy).then_inc(ozh_made, 1)

            tasks = {1: [(o_square, 0)], 2: [(o_root, 0)], 3: [(o_hi, 0), (o_square, 1)], 4: [(o_root, 1)],
                     5: [(o_hi, 1)]}
            for c in range(KC):
                hi(PB + 2 * c + 2)
                hi(PB + 2 * c + 3)
                g = G_PB + c
                func(g, ta[:, c % 2, 0:T], ps[:, bank(g), 0:T], ACT.Sigmoid, unit=PB + 2 * c + 1,
                     bias=vecs[:, V_BGATE + 8 + c:V_BGATE + 9 + c])
                while queue:
                    scan_step(*queue.pop(0))
                for f, b in tasks.get(c, []):
                    f(b)
            for c in range(KC):
                hi(PA + c + 2)
                act.wait_ge(yf_made, c + 1)
                nc.scalar.activation(yh[:, c], tb[:, c % 2, 0:T], ACT.Copy).then_inc(yh_made, 1)
            nc.scalar.preload_act_table(ACT.Sqrt)
            for c in range(KC):
                hi(WO + c + 2)
                act.wait_ge(bank_read, G_WO + c + 1)
                square(3, lat, c)
            root(3, T, 2 * T)
            for c in range(KC):
                u_hi(3, 1, c, 6)
            nc.scalar.preload_act_table(ACT.Silu)
            with act.Fori(0, 11) as i:
                up_body(UP2, G_UP2, i, 4, T)
            nc.scalar.preload_act_table(ACT.Sqrt)
            down_body(DOWN2, down_units(), [], G_DOWN2, 4, lat)
            root(4, T, 2 * T)

        @block.gpsimd
        def _(pool):
            nc.gpsimd.memset(ones[:], 1.0).then_inc(ready, 1)
            nc.gpsimd.memset(eps[:], EPS).then_inc(ready, 1)

            pool.wait_ge(unit_done, GLU)
            pool.wait_ge(dot_made, ADA - ADA_PE)
            nc.gpsimd.memset(glu[:, :, 0:PAD], 0.0)
            nc.gpsimd.memset(glu[:, :, PAD + T:GLUW], 0.0).then_inc(ready, 1)
            nc.gpsimd.memset(dec[:, 0, :, T - 1:T], 1.0)
            nc.gpsimd.memset(dec[:, 1, :, 0:1], 1.0).then_inc(ready, 1)
            for n in range(*SPLIT_POOL):
                pool.wait_ge(hi_made, n + 1)
                nc.gpsimd.tensor_tensor(wl[:, n % 4], raw[:, n % 4], wh[:, n % 4].bitcast(F32),
                                        ALU.subtract).then_inc(lo_pool, 1)

            pool.wait_ge(conv_step, KC * TAPS)
            pool.wait_ge(masks_in, 16)
            nc.gpsimd.tensor_copy(masks[:], masks_f[:]).then_inc(masks_made, 1)
            pool.wait_ge(masks_made, 1)
            for level in range(1, 8):
                m = 1 << (level - 1)
                for gr in range(2):
                    if level == 1:
                        pool.wait_ge(q_first, gr + 1)
                    pool.wait_ge(khat_made[gr], level)
                    if level > 1:
                        pool.wait_ge(tot_up[gr], level - 1)
                        pool.wait_ge(k_up[gr], level - 1)
                        pool.wait_ge(q_up[gr], level - 1)
                    tk = tot_pairs(gr, m, swap=True)
                    x = k_pairs(gr, m)
                    nc.gpsimd.tensor_tensor(x, x, tk, ALU.mult).then_inc(k_up[gr], 1)
                    even, odd, dst = tot_halves(gr, m)
                    nc.gpsimd.tensor_tensor(dst, even, odd, ALU.mult).then_inc(tot_up[gr], 1)

        @block.vector
        def _(dve):
            links = [0]

            def link(ins):
                links[0] += 1
                ins.then_inc(chain, 1)
                dve.wait_ge(chain, links[0])

            def lo(n, k=8, i=0, per=0):
                dve.wait_ge(hi_made, n + 1 + per * i)
                nc.vector.tensor_tensor(wl[:, n % 4, 0:k], raw[:, n % 4, 0:k], wh[:, n % 4, 0:k].bitcast(F32),
                                        ALU.subtract).then_inc(lo_dve, 1)

            def col(o):
                return vecs[:, o:o + 1]

            def gain(which, m, norm, w=0):
                g = vecs[:, norm:norm + 8].unsqueeze(2).to_broadcast([P, KC, 2 - w])
                link(nc.vector.scalar_tensor_tensor(scale[:, which, :, w:2], mod[:, 8 * m:8 * m + 8, w:2], 1.0, g,
                                                    ALU.add, ALU.mult))

            def half(which, m, w=0):
                link(nc.vector.tensor_scalar(half_gate[:, which, :, w:2], mod[:, 8 * m:8 * m + 8, w:2], 0.5, None,
                                             ALU.mult))

            def dot(a, slot, ways, i=0, per=0, terms=junk):
                dve.wait_ge(ada_in[a % 2], 16 * (a // 2 + 1) + 8 * per * i)
                if a:
                    dve.wait_ge(dot_made, a + per * i)
                src = ada_raw[:, a % 2]
                if ways == 2:
                    nc.vector.tensor_tensor_reduce(out=terms[:], in0=src, in1=csil_all[:, 0], scale=1.0, scalar=0.0,
                                                   op0=ALU.mult, op1=ALU.add,
                                                   accum_out=dots[:, slot, 0:1]).then_inc(dot_both, 1)
                    dve.wait_ge(dot_both, a + 1 + per * i)
                nc.vector.tensor_tensor_reduce(out=src, in0=src, in1=csil_all[:, 1], scale=1.0, scalar=0.0,
                                               op0=ALU.mult, op1=ALU.add,
                                               accum_out=dots[:, slot, 1:2]).then_inc(dot_made, 1)

            def add_bias(a, n, ways, i=0, per=0, k=0):
                dve.wait_ge(dot_made, a + n + per * i)
                if per:
                    to = mod[:, bass.ds(per * i + (ADA_PE + a), n), 2 - ways:2]
                    bias = vecs[:, bass.ds(per * i + (V_BADA + ADA_PE + a), n)]
                else:
                    to = mod[:, ADA_PE + a:ADA_PE + a + n, 2 - ways:2]
                    bias = vecs[:, V_BADA + ADA_PE + a:V_BADA + ADA_PE + a + n]
                nc.vector.tensor_tensor(to, dots[:, 0:n, 2 - ways:2], bias.unsqueeze(2).to_broadcast([P, n, ways]),
                                        ALU.add).then_inc(dots_read, 1)
                dve.wait_ge(dots_read, k + 1 + i)

            def add_squares(which, w, c):
                n = 8 * SUMS.index(which) + c
                a, b = 2 * T - w, 2 * T
                dve.wait_ge(sq_made, n + 1)
                if c:
                    dve.wait_ge(ssq_made, n)
                    nc.vector.tensor_tensor(ssq[:, a:b], ssq[:, a:b], ta[:, c % 2, a:b], ALU.add).then_inc(ssq_made, 1)
                else:
                    nc.vector.tensor_copy(ssq[:, a:b], ta[:, 0, a:b]).then_inc(ssq_made, 1)

            def invert(which, a, b):
                dve.wait_ge(rms_made, which + 1)
                nc.vector.reciprocal(rstd[:, a:b], rstd[:, a:b]).then_inc(rstd_made, 1)
                dve.wait_ge(rstd_made, which + 1)

            def normed(which, s, c, sc):
                if c >= 2:
                    dve.wait_ge(ul_made, 8 * which + c - 1)
                nc.vector.scalar_tensor_tensor(tb[:, c % 2, T:2 * T], h[:, s, c], scale[:, sc, c, s:s + 1],
                                               rstd[:, s * T:s * T + T], ALU.mult, ALU.mult).then_inc(uf_made, 1)

            def u_lo(which, s, c, shift):
                dve.wait_ge(uh_made, 8 * which + c + 1)
                nc.vector.scalar_tensor_tensor(ul[:, s, c], tb[:, c % 2, T:2 * T], mod[:, 8 * shift + c, s:s + 1],
                                               uh[:, s, c].bitcast(F32), ALU.add, ALU.subtract).then_inc(ul_made, 1)

            both, con, lat = slice(0, 2), slice(0, 1), slice(1, 2)
            for c in range(KC):
                add_squares(0, 2 * T, c)
            invert(0, 0, 2 * T)
            for c in range(KC):
                nc.vector.tensor_tensor(t_first[:, :, c], h[:, :, c], rstd[:].rearrange("p (a t) -> p a t", t=T),
                                        ALU.mult).then_inc(tf_made, 1)
                if c == 1:
                    dve.wait_ge(csil_ps, 1)
                if c in (1, 4):
                    dot(c // 3, c // 3, 2, terms=junk0)
            dot(2, 2, 2, terms=junk0)
            lo(UP1)
            dot(3, 3, 2, terms=junk0)
            dve.wait_ge(small_in, 32)
            add_bias(0, 4, 2)
            dve.wait_ge(ada0_done, ADA_GROUPS)
            bias = vecs[:, V_BADA:V_BADA + ADA_PE].unsqueeze(2).to_broadcast([P, ADA_PE, 2])
            link(nc.vector.tensor_tensor(mod[:, 0:ADA_PE], ps[:, 2, 0:2 * ADA_PE].rearrange(
                "p (a t) -> p a t", t=2), bias, ALU.add))
            gain(0, 1, V_N1)
            assert links[0] == MOD_FIRST
            dve.wait_ge(tf_made, KC)
            for c in range(KC + 1):
                if c < KC:
                    if c >= 2:
                        dve.wait_ge(ul_made, c - 1)
                    nc.vector.tensor_scalar(tb[:, c % 2, T:2 * T], t_first[:, 1, c], scale[:, 0, c, 1:2],
                                            mod[:, c, 1:2], ALU.mult, ALU.add).then_inc(uf_made, 1)
                if c:
                    dve.wait_ge(uh_made, c)
                    nc.vector.tensor_tensor(ul[:, :, c - 1], tb[:, (c - 1) % 2].rearrange("p (a t) -> p a t", t=T),
                                            uh[:, :, c - 1].bitcast(F32), ALU.subtract).then_inc(ul_made, 1)
                if c == 1:
                    lo(UP1 + 1)

            def up_body(first, g0, j0, i, per, w, ah, al, js, after=None):
                for s in range(2):
                    for e in range(2):
                        lo(first + 2 * s + e + 2, i=i, per=per)
                    g = g0 + s
                    dve.wait_ge(act_made, acts(g) + 2 * i)
                    nc.vector.tensor_tensor(tb[:, s, 0:w], ta[:, s, 0:w], ps[:, 2 * s + 1, 0:w],
                                            ALU.mult).then_inc(bank_read, 1)
                    dve.wait_ge(bank_read, g + 1 + 2 * i)
                    j = js + j0 + s
                    at_j = j0 + s + 2 * i
                    hj = ah[:, bass.ds(at_j, 1)] if per else ah[:, at_j:at_j + 1]
                    lj = al[:, bass.ds(at_j, 1)] if per else al[:, at_j:at_j + 1]
                    f = tb[:, s, 0:w].unsqueeze(1)
                    nc.vector.tensor_copy(hj, f).then_inc(acth_made, 1)
                    dve.wait_ge(acth_made, j + 1 + 2 * i)
                    nc.vector.tensor_tensor(lj, f, hj.bitcast(F32), ALU.subtract).then_inc(actl_made, 1)
                    if after:
                        after(s)

            ah, al = (x[:].rearrange("p f a t -> p f (a t)") for x in (act_h, act_l))
            def dots_beside(a, k, ways, i=0, per=0):
                def after(s):
                    dot(a + 2 * s, 2 * s, ways, i, per)
                    dot(a + 2 * s + 1, 2 * s + 1, ways, i, per)
                    if s:
                        add_bias(a, 4, ways, i, per, k)
                return after

            up_body(UP1, G_UP1, 0, 0, 0, 512, ah, al, 0, dots_beside(4, 1, 2))
            with dve.Fori(0, 5) as i:
                up_body(UP1 + 4, G_UP1 + 2, 2, i, 4, 512, ah, al, 0, dots_beside(8, 2, 2, i, 4))
            with dve.Fori(0, 5) as i:
                up_body(UP1 + 24, G_UP1 + 12, 12, i, 4, 512, ah, al, 0, dots_beside(28, 7, 1, i, 4))
            half(0, 2)
            gain(1, 4, V_NM)
            l0, l1 = vecs[:, V_LB:V_LB + 16], vecs[:, V_LB + 16:V_LB + 32]
            link(nc.vector.tensor_tensor(lbt[:, 0], l0, l1, ALU.max))
            nc.vector.tensor_tensor(lbt[:, 1], l0, lbt[:, 0], ALU.subtract)
            nc.vector.tensor_tensor(lbt[:, 2], l1, lbt[:, 0], ALU.subtract).then_inc(logits_made, 1)
            dve.wait_ge(exp_made, 1)
            link(nc.vector.tensor_tensor(lbt[:, 3], lbt[:, 1], lbt[:, 2], ALU.add))
            link(nc.vector.reciprocal(lbt[:, 0], lbt[:, 3]))
            link(nc.vector.tensor_tensor(lbt[:, 4], lbt[:, 1], lbt[:, 0], ALU.mult))
            link(nc.vector.tensor_scalar(lbt[:, 5], lbt[:, 4], -1.0, 1.0, ALU.mult, ALU.add))

            def down_body(first, units, after, g0, gates, which, halves):
                units = list(units)
                w = T * (halves.stop - halves.start)
                ks = ahead(units, after)
                for e in range(len(units)):
                    c, k0, k = units[e]
                    if which == 1 and e == len(units) - 1:
                        dve.wait_ge(lat_ps, 1)
                        add_product(c, bank(g0 + c), gates, 1, 0).then_inc(lat_added, 1)
                        add_squares(which, 2 * T, c - 1)
                        add_squares(which, T, c)
                        lo(first + e + 2, ks[e])
                        return
                    if e < len(ks):
                        lo(first + e + 2, ks[e])
                    if which == 1 and e == len(units) - 2:
                        for a in ada_beside(c):
                            dot(a - ADA_PE, a - ADA_FIRST - ADA_UP, 1)
                    if k0 + k == FC:
                        down_epilogue(c, first + e, g0, gates, which, halves, w)
                        if g0 == G_DOWN1:
                            for a in ada_beside(c):
                                dot(a - ADA_PE, a - ADA_FIRST - ADA_UP, 1)
                add_squares(which, w, KC - 1)

            def add_product(c, bk, gates, s, j):
                return nc.vector.scalar_tensor_tensor(h[:, s, c], ps[:, bk, j * T:j * T + T],
                                                      half_gate[:, gates, c, s:s + 1], h[:, s, c], ALU.mult, ALU.add)

            def down_epilogue(c, n, g0, gates, which, halves, w):
                dve.wait_ge(unit_done, n + 1)
                for s in range(halves.start, halves.stop):
                    x = add_product(c, bank(g0 + c), gates, s, s - halves.start)
                x.then_inc(bank_read, 1)
                if c:
                    add_squares(which, w, c - 1)

            down_body(DOWN1, down_units(), [8, 8], G_DOWN1, 0, 1, both)
            invert(1, T, 2 * T)
            for c in range(KC + 1):
                if c < KC:
                    normed(1, 1, c, 1)
                if c:
                    u_lo(1, 1, c - 1, 3)
                if c == 3:
                    dve.wait_ge(unit_done, GLU)
                    add_product(KC - 1, bank(G_DOWN1 + KC - 1) + 1, 0, 0, 0).then_inc(bank_read, 1)
                if c == 6:
                    dve.wait_ge(con_square, 1)
                    nc.vector.tensor_tensor(ssq[:, 0:T], ssq[:, 0:T], ta[:, 1, 0:T], ALU.add).then_inc(con_ssq, 1)
            add_bias(ADA_FIRST + ADA_UP - ADA_PE, ADA - ADA_FIRST - ADA_UP, 1, k=12)
            gain(2, 7, V_N2, 1)
            half(1, 8, 1)
            invert(2, 0, T)
            dve.wait_ge(ready, 4)

            steps = [(c, tap) for c0 in range(0, KC, 2) for tap in range(TAPS) for c in (c0, c0 + 1)]
            done = [0]

            def convolve(count):
                for _ in range(count):
                    if done[0] == len(steps):
                        return
                    c, tap = steps[done[0]]
                    src = glu[:, c, tap:tap + T]
                    w = wdw[:, tap, c:c + 1]
                    if tap == 0:
                        dve.wait_ge(bank_read, G_GLU + c + 1)
                        dve.wait_ge(ul_made, 16 + c + 1)
                        x = nc.vector.tensor_scalar(hb[:, c], src, w, col(V_BDW + c), ALU.mult, ALU.add)
                    else:
                        dve.wait_ge(conv_step, done[0] - 1)
                        x = nc.vector.scalar_tensor_tensor(hb[:, c], src, w, hb[:, c], ALU.mult, ALU.add)
                    x.then_inc(conv_step, 1)
                    done[0] += 1

            for c in range(KC):
                if c < 7:
                    lo(GLU + 2 * c + 2)
                    lo(GLU + 2 * c + 3)
                normed(2, 0, c, 1)
                g = G_GLU + c
                dve.wait_ge(act_made, acts(g))
                nc.vector.tensor_tensor(glu[:, c, PAD:PAD + T], ps[:, bank(g), 0:T], ta[:, c % 2, 0:T],
                                        ALU.mult).then_inc(bank_read, 1)
                u_lo(2, 0, c, 3)
                if c:
                    convolve(GLU_STEPS)

            for c in range(2):
                convolve(V_STEPS[c])
                dve.wait_ge(act_made, acts(G_V + c))
                for b in (2, 3):
                    x = nc.vector.tensor_copy(v[:, b, 512 * c:512 * c + 512], ps[:, (4 - 4 * c) + b])
                x.then_inc(bank_read, 1)

            for j in range(16):
                way, hd = divmod(j, HEADS)
                gr, hl = divmod(hd, HG)
                g = G_Z + j
                lb, oml = lbt[:, 4, j:j + 1], lbt[:, 5, j:j + 1]
                dve.wait_ge(act_made, acts(g))
                f = kdec[:, way, hd]
                nc.vector.tensor_scalar(f, ta[:, j % 2, 0:T], oml, lb, ALU.mult, ALU.add).then_inc(z_step, 1)
                fl = tot1[gr][:, 1 - way, hl]
                nc.vector.tensor_scalar(fl, ta[:, j % 2, T:2 * T], oml, lb, ALU.mult, ALU.add).then_inc(bank_read, 1)
                dve.wait_ge(z_step, 3 * j + 1)
                if way == 0:
                    dst, src = dec[:, 0, j % 2, T - 2::-1], f[:, T - 1:0:-1]
                else:
                    dst, src = dec[:, 1, j % 2, 1:T], f[:, 0:T - 1]
                nc.vector.tensor_tensor_scan(dst, src, src, 1.0, ALU.mult, ALU.bypass).then_inc(z_step, 1)
                dve.wait_ge(bank_read, g + 1)
                nc.vector.tensor_scalar(K[:, way, hd], fl, -1.0, 1.0, ALU.mult, ALU.add)
                dve.wait_ge(z_step, 3 * j + 2)
                nc.vector.scalar_tensor_tensor(f, f, -1.0, dec[:, way, j % 2], ALU.add, ALU.mult).then_inc(z_step, 1)
                convolve(Z_STEPS)
                if j >= 14:
                    lo(QQ + j - 14)
            convolve(KC * TAPS)

            per_token = hb[:].rearrange("p c t -> p t c")
            bcast = lambda x: x.unsqueeze(1).to_broadcast([P, KC, T])
            dve.wait_ge(conv_step, KC * TAPS)
            for j in range(8):
                lo(QQ + j + 2)
                g = G_Q + j
                dve.wait_ge(act_made, acts(g))
                nc.vector.tensor_tensor(q[:, j], ps[:, bank(g), 0:T], ta[:, j % 2, 0:T], ALU.mult).then_inc(bank_read, 1)
                if j == 0:
                    nc.vector.tensor_reduce(ssq[:, 0:T], per_token, AX.X, ALU.add).then_inc(ln_dve, 1)
                if j == 2:
                    dve.wait_ge(ln_ps, 1)
                    nc.vector.tensor_scalar(rstd[:, 0:T], ps[:, 6, 0:T], 1.0 / D, None, ALU.mult).then_inc(ln_dve, 1)
                    dve.wait_ge(ln_dve, 2)
                    nc.vector.tensor_tensor(hb[:], hb[:], bcast(rstd[:, 0:T]), ALU.subtract).then_inc(ln_dve, 1)
                if j == 4:
                    dve.wait_ge(ln_act, 1)
                    nc.vector.tensor_reduce(ssq[:, T:2 * T], lnsq[:].rearrange("p c t -> p t c"), AX.X,
                                            ALU.add).then_inc(ln_dve, 1)
                if j == 6:
                    dve.wait_ge(ln_act, 2)
                    nc.vector.reciprocal(rstd[:, T:2 * T], rstd[:, T:2 * T]).then_inc(ln_dve, 1)
                    dve.wait_ge(ln_dve, 5)
                    nc.vector.tensor_tensor(hb[:], hb[:], bcast(rstd[:, T:2 * T]), ALU.mult).then_inc(ln_dve, 1)

            dve.wait_ge(bank_read, G_GO)
            dve.wait_ge(turned, HEADS)
            for gr in range(2):
                qv = q[:, HG * gr:HG * gr + HG].rearrange("p h t -> p (h t)").unsqueeze(1).to_broadcast([P, 2, HG * T])
                nc.vector.tensor_tensor(Q[:, :, HG * gr:HG * gr + HG].rearrange("p a h t -> p a (h t)"),
                                        tot1[gr][:].rearrange("p a h t -> p a (h t)"), qv,
                                        ALU.mult).then_inc(q_first, 1)
            nc.vector.tensor_copy(lbt[:, 0], lbt[:, 1]).then_inc(ln_dve, 1)
            dve.wait_ge(ln_dve, 7)
            nc.vector.tensor_copy(lbt[:, 0], lbt[:, 1]).then_inc(ln_dve, 1)

            def level_dve(gr, level):
                m = 1 << (level - 1)
                dve.wait_ge(level_ps[gr], level + 1)
                if level <= 7:
                    if level == 1:
                        dve.wait_ge(masks_made, 1)
                        dve.wait_ge(a_act[gr], 1)
                    else:
                        dve.wait_ge(a_dve[gr], level - 1)
                    diag = bass.AP(A[gr], 0, [[HG * 2 * T, P], [2 * T, HG], [T + P, 2], [1, P]])
                    x = ps[:, 4 + 2 * gr:6 + 2 * gr].rearrange("p a (h b t) -> p (a h) b t", h=2, b=2)
                    mk = bass.AP(masks, (level - 1) * P, [[7 * P, P], [0, HG], [0, 2], [1, P]])
                    nc.vector.copy_predicated(diag, mask=mk, data=x).then_inc(a_dve[gr], 1)
                    if level > 1:
                        dve.wait_ge(tot_up[gr], level - 1)
                        dve.wait_ge(q_up[gr], level - 1)
                    x = q_pairs(gr, m)
                    nc.vector.tensor_tensor(x, x, tot_pairs(gr, m, swap=False), ALU.mult).then_inc(q_up[gr], 1)
                else:
                    dve.wait_ge(tot_up[gr], 7)
                    dve.wait_ge(q_up[gr], 7)
                    x = q_pairs(gr, m)
                    nc.vector.tensor_tensor(x, x, tot_pairs(gr, m, swap=False), ALU.mult).then_inc(q_up[gr], 1)

            def z_dve(c):
                if c == 0:
                    for gr in range(2):
                        dve.wait_ge(k_up[gr], 1)
                        dve.wait_ge(tot_up[gr], 1)
                        dve.wait_ge(q_up[gr], 1)
                nc.vector.tensor_scalar(tb[:, c % 2, T:2 * T], hb[:, c], col(V_LNG + c), col(V_LNB + c),
                                        ALU.mult, ALU.add).then_inc(chain, 1)
                links[0] += 1
                dve.wait_ge(chain, links[0])
                dve.wait_ge(zs_made, c + 1)
                nc.vector.tensor_tensor(tb[:, c % 2, T:2 * T], tb[:, c % 2, T:2 * T], tb[:, c % 2, 0:T],
                                        ALU.mult).then_inc(zf_made, 1)
                dve.wait_ge(zh_made, c + 1)
                nc.vector.tensor_tensor(zl[:, c], tb[:, c % 2, T:2 * T], zh[:, c].bitcast(F32),
                                        ALU.subtract).then_inc(zl_made, 1)

            queue = [(gr, level) for level in range(9) for gr in range(2)]

            def scan_step():
                if queue:
                    gr, level = queue.pop(0)
                    if level:
                        level_dve(gr, level)

            for j in range(8):
                lo(GO + j + 2)
                g = G_GO + j
                dve.wait_ge(act_made, acts(g))
                nc.vector.tensor_tensor(gout[:, j], ps[:, bank(g), 0:T], ta[:, j % 2, 0:T], ALU.mult).then_inc(bank_read, 1)
                scan_step()
                if j >= 4:
                    z_dve(j - 4)
            for j in range(8):
                lo(GA + j + 2)
                g = G_GA + j
                dve.wait_ge(act_made, acts(g))
                nc.vector.tensor_copy(ga[:, j], ta[:, j % 2, 0:T]).then_inc(bank_read, 1)
                scan_step()
                if j < 4:
                    z_dve(j + 4)

            def o_dve(b):
                dve.wait_ge(orms_made, b + 1)
                link(nc.vector.reciprocal(orms[:], orms[:]))
                link(nc.vector.tensor_tensor(onorm[:].rearrange("p (a h) t -> p a (h t)", a=2),
                                             ps[:, 4 + 2 * b:6 + 2 * b],
                                             orms[:].rearrange("p (a h) t -> p a (h t)", a=2), ALU.mult))
                nc.vector.scalar_tensor_tensor(onorm[:], onorm[:], col(V_HN), gout[:, HG * b:HG * b + HG],
                                               ALU.mult, ALU.mult).then_inc(of_made, 1)

            def o_lo(b):
                dve.wait_ge(ozh_made, b + 1)
                nc.vector.tensor_tensor(ozl[:, HG * b:HG * b + HG], onorm[:],
                                        ozh[:, HG * b:HG * b + HG].bitcast(F32), ALU.subtract).then_inc(ozl_made, 1)

            tasks = {2: (o_dve, 0), 3: (o_lo, 0), 4: (o_dve, 1), 5: (o_lo, 1)}
            for c in range(KC):
                lo(PB + 2 * c + 2)
                lo(PB + 2 * c + 3)
                g = G_PB + c
                dve.wait_ge(act_made, acts(g))
                nc.vector.tensor_tensor(yb[:, c], ps[:, bank(g) + 1, 0:T], ta[:, c % 2, 0:T], ALU.mult).then_inc(bank_read, 1)
                while queue:
                    scan_step()
                if c in tasks:
                    f, b = tasks[c]
                    f(b)
            for c in range(KC):
                lo(PA + c + 2)
                g = G_PA + c
                dve.wait_ge(unit_done, PA + c + 1)
                nc.vector.tensor_tensor(tb[:, c % 2, 0:T], ps[:, bank(g), 0:T], ga[:, c], ALU.mult).then_inc(bank_read, 1)
                dve.wait_ge(bank_read, g + 1)
                nc.vector.tensor_tensor(tb[:, c % 2, 0:T], tb[:, c % 2, 0:T], yb[:, c], ALU.add).then_inc(yf_made, 1)
                dve.wait_ge(yh_made, c + 1)
                nc.vector.tensor_tensor(yl[:, c], tb[:, c % 2, 0:T], yh[:, c].bitcast(F32),
                                        ALU.subtract).then_inc(yl_made, 1)
            for c in range(KC):
                lo(WO + c + 2)
                g = G_WO + c
                dve.wait_ge(unit_done, WO + c + 1)
                nc.vector.scalar_tensor_tensor(h[:, 1, c], ps[:, bank(g), 0:T], mod[:, 40 + c, 1:2], h[:, 1, c],
                                               ALU.mult, ALU.add).then_inc(bank_read, 1)
                if c:
                    add_squares(3, T, c - 1)
            add_squares(3, T, KC - 1)
            invert(3, T, 2 * T)
            for c in range(KC + 1):
                if c < KC:
                    normed(3, 1, c, 2)
                if c:
                    u_lo(3, 1, c - 1, 6)
            with dve.Fori(0, 11) as i:
                up_body(UP2, G_UP2, 0, i, 4, T, act2_h, act2_l, 22)
            down_body(DOWN2, down_units(), [], G_DOWN2, 1, 4, lat)
            invert(4, T, 2 * T)
            for c in range(KC):
                nc.vector.scalar_tensor_tensor(h[:, 1, c], h[:, 1, c], col(V_NF + c), rstd[:, T:2 * T],
                                               ALU.mult, ALU.mult).then_inc(out_made, 1)

        @block.tensor
        def _(pe):
            def three(out, w_hi, w_lo, x_hi, x_lo, start, stop):
                nc.tensor.matmul(out, w_hi, x_hi, start=start, stop=False)
                nc.tensor.matmul(out, w_hi, x_lo, start=False, stop=False)
                return nc.tensor.matmul(out, w_lo, x_hi, start=False, stop=stop)

            def unit(n, out, xs, k0=0, k=8, start=True, stop=True, i=0, per=0, need=None, made=ul_made,
                     signal=unit_done):
                lo_wait(pe, n, i, per)
                for j in range(k):
                    if need is not None:
                        pe.wait_ge(made, need + j + 1)
                    x = three(out, wh[:, n % 4, j], wl[:, n % 4, j], *xs(k0 + j),
                              start=start and j == 0, stop=stop and j == k - 1)
                if signal is not None:
                    x.then_inc(signal, 1)

            def free(g, i=0, per=0):
                if g >= 2:
                    pe.wait_ge(bank_read, g - 1 + per * i)

            def out512(b):
                return ps[:, b].rearrange("p (a t) -> p a t", a=2)

            u_both = lambda k: (uh[:, :, k], ul[:, :, k])
            u_lat = lambda k: (uh[:, 1, k], ul[:, 1, k])

            def statistics(which, a, b, bk=7):
                if which == 2:
                    pe.wait_ge(con_ssq, 1)
                else:
                    pe.wait_ge(ssq_made, 8 * SUMS.index(which) + 8)
                nc.tensor.matmul(ps[:, bk, a:b], ones[:], ssq[:, a:b], start=True, stop=True).then_inc(stat_made, 1)

            pe.wait_ge(ready, 1)
            pe.wait_ge(c_row_made, 1)
            for n in range(4):
                x = nc.tensor.matmul(ps[:, 4 + n], ones[0:1], c_row[0:1].rearrange("p x n -> p (x n)")[
                    :, 512 * n:512 * n + 512], start=True, stop=True)
            x.then_inc(csil_ps, 1)

            def columns(g):
                pe.wait_ge(mrow_made, g + 1)
                for e in range(4):
                    a = 4 * g + e
                    x = nc.tensor.matmul(ps[:, 2, 2 * a:2 * a + 2], mrow[0:2, g, P * e:P * e + P], ident0[0:2],
                                         start=True, stop=True)
                x.then_inc(ada0_done, 1)

            pe.wait_ge(cvec_in, 32)
            pe.wait_ge(csil_made, 1)
            for g in range(ADA_GROUPS):
                if g == 2:
                    pe.wait_ge(mrow_made, 1)
                for k in range(KC):
                    if k % 4 == 0:
                        pe.wait_ge(ada0_in[2 * g + k // 4], 16)
                    x = nc.tensor.matmul(ps[0:2, g % 2], csil[:, k], ada0[:, g, k], start=(k == 0), stop=(k == KC - 1))
                x.then_inc(ada0_ps, 1)
                if g == 0:
                    statistics(0, 0, 2 * T, 3)
                else:
                    columns(g - 1)
            columns(2)

            def up_body(first, g0, i, per, w, xs, need=None):
                for s in range(2):
                    g = g0 + s
                    free(g, i, 2)
                    for e in range(2):
                        b = 2 * s + e
                        unit(first + b, out512(b) if w == 512 else ps[:, b, 0:w], xs, i=i, per=per,
                             need=need if b == 0 else None)

            up_body(UP1, G_UP1, 0, 0, 512, u_both, need=0)
            with pe.Fori(0, 10) as i:
                up_body(UP1 + 4, G_UP1 + 2, i, 4, 512, u_both)

            def down_body(first, units, g0, js, xs, view):
                for n, (c, k0, k) in enumerate(units, first):
                    if k0 == 0:
                        free(g0 + c)
                    if c == 0:
                        pe.wait_ge(actl_made, js + k0 + k)
                    unit(n, view(bank(g0 + c)), xs, k0, k, start=(k0 == 0), stop=(k0 + k == FC))

            units = list(down_units())
            down_body(DOWN1, units[:-3], G_DOWN1, 0, lambda k: (act_h[:, k], act_l[:, k]), out512)
            bk = bank(G_DOWN1 + KC - 1)
            free(G_DOWN1 + KC - 1)
            for s in (1, 0):
                for n, (c, k0, k) in enumerate(units[-3:], GLU - 3):
                    if s == 0 and n == GLU - 1:
                        statistics(1, T, 2 * T, 1)
                    unit(n, ps[:, bk + 1 - s, 0:T], lambda j: (act_h[:, j, s], act_l[:, j, s]), k0, k,
                         start=(k0 == 0), stop=(k0 + k == FC), signal=unit_done if s == 0 else lat_ps if n == GLU - 1 else None)
            for c in range(KC):
                g = G_GLU + c
                free(g)
                unit(GLU + 2 * c, ps[:, bank(g), 0:T], u_lat, need=8 if c == 0 else None)
                if c == 0:
                    pe.wait_ge(dot_made, ADA - ADA_PE)
                    statistics(2, 0, T, 5)
                unit(GLU + 2 * c + 1, ps[:, bank(g) + 1, 0:T], u_lat)
            pe.wait_ge(ul_made, 24)
            for c in range(2):
                pe.wait_ge(bank_read, G_GLU if c == 0 else G_V)
                for j in range(4):
                    n = VV + 4 * c + j
                    lo_wait(pe, n)
                    w_hi = wh[:, n % 4].rearrange("p k c -> p (k c)")
                    w_lo = wl[:, n % 4].rearrange("p k c -> p (k c)")
                    for e in range(2):
                        k = 2 * j + e
                        for b in range(4):
                            uhb = uh[:, b // 2, k, P * (b % 2):P * (b % 2) + P]
                            ulb = ul[:, b // 2, k, P * (b % 2):P * (b % 2) + P]
                            x = three(ps[:, (4 - 4 * c) + b], uhb, ulb, w_hi[:, 512 * e:512 * e + 512],
                                      w_lo[:, 512 * e:512 * e + 512], start=(k == 0), stop=(k == KC - 1))
                    x.then_inc(unit_done, 1)
            for j in range(16):
                g = G_Z + j
                if j < 2:
                    pe.wait_ge(bank_read, G_Z)
                else:
                    free(g)
                unit(ZZ + j, out512(bank(g)), u_both)
            pe.wait_ge(ident_in, 16)

            def states(j):
                pe.wait_ge(turned_read, j + 1)
                if j:
                    pe.wait_ge(state_made, j)
                for way in range(2):
                    for b in range(2):
                        x = nc.tensor.matmul(ps[:, 5, way * P:way * P + P],
                                             tb[:, j % 2, (2 * way + b) * P:(2 * way + b) * P + P],
                                             v[:, b, P * j:P * j + P], start=(b == 0), stop=(b == 1))
                x.then_inc(state_ps, 1)

            for j in range(8):
                g = G_Q + j
                free(g)
                unit(QQ + j, ps[:, bank(g), 0:T], u_lat)
                if j == 0:
                    pe.wait_ge(z_step, 48)
                else:
                    pe.wait_ge(turned_read, j)
                for way in range(2):
                    for b in range(2):
                        x = nc.tensor.transpose(ps[:, 4, (2 * way + b) * P:(2 * way + b) * P + P],
                                                kdec[:, way, j, P * b:P * b + P], ident[:])
                x.then_inc(turned, 1)
                if j:
                    states(j - 1)
                if j == 1:
                    pe.wait_ge(ln_dve, 1)
                    nc.tensor.matmul(ps[:, 6, 0:T], ones[:], ssq[:, 0:T], start=True, stop=True).then_inc(ln_ps, 1)
                if j == 5:
                    pe.wait_ge(ln_dve, 4)
                    nc.tensor.matmul(ps[:, 7, 0:T], ones[:], ssq[:, T:2 * T], start=True, stop=True).then_inc(ln_ps, 1)
            states(7)

            def level_mm(gr, level):
                m = 1 << max(level - 1, 0)
                if level == 0:
                    pe.wait_ge(q_first, gr + 1)
                    if gr == 0:
                        pe.wait_ge(state_made, HEADS)
                else:
                    if level == 1:
                        pe.wait_ge(a_act[gr], 1)
                    else:
                        pe.wait_ge(a_dve[gr], level - 1)
                        pe.wait_ge(q_up[gr], level - 1)
                    if level < 8:
                        pe.wait_ge(khat_made[gr], level)
                    else:
                        pe.wait_ge(k_up[gr], 7)
                for hl in range(HG):
                    hd = HG * gr + hl
                    for b in range(2):
                        out = ps[:, 4 + 2 * gr + hl // 2, (hl % 2) * T + b * P:(hl % 2) * T + b * P + P]
                        if level == 0:
                            for way in range(2):
                                x = nc.tensor.matmul(out, K[:, way, hd, P * b:P * b + P], q[:, hd, P * b:P * b + P],
                                                     start=(way == 0), stop=(way == 1))
                        elif level < 8:
                            o3 = out.rearrange("p (n a m) -> p n a m", a=2, m=m)
                            x = nc.tensor.matmul(out, khat[:, gr, hl, P * b:P * b + P], operand(Q, hd, b, m), start=True, stop=True)
                        else:
                            x = nc.tensor.matmul(out, K[:, b, hd, P * b:P * b + P],
                                                 Q[:, 1 - b, hd, P * (1 - b):P * (1 - b) + P], start=True, stop=True)
                x.then_inc(level_ps[gr], 1)

            queue = [(gr, level) for level in range(9) for gr in range(2)]
            for first, g0 in ((GO, G_GO), (GA, G_GA)):
                for j in range(8):
                    free(g0 + j)
                    unit(first + j, ps[:, bank(g0 + j), 0:T], u_lat)
                    level_mm(*queue.pop(0))

            def o_mm(b):
                if b == 0:
                    for gr in range(2):
                        pe.wait_ge(a_act[gr], 2)
                        pe.wait_ge(q_up[gr], 8)
                else:
                    pe.wait_ge(orms_made, 1)
                for hl in range(HG):
                    hd = HG * b + hl
                    out = ps[:, 4 + 2 * b + hl // 2, (hl % 2) * T:(hl % 2) * T + T]
                    for s in range(2):
                        nc.tensor.matmul(out, v[:, 2 + s, P * hd:P * hd + P], A[b][:, hl, s], start=(s == 0), stop=False)
                    nc.tensor.matmul(out, state[:, hd, 0], Q[:, 1, hd], start=False, stop=False)
                    x = nc.tensor.matmul(out, state[:, hd, 1], Q[:, 0, hd], start=False, stop=True)
                x.then_inc(o_ps, 1)

            def o_statistics(b):
                pe.wait_ge(osq_made, b + 1)
                if b:
                    pe.wait_ge(ozl_made, 1)
                for e in range(2):
                    x = nc.tensor.matmul(ps[:, 6 - 2 * b + e], ones[:], osq[:, 2 * e:2 * e + 2].rearrange("p h t -> p (h t)"),
                                         start=True, stop=True)
                x.then_inc(ostat_ps, 1)

            tasks = {1: (o_mm, 0), 2: (o_statistics, 0), 3: (o_mm, 1), 4: (o_statistics, 1)}
            for c in range(KC):
                g = G_PB + c
                free(g)
                unit(PB + 2 * c, ps[:, bank(g), 0:T], u_lat)
                if c == 0:
                    pe.wait_ge(zl_made, 8)
                unit(PB + 2 * c + 1, ps[:, bank(g) + 1, 0:T], lambda k: (zh[:, k], zl[:, k]))
                while queue:
                    level_mm(*queue.pop(0))
                if c in tasks:
                    f, b = tasks[c]
                    f(b)
            pe.wait_ge(ozl_made, 2)
            for c in range(KC):
                g = G_PA + c
                free(g)
                unit(PA + c, ps[:, bank(g), 0:T], lambda k: (ozh[:, k], ozl[:, k]))
            for c in range(KC):
                g = G_WO + c
                free(g)
                unit(WO + c, ps[:, bank(g), 0:T], lambda k: (yh[:, k], yl[:, k]), need=0 if c == 0 else None,
                     made=yl_made)
            statistics(3, T, 2 * T)
            up_body(UP2, G_UP2, 0, 0, T, u_lat, need=24)
            with pe.Fori(0, 10) as i:
                up_body(UP2 + 4, G_UP2 + 2, i, 4, T, u_lat)
            down_body(DOWN2, down_units(), G_DOWN2, 22, lambda k: (act2_h[:, k], act2_l[:, k]),
                      lambda b: ps[:, b, 0:T])
            statistics(4, T, 2 * T)


def _units(w):
    k, n = w.shape
    return np.ascontiguousarray(w.reshape(k // P, P, n // P, P).transpose(2, 1, 0, 3))


def _columns(x):
    return x.reshape(-1, P).T


def kernel(**inputs):
    import concourse.bacc as _bacc
    from concourse.bass_utils import run_bass_kernel_spmd as _run

    a = {k: np.asarray(x) for k, x in inputs.items()}
    nc = _bacc.Bacc("TRN2", target_bir_lowering=False, num_devices=1)

    def tokens(x):
        return x.reshape(T, KC, P).transpose(2, 1, 0)

    def pairs(w):
        u = _units(w)
        return u.reshape(2, FC, P, KC, P).transpose(1, 0, 2, 3, 4).reshape(2 * FC, P, KC, P)

    w_in = a["w_in"][0]
    level = np.arange(P)
    masks = np.zeros((P, 7, P), np.float32)
    for i in range(7):
        m = 1 << i
        same = (level[:, None] // (2 * m)) == (level[None, :] // (2 * m))
        masks[:, i] = same & ((level[:, None] // m) != (level[None, :] // m))
    arrays = {
        "x": tokens(a["x"][0]),
        "ctx": tokens(a["ctx"][0]),
        "cvec": np.stack([_columns(a["c_ctx"]), _columns(a["c"][0])], axis=2),
        "vecs": np.concatenate(
            [_columns(a[n].reshape(-1)) for n in ("norm_ffn1", "norm_mix", "norm_ffn2", "final_norm", "b_ada",
                                                  "b_gate", "lb_logits", "hgrn_norm", "b_dw", "conv_ln_g",
                                                  "conv_ln_b")], axis=1),
        "wdw": a["w_dw"][0].reshape(TAPS, KC, P).transpose(2, 0, 1),
        "masks": masks,
        "ident": np.eye(P, dtype=np.float32),
        "c_rows": np.stack([a["c_ctx"], a["c"][0]])[None],
        "ident0": np.eye(2, dtype=np.float32),
        "ada0": a["w_ada"][0][:, :ADA_PE * P].reshape(KC, P, ADA_GROUPS, 4 * P).transpose(1, 2, 0, 3),
        "ada": a["w_ada"][0][:, ADA_PE * P:].T.reshape(ADA - ADA_PE, P, D),
        "up1": pairs(a["w_ffn1_up"][0]),
        "down1": _units(a["w_ffn1_down"][0]),
        "w_in": _units(w_in),
        "w_v": w_in[:, 3 * D:4 * D].reshape(4, 2, P, 2, 512).transpose(3, 0, 2, 1, 4),
        "gate": _units(a["w_gate"][0]),
        "proj_a": _units(a["w_proj_a"][0]),
        "proj_b": _units(a["w_proj_b"][0]),
        "w_o": _units(a["w_o"][0]),
        "up2": pairs(a["w_ffn2_up"][0]),
        "down2": _units(a["w_ffn2_down"][0]),
    }
    arrays = {f"{k}_dram": np.ascontiguousarray(x) for k, x in arrays.items()}
    d = {k[:-5]: nc.dram_tensor(k, x.shape, mybir.dt.from_np(x.dtype), kind="ExternalInput").ap()
         for k, x in arrays.items()}
    d["out"] = nc.dram_tensor("out_dram", (KC, P, T), F32, kind="ExternalOutput").ap()
    layer(nc, d)
    r = _run(nc, [arrays], core_ids=[0])
    return r.results[0]["out_dram"].transpose(2, 0, 1).reshape(1, T, D)
```

```python
from contextlib import ExitStack

import numpy as np

import concourse.bass as bass
from concourse import mybir

F32 = mybir.dt.float32
F32R = mybir.dt.float32r
U8 = mybir.dt.uint8
ACT = mybir.ActivationFunctionType
ALU = mybir.AluOpType
AX = mybir.AxisListType

P = 128
D = 1024
KC = D // P
T = 256
F = 2816
FC = F // P
HEADS = 8
TAPS = 31
PAD = TAPS // 2
GLUW = T + 2 * PAD
ADA = 72
EPS = 1e-6
HG = 4
SUMS = (0, 1, 3, 4)

V_N1, V_NM, V_N2, V_NF = 0, 8, 16, 24
V_BADA, V_BGATE, V_LB, V_HN = 32, 104, 120, 152
V_BDW, V_LNG, V_LNB, V_END = 153, 161, 169, 177

UP1, DOWN1, GLU, VV, ZZ, QQ, GO, GA, PB, PA, WO, UP2, DOWN2, UNITS = (
    0, 44, 68, 84, 92, 108, 116, 124, 132, 148, 156, 164, 208, 232)
(G_UP1, G_DOWN1, G_GLU, G_V, G_Z, G_Q, G_GO, G_GA, G_PB, G_PA, G_WO, G_UP2, G_DOWN2) = (
    0, 22, 30, 38, 40, 56, 64, 72, 80, 88, 96, 104, 126)
DOWN_K = (8, 8, 6)
ADA_FIRST = 16
ADA_PE = 12
ADA_GROUPS = ADA_PE // 4
ADA_UP = 44


def down_units():
    for c in range(KC):
        k0 = 0
        for k in DOWN_K:
            yield c, k0, k
            k0 += k


def ada_beside(c):
    a = ADA_FIRST + ADA_UP + c + c // 2
    return range(a, a + 1 + c % 2)


def ahead(units, after):
    ks = [k for _, _, k in units] + after
    return ks[2:len(units) + 2]


GLU_STEPS, V_STEPS, Z_FIRST, Z_STEPS = 4, (48, 46), 14, (8,) * 12 + (4,) * 4
MOD_FIRST = 2
SPLIT_POOL = (VV, QQ)


def layer(nc, d):
    with ExitStack() as ctx:
        def sem(name):
            return ctx.enter_context(nc.semaphore(name))

        base = (nc.sbuf_base + 31) // 32 * 32
        slab = ctx.enter_context(nc.sbuf_tensor("slab", [P, (nc.sbuf_usable_end - base) // 4 - 16], F32))

        def at(name, shape, offset, dt=F32):
            return nc.alloc_sbuf_tensor_at(name, [P, *shape], dt, offset=base + offset)

        KB = 1024
        h = at("h", [2, KC, T], 0)
        uh = at("uh", [2, KC, T], 16 * KB, F32R)
        ul = at("ul", [2, KC, T], 32 * KB, F32R)
        raw = at("raw", [4, 8, P], 48 * KB)
        wh = at("wh", [4, 8, P], 64 * KB, F32R)
        wl = at("wl", [4, 8, P], 80 * KB, F32R)
        M = 96 * KB
        junk0 = at("junk0", [D], M + 16 * KB)
        c_row = at("c_row", [2, D], M + 72 * KB)
        mrow = at("mrow", [ADA_GROUPS, 4 * P], M + 80 * KB)
        ada0 = at("ada0", [ADA_GROUPS, KC, 4 * P], M + 24 * KB)
        ada_raw = at("ada_raw", [2, D], M + 88 * KB)
        t_first = at("t_first", [2, KC, T], M)
        act_h = at("act_h", [FC, 2, T], M, F32R)
        act_l = at("act_l", [FC, 2, T], M + 44 * KB, F32R)
        act2_h = at("act2_h", [FC, T], M, F32R)
        act2_l = at("act2_l", [FC, T], M + 22 * KB, F32R)
        q = at("q", [HEADS, T], M)
        khat = at("khat", [2, HG, T], M)
        kdec = at("kdec", [2, HEADS, T], M + 8 * KB)
        Q = at("Q", [2, HEADS, T], M + 8 * KB)
        K = at("K", [2, HEADS, T], M + 24 * KB)
        tot1 = [at(f"tot1_{g}", [2, HG, T], M + (40 + 8 * g) * KB) for g in range(2)]
        v = at("v", [4, D], M + 56 * KB)
        state = at("state", [HEADS, 2, P], M + 72 * KB)
        glu = at("glu", [KC, GLUW], M + 72 * KB)
        gout = at("gout", [HEADS, T], M + 80 * KB)
        lnsq = at("lnsq", [KC, T], M + 80 * KB)
        tot2 = at("tot2", [2, 2, HG, T // 2], M + 88 * KB)
        dec = at("dec", [2, 2, T], M + 88 * KB)
        ident = at("ident", [P], M + 92 * KB)
        masks_f = at("masks_f", [7, P], M + 92 * KB + 512)
        zh = at("zh", [KC, T], M + 40 * KB, F32R)
        zl = at("zl", [KC, T], M + 48 * KB, F32R)
        ozh = at("ozh", [HEADS, T], M, F32R)
        ozl = at("ozl", [HEADS, T], M + 88 * KB, F32R)
        yh = at("yh", [KC, T], M + 24 * KB, F32R)
        yl = at("yl", [KC, T], M + 32 * KB, F32R)
        orms = at("orms", [HG, T], M + 24 * KB)
        onorm = at("onorm", [HG, T], M + 28 * KB)
        A = [at("A0", [HG, 2, T], 16 * KB), at("A1", [HG, 2, T], 32 * KB)]
        hb = at("hb", [KC, T], 0)
        yb = at("yb", [KC, T], 0)
        ga = at("ga", [KC, T], M + 56 * KB)
        ta = at("ta", [2, 512], M + 96 * KB)
        tb = at("tb", [2, 512], M + 100 * KB)
        ssq = at("ssq", [512], M + 104 * KB)
        rstd = at("rstd", [512], M + 106 * KB)
        junk = at("junk", [D], M + 104 * KB)
        tot4 = at("tot4", [2, 2, HG, T // 4], M + 104 * KB)
        osq = at("osq", [HG, T], M + 104 * KB)
        S0 = M + 108 * KB
        vecs = at("vecs", [V_END], S0)
        wdw = at("wdw", [TAPS, KC], S0 + 736)
        masks = at("masks", [7, P], S0 + 736, U8)
        mod = at("mod", [ADA, 2], S0 + 1760)
        ones = at("ones", [P], S0 + 2336)
        cvec = at("cvec", [KC, 2], S0 + 2848)
        csil = at("csil", [KC, 2], S0 + 2912)
        ident0 = at("ident0", [2], S0 + 3808)
        dots = at("dots", [12, 2], S0 + 3712)
        scale = at("scale", [3, KC, 2], S0 + 2976)
        half_gate = at("half_gate", [2, KC, 2], S0 + 3168)
        lbt = at("lbt", [6, 16], S0 + 3296)
        eps = at("eps", [1], S0 + 3680)
        ps = ctx.enter_context(nc.psum_tensor("ps", [P, 8, 512], F32))
        csil_all = ps[:, 4:8].rearrange("p (x k) n -> p x (k n)", x=2)

        raw_in = [sem(f"raw_in{i}") for i in range(4)]
        small_in = sem("small_in")
        x_in = sem("x_in")
        ident_in, masks_in = sem("ident_in"), sem("masks_in")
        masks_made = sem("masks_made")
        out_sent = sem("out_sent")
        hi_made = sem("hi_made")
        lo_dve, lo_pool = sem("lo_dve"), sem("lo_pool")
        unit_done = sem("unit_done")
        cvec_in = sem("cvec_in")
        ada0_in = [sem(f"ada0_in{a}") for a in range(2 * ADA_GROUPS)]
        ada_in = [sem("ada_in0"), sem("ada_in1")]
        ada0_done = sem("ada0_done")
        dot_both, dot_made = sem("dot_both"), sem("dot_made")
        dots_read = sem("dots_read")
        c_row_in = sem("c_row_in")
        c_row_made, csil_made = sem("c_row_made"), sem("csil_made")
        csil_ps = sem("csil_ps")
        ada0_ps = sem("ada0_ps")
        mrow_made = sem("mrow_made")
        bank_read = sem("bank_read")
        act_made = sem("act_made")
        acth_made, actl_made = sem("acth_made"), sem("actl_made")
        ready = sem("ready")
        logits_made = sem("logits_made")
        exp_made = sem("exp_made")
        chain = sem("chain")
        sq_made, ssq_made = sem("sq_made"), sem("ssq_made")
        stat_made = sem("stat_made")
        rms_made, rstd_made = sem("rms_made"), sem("rstd_made")
        tf_made = sem("tf_made")
        uf_act = sem("uf_act")
        uf_made = sem("uf_made")
        uh_made, ul_made = sem("uh_made"), sem("ul_made")
        lat_ps, lat_added = sem("lat_ps"), sem("lat_added")
        con_square = sem("con_square")
        out_made = sem("out_made")
        conv_step = sem("conv_step")
        z_step = sem("z_step")
        turned, turned_read = sem("turned"), sem("turned_read")
        state_ps, state_made = sem("state_ps"), sem("state_made")
        ln_dve, ln_ps, ln_act = sem("ln_dve"), sem("ln_ps"), sem("ln_act")
        q_first = sem("q_first")
        level_ps = [sem(f"level_ps{g}") for g in range(2)]
        a_act = [sem(f"a_act{g}") for g in range(2)]
        a_dve = [sem(f"a_dve{g}") for g in range(2)]
        khat_made = [sem(f"khat_made{g}") for g in range(2)]
        q_up = [sem(f"q_up{g}") for g in range(2)]
        k_up = [sem(f"k_up{g}") for g in range(2)]
        tot_up = [sem(f"tot_up{g}") for g in range(2)]
        zs_made, zf_made, zh_made, zl_made = sem("zs_made"), sem("zf_made"), sem("zh_made"), sem("zl_made")
        o_ps, osq_made, ostat_ps, orms_made, of_made, ozh_made, ozl_made = (
            sem("o_ps"), sem("osq_made"), sem("ostat_ps"), sem("orms_made"), sem("of_made"),
            sem("ozh_made"), sem("ozl_made"))
        yf_made, yh_made, yl_made = sem("yf_made"), sem("yh_made"), sem("yl_made")

        block = ctx.enter_context(nc.Block())

        def lo_wait(eng, n, i=0, per=0):
            a, b = SPLIT_POOL
            if n < a:
                eng.wait_ge(lo_dve, n + 1 + per * i)
            elif n < b:
                eng.wait_ge(lo_pool, n + 1 - a + per * i)
            else:
                eng.wait_ge(lo_dve, n + 1 - (b - a) + per * i)

        def bank(g):
            return 2 * (g % 2)

        def acts(g):
            if g < G_DOWN1:
                return g + 1
            if g < G_GLU:
                return 22
            if g < G_PA:
                return g + 1 - 8
            return g + 1 - 24

        def tot_view(gr, m):
            if m == 1:
                return tot1[gr], 0, HG * T, 2 * HG * T
            t, w = (tot2, HG * T) if m.bit_length() % 2 == 0 else (tot4, HG * T // 2)
            return t, gr * w, HG * T // m, 2 * w

        def tot_halves(gr, m):
            t, o, pl, row = tot_view(gr, m)
            n = HG * T // (2 * m)
            t2, o2, pl2, row2 = tot_view(gr, 2 * m)
            return (bass.AP(t, o, [[row, P], [pl, 2], [2, n]]),
                    bass.AP(t, o + 1, [[row, P], [pl, 2], [2, n]]),
                    bass.AP(t2, o2, [[row2, P], [pl2, 2], [1, n]]))

        def tot_pairs(gr, m, swap):
            t, o, pl, row = tot_view(gr, m)
            n = HG * T // (2 * m)
            if swap:
                return bass.AP(t, o + pl + 1, [[row, P], [2, n], [-pl - 1, 2], [0, m]])
            return bass.AP(t, o + 1, [[row, P], [2, n], [pl - 1, 2], [0, m]])

        def pairs(t, gr, m):
            return bass.AP(t, gr * HG * T, [[2 * HEADS * T, P], [2 * m, HG * T // (2 * m)], [HEADS * T + m, 2], [1, m]])

        def q_pairs(gr, m):
            return pairs(Q, gr, m)

        def k_pairs(gr, m):
            return pairs(K, gr, m)

        def operand(t, head, blk, m):
            o = head * T + blk * P
            return bass.AP(t, o, [[2 * HEADS * T, P], [2 * m, P // (2 * m)], [HEADS * T + m, 2], [1, m]])

        def scan_steps(n):
            return {GO: 0, GO + 1: 2}.get(n, 1)

        def o_pair(t, p):
            return t[:, 2 * (p % 2):2 * (p % 2) + 2].rearrange("p h t -> p (h t)")

        @block.sync
        def _(sp):
            def load(n, src, k=8, i=0, per=0, shape=None):
                if n >= 4:
                    lo_wait(sp, n - 4, i, per)
                dst = raw[:, n % 4, 0:k]
                if shape:
                    dst = dst.rearrange("p k c -> p (k c)").rearrange("p (a b) -> p a b", a=shape)
                sp.dma_start(dst, src).then_inc(raw_in[n % 4], 16)

            def load_first(g, half):
                k = slice(4 * half, 4 * half + 4)
                sp.dma_start(ada0[:, g, k], d["ada0"][:, g, k]).then_inc(ada0_in[2 * g + half], 16)

            def load_ada(a, src, i=0, per=0):
                if a >= 2:
                    sp.wait_ge(dot_made, a - 1 + per * i)
                sp.dma_start(ada_raw[:, a % 2], src).then_inc(ada_in[a % 2], 16)

            sp.dma_start(c_row[0:1], d["c_rows"]).then_inc(c_row_in, 16)
            sp.dma_start(cvec[:], d["cvec"]).then_inc(cvec_in, 16)
            sp.dma_start(ident0[0:2], d["ident0"]).then_inc(cvec_in, 16)
            sp.dma_start(h[:, 0], d["ctx"]).then_inc(x_in, 16)
            sp.dma_start(h[:, 1], d["x"]).then_inc(x_in, 16)
            load_first(0, 0)
            load_first(0, 1)
            load_ada(0, d["ada"][0])
            load_first(1, 0)
            load_ada(1, d["ada"][1])
            load_first(1, 1)
            load_first(2, 0)
            load_first(2, 1)
            load_ada(2, d["ada"][2])
            load_ada(3, d["ada"][3])
            sp.dma_start(vecs[:], d["vecs"]).then_inc(small_in, 16)
            sp.dma_start(wdw[:], d["wdw"]).then_inc(small_in, 16)
            for s in range(4):
                load(UP1 + s, d["up1"][s])

            def one(t, at):
                return t[bass.ds(at, 1)].rearrange("o p k c -> (o p) k c")

            for a in (4, 5):
                load_ada(a, d["ada"][a])
            with sp.Fori(0, 10) as i:
                for s in (0, 2):
                    for e in (s, s + 1):
                        load(UP1 + 4 + e, one(d["up1"], 4 * i + (4 + e)), i=i, per=4)
                    for e in (s, s + 1):
                        load_ada(6 + e, d["ada"][bass.ds(4 * i + (6 + e), 1)].rearrange("o p n -> (o p) n"), i, 4)
            for n, (c, k0, k) in enumerate(down_units(), DOWN1):
                load(n, d["down1"][c, :, k0:k0 + k], k)
                if n == DOWN1 + 1:
                    for a in (ADA_UP + 2, ADA_UP + 3):
                        load_ada(a, d["ada"][a])
                if k0 + k == FC:
                    last = ada_beside(c).start - ADA_PE + 2
                    for a in range(ada_beside(c - 1).start - ADA_PE + 2 if c else last - 2, last):
                        load_ada(a, d["ada"][a])
            w_in = d["w_in"]
            for c in range(KC):
                load(GLU + 2 * c, w_in[40 + c])
                load(GLU + 2 * c + 1, w_in[48 + c])
            for j in range(8):
                load(VV + j, d["w_v"][j // 4, j % 4], 8, shape=2)
            sp.dma_start(ident[:], d["ident"]).then_inc(ident_in, 16)
            sp.dma_start(masks_f[:], d["masks"]).then_inc(masks_in, 16)
            for j in range(16):
                load(ZZ + j, w_in[8 + j])
            for j in range(8):
                load(QQ + j, w_in[j])
            for j in range(8):
                load(GO + j, w_in[32 + j])
            for c in range(KC):
                load(GA + c, d["gate"][c])
            for c in range(KC):
                load(PB + 2 * c, d["gate"][8 + c])
                load(PB + 2 * c + 1, d["proj_b"][c])
            for c in range(KC):
                load(PA + c, d["proj_a"][c])
            for c in range(KC):
                load(WO + c, d["w_o"][c])
            with sp.Fori(0, 11) as i:
                for s in range(4):
                    load(UP2 + s, one(d["up2"], 4 * i + s), i=i, per=4)
            for n, (c, k0, k) in enumerate(down_units(), DOWN2):
                load(n, d["down2"][c, :, k0:k0 + k], k)
            for c in range(KC):
                sp.wait_ge(out_made, c + 1)
                sp.dma_start(d["out"][c], h[:, 1, c]).then_inc(out_sent, 16)
            sp.wait_ge(out_sent, 16 * KC)

        @block.scalar
        def _(act):
            def hi(n, k=8, i=0, per=0):
                act.wait_ge(raw_in[n % 4], 16 * (n // 4 + 1) + 4 * per * i)
                if n >= 4:
                    act.wait_ge(unit_done, n - 3 + per * i)
                nc.scalar.activation(wh[:, n % 4, 0:k], raw[:, n % 4, 0:k], ACT.Copy).then_inc(hi_made, 1)

            def func(g, dst, src, f, i=0, per=0, unit=0, **kw):
                act.wait_ge(unit_done, unit + 1 + 2 * per * i)
                if g >= 2:
                    act.wait_ge(bank_read, g - 1 + per * i)
                nc.scalar.activation(dst, src, f, **kw).then_inc(act_made, 1)

            def square(which, halves, c):
                if c >= 2:
                    act.wait_ge(ssq_made, 7 * SUMS.index(which) + c - 1)
                w = T * (halves.stop - halves.start)
                src = h[:, halves, c]
                dst = ta[:, c % 2, 2 * T - w:2 * T].rearrange("p (a t) -> p a t", t=T)
                nc.scalar.activation(dst, src, ACT.Square).then_inc(sq_made, 1)

            def root(which, a, b, bk=7):
                act.wait_ge(stat_made, which + 1)
                nc.scalar.activation(rstd[:, a:b], ps[:, bk, a:b], ACT.Sqrt, scale=1.0 / D,
                                     bias=eps[:]).then_inc(rms_made, 1)

            def u_hi(which, s, c, shift=0):
                act.wait_ge(uf_made, 8 * which + c + 1)
                if which == 0:
                    act.wait_ge(uf_act, c + 1)
                    nc.scalar.activation(uh[:, :, c], tb[:, c % 2].rearrange("p (a t) -> p a t", t=T),
                                         ACT.Copy).then_inc(uh_made, 1)
                else:
                    nc.scalar.activation(uh[:, s, c], tb[:, c % 2, T:2 * T], ACT.Identity,
                                         bias=mod[:, 8 * shift + c, s:s + 1]).then_inc(uh_made, 1)

            both, lat = slice(0, 2), slice(1, 2)
            def rows(g):
                act.wait_ge(ada0_ps, g + 1)
                nc.scalar.activation(mrow[0:2, g], ps[0:2, g % 2], ACT.Copy).then_inc(mrow_made, 1)

            nc.scalar.preload_act_table(ACT.Silu)
            act.wait_ge(c_row_in, 16)
            nc.scalar.activation(c_row[0:1], c_row[0:1], ACT.Silu).then_inc(c_row_made, 1)
            act.wait_ge(cvec_in, 32)
            nc.scalar.activation(csil[:], cvec[:], ACT.Silu).then_inc(csil_made, 1)
            nc.scalar.preload_act_table(ACT.Sqrt)
            act.wait_ge(ready, 2)
            act.wait_ge(x_in, 32)
            for c in range(KC):
                square(0, both, c)
            root(0, 0, 2 * T, 3)
            rows(0)
            rows(1)
            nc.scalar.preload_act_table(ACT.Silu)
            rows(2)
            hi(UP1)
            hi(UP1 + 1)
            for c in range(KC):
                if c == 0:
                    act.wait_ge(chain, MOD_FIRST)
                else:
                    u_hi(0, None, c - 1)
                if c >= 2:
                    act.wait_ge(ul_made, c - 1)
                nc.scalar.activation(tb[:, c % 2, 0:T], t_first[:, 0, c], ACT.Identity, scale=scale[:, 0, c, 0:1],
                                     bias=mod[:, c, 0:1]).then_inc(uf_act, 1)
            u_hi(0, None, KC - 1)

            def up_body(first, g0, i, per, w):
                for s in range(2):
                    for e in range(2):
                        hi(first + 2 * s + e + 2, i=i, per=per)
                    func(g0 + s, ta[:, s, 0:w], ps[:, 2 * s, 0:w], ACT.Silu, i, 2, first + 2 * s + 1)

            up_body(UP1, G_UP1, 0, 0, 512)
            with act.Fori(0, 10) as i:
                up_body(UP1 + 4, G_UP1 + 2, i, 4, 512)

            def down_body(first, units, after, g0, which, halves):
                units = list(units)
                ks = ahead(units, after)
                split = which == 1
                for e, (c, k0, k) in enumerate(units):
                    if split and e == len(units) - 1:
                        act.wait_ge(lat_added, 1)
                        square(which, lat, c)
                    if e < len(ks):
                        hi(first + e + 2, ks[e])
                    if split and e == 1:
                        act.wait_ge(logits_made, 1)
                        nc.scalar.activation(lbt[:, 1:3], lbt[:, 1:3], ACT.Exp).then_inc(exp_made, 1)
                        nc.scalar.preload_act_table(ACT.Sqrt)
                    if k0 + k == FC and not (split and c == KC - 1):
                        act.wait_ge(bank_read, g0 + c + 1)
                        square(which, halves, c)

            down_body(DOWN1, down_units(), [8, 8], G_DOWN1, 1, both)
            root(1, T, 2 * T, 1)
            for c in range(KC):
                u_hi(1, 1, c, 3)
                if c == 3:
                    act.wait_ge(bank_read, G_GLU)
                    nc.scalar.activation(ta[:, 1, 0:T], h[:, 0, KC - 1], ACT.Square).then_inc(con_square, 1)
            root(2, 0, T, 5)
            for c in range(KC):
                hi(GLU + 2 * c + 2)
                hi(GLU + 2 * c + 3)
                g = G_GLU + c
                func(g, ta[:, c % 2, 0:T], ps[:, bank(g) + 1, 0:T], ACT.Sigmoid, unit=GLU + 2 * c + 1)
                u_hi(2, 0, c, 3)
            for c in range(2):
                for j in range(4):
                    hi(VV + 4 * c + j + 2)
                act.wait_ge(unit_done, VV + 4 * c + 4)
                for b in (0, 1):
                    x = nc.scalar.activation(v[:, b, 512 * c:512 * c + 512], ps[:, (4 - 4 * c) + b], ACT.Copy)
                x.then_inc(act_made, 1)
            for j in range(16):
                hi(ZZ + j + 2)
                g = G_Z + j
                func(g, ta[:, j % 2], ps[:, bank(g)], ACT.Sigmoid, unit=ZZ + j)

            def state_copy(j):
                act.wait_ge(state_ps, j + 1)
                nc.scalar.activation(state[:, j], ps[:, 5, 0:2 * P].rearrange("p (a e) -> p a e", a=2), ACT.Copy,
                                     scale=-1.0).then_inc(state_made, 1)

            for j in range(8):
                hi(QQ + j + 2)
                g = G_Q + j
                func(g, ta[:, j % 2, 0:T], ps[:, bank(g), 0:T], ACT.Sigmoid, unit=QQ + j)
                act.wait_ge(turned, j + 1)
                if j >= 2:
                    act.wait_ge(state_ps, j - 1)
                nc.scalar.activation(tb[:, j % 2], ps[:, 4], ACT.Copy).then_inc(turned_read, 1)
                if j:
                    state_copy(j - 1)
                if j == 3:
                    act.wait_ge(ln_dve, 3)
                    nc.scalar.activation(lnsq[:], hb[:], ACT.Square).then_inc(ln_act, 1)
                if j == 6:
                    act.wait_ge(ln_ps, 2)
                    nc.scalar.activation(rstd[:, T:2 * T], ps[:, 7, 0:T], ACT.Sqrt, scale=1.0 / D,
                                         bias=eps[:]).then_inc(ln_act, 1)
            def a_copy(gr, level):
                act.wait_ge(level_ps[gr], level + 1)
                x = ps[:, 4 + 2 * gr:6 + 2 * gr].rearrange("p a (h b t) -> p (a h) b t", h=2, b=2)
                for b in range(2):
                    c = b if level == 0 else 1 - b
                    y = nc.scalar.activation(A[gr][:, :, b, P * c:P * c + P], x[:, :, b], ACT.Copy)
                y.then_inc(a_act[gr], 1)

            def keys(gr, level):
                m = 1 << (level - 1)
                act.wait_ge(level_ps[gr], level)
                if level > 1:
                    act.wait_ge(k_up[gr], level - 1)
                nc.scalar.activation(khat[:, gr].rearrange("p h t -> p (h t)").rearrange(
                    "p (n a m) -> p n a m", a=2, m=m), k_pairs(gr, m), ACT.Copy).then_inc(khat_made[gr], 1)

            def scan_step(gr, level):
                if level == 0:
                    a_copy(gr, 0)
                if level < 7:
                    keys(gr, level + 1)
                if level == 8:
                    a_copy(gr, 8)

            def z_sigmoid(c):
                if c == 0:
                    act.wait_ge(ln_dve, 8)
                if c >= 2:
                    act.wait_ge(zf_made, c - 1)
                nc.scalar.activation(tb[:, c % 2, 0:T], hb[:, c], ACT.Sigmoid, scale=vecs[:, V_LNG + c:V_LNG + c + 1],
                                     bias=vecs[:, V_LNB + c:V_LNB + c + 1]).then_inc(zs_made, 1)

            def z_act(s):
                if s == 0:
                    z_sigmoid(0)
                if 1 <= s <= KC:
                    act.wait_ge(zf_made, s)
                    nc.scalar.activation(zh[:, s - 1], tb[:, (s - 1) % 2, T:2 * T], ACT.Copy).then_inc(zh_made, 1)
                if s + 1 < KC:
                    z_sigmoid(s + 1)

            queue = [(gr, level) for level in range(9) for gr in range(2)]
            for j in range(8):
                hi(GO + j + 2)
                g = G_GO + j
                func(g, ta[:, j % 2, 0:T], ps[:, bank(g), 0:T], ACT.Sigmoid, unit=GO + j)
                if j == 0:
                    state_copy(7)
                if j >= 4:
                    z_act(j - 4)
                for _ in range(scan_steps(GO + j)):
                    scan_step(*queue.pop(0))
            for j in range(8):
                hi(GA + j + 2)
                g = G_GA + j
                func(g, ta[:, j % 2, 0:T], ps[:, bank(g), 0:T], ACT.Sigmoid, unit=GA + j,
                     bias=vecs[:, V_BGATE + j:V_BGATE + j + 1])
                z_act(j + 4)
                scan_step(*queue.pop(0))

            def o_square(p):
                act.wait_ge(o_ps, p + 1)
                if p == 0:
                    act.wait_ge(tot_up[0], 7)
                    act.wait_ge(tot_up[1], 7)
                if p >= 2:
                    act.wait_ge(ostat_ps, p - 1)
                nc.scalar.activation(o_pair(osq, p), ps[:, 4 + p], ACT.Square).then_inc(osq_made, 1)

            def o_root(p):
                act.wait_ge(ostat_ps, p + 1)
                if p >= 2:
                    act.wait_ge(of_made, p - 1)
                nc.scalar.activation(o_pair(orms, p), ps[:, 2 + p % 2], ACT.Sqrt, scale=1.0 / P,
                                     bias=eps[:]).then_inc(orms_made, 1)

            def o_hi(p):
                act.wait_ge(of_made, p + 1)
                nc.scalar.activation(ozh[:, 2 * p:2 * p + 2], onorm[:, 2 * (p % 2):2 * (p % 2) + 2],
                                     ACT.Copy).then_inc(ozh_made, 1)

            for c in range(KC):
                hi(PB + 2 * c + 2)
                hi(PB + 2 * c + 3)
                g = G_PB + c
                func(g, ta[:, c % 2, 0:T], ps[:, g % 2, 0:T], ACT.Sigmoid, unit=PB + 2 * c + 1,
                     bias=vecs[:, V_BGATE + 8 + c:V_BGATE + 9 + c])
                while queue:
                    scan_step(*queue.pop(0))
                for f, lag in ((o_hi, 3), (o_root, 1), (o_square, 0)):
                    if 0 <= c - lag < 4:
                        f(c - lag)
            for c in range(KC):
                hi(PA + c + 2)
                act.wait_ge(yf_made, c + 1)
                nc.scalar.activation(yh[:, c], tb[:, c % 2, 0:T], ACT.Copy).then_inc(yh_made, 1)
            nc.scalar.preload_act_table(ACT.Sqrt)
            for c in range(KC):
                hi(WO + c + 2)
                act.wait_ge(bank_read, G_WO + c + 1)
                square(3, lat, c)
            root(3, T, 2 * T)
            for c in range(KC):
                u_hi(3, 1, c, 6)
            nc.scalar.preload_act_table(ACT.Silu)
            with act.Fori(0, 11) as i:
                up_body(UP2, G_UP2, i, 4, T)
            nc.scalar.preload_act_table(ACT.Sqrt)
            down_body(DOWN2, down_units(), [], G_DOWN2, 4, lat)
            root(4, T, 2 * T)

        @block.gpsimd
        def _(pool):
            nc.gpsimd.memset(ones[:], 1.0).then_inc(ready, 1)
            nc.gpsimd.memset(eps[:], EPS).then_inc(ready, 1)

            pool.wait_ge(unit_done, GLU)
            pool.wait_ge(dot_made, ADA - ADA_PE)
            nc.gpsimd.memset(glu[:, :, 0:PAD], 0.0)
            nc.gpsimd.memset(glu[:, :, PAD + T:GLUW], 0.0).then_inc(ready, 1)
            nc.gpsimd.memset(dec[:, 0, :, T - 1:T], 1.0)
            nc.gpsimd.memset(dec[:, 1, :, 0:1], 1.0).then_inc(ready, 1)
            for n in range(*SPLIT_POOL):
                pool.wait_ge(hi_made, n + 1)
                nc.gpsimd.tensor_tensor(wl[:, n % 4], raw[:, n % 4], wh[:, n % 4].bitcast(F32),
                                        ALU.subtract).then_inc(lo_pool, 1)

            pool.wait_ge(conv_step, KC * TAPS)
            pool.wait_ge(masks_in, 16)
            nc.gpsimd.tensor_copy(masks[:], masks_f[:]).then_inc(masks_made, 1)
            pool.wait_ge(masks_made, 1)
            for level in range(1, 8):
                m = 1 << (level - 1)
                for gr in range(2):
                    if level == 1:
                        pool.wait_ge(q_first, gr + 1)
                    pool.wait_ge(khat_made[gr], level)
                    if level > 1:
                        pool.wait_ge(tot_up[gr], level - 1)
                        pool.wait_ge(k_up[gr], level - 1)
                        pool.wait_ge(q_up[gr], level - 1)
                    tk = tot_pairs(gr, m, swap=True)
                    x = k_pairs(gr, m)
                    nc.gpsimd.tensor_tensor(x, x, tk, ALU.mult).then_inc(k_up[gr], 1)
                    even, odd, dst = tot_halves(gr, m)
                    nc.gpsimd.tensor_tensor(dst, even, odd, ALU.mult).then_inc(tot_up[gr], 1)

        @block.vector
        def _(dve):
            links = [0]

            def link(ins):
                links[0] += 1
                ins.then_inc(chain, 1)
                dve.wait_ge(chain, links[0])

            def lo(n, k=8, i=0, per=0):
                dve.wait_ge(hi_made, n + 1 + per * i)
                nc.vector.tensor_tensor(wl[:, n % 4, 0:k], raw[:, n % 4, 0:k], wh[:, n % 4, 0:k].bitcast(F32),
                                        ALU.subtract).then_inc(lo_dve, 1)

            def col(o):
                return vecs[:, o:o + 1]

            def gain(which, m, norm, w=0):
                g = vecs[:, norm:norm + 8].unsqueeze(2).to_broadcast([P, KC, 2 - w])
                link(nc.vector.scalar_tensor_tensor(scale[:, which, :, w:2], mod[:, 8 * m:8 * m + 8, w:2], 1.0, g,
                                                    ALU.add, ALU.mult))

            def half(which, m, w=0):
                link(nc.vector.tensor_scalar(half_gate[:, which, :, w:2], mod[:, 8 * m:8 * m + 8, w:2], 0.5, None,
                                             ALU.mult))

            def dot(a, slot, ways, i=0, per=0, terms=junk):
                dve.wait_ge(ada_in[a % 2], 16 * (a // 2 + 1) + 8 * per * i)
                if a:
                    dve.wait_ge(dot_made, a + per * i)
                src = ada_raw[:, a % 2]
                if ways == 2:
                    nc.vector.tensor_tensor_reduce(out=terms[:], in0=src, in1=csil_all[:, 0], scale=1.0, scalar=0.0,
                                                   op0=ALU.mult, op1=ALU.add,
                                                   accum_out=dots[:, slot, 0:1]).then_inc(dot_both, 1)
                    dve.wait_ge(dot_both, a + 1 + per * i)
                nc.vector.tensor_tensor_reduce(out=src, in0=src, in1=csil_all[:, 1], scale=1.0, scalar=0.0,
                                               op0=ALU.mult, op1=ALU.add,
                                               accum_out=dots[:, slot, 1:2]).then_inc(dot_made, 1)

            def add_bias(a, n, ways, i=0, per=0, k=0):
                dve.wait_ge(dot_made, a + n + per * i)
                if per:
                    to = mod[:, bass.ds(per * i + (ADA_PE + a), n), 2 - ways:2]
                    bias = vecs[:, bass.ds(per * i + (V_BADA + ADA_PE + a), n)]
                else:
                    to = mod[:, ADA_PE + a:ADA_PE + a + n, 2 - ways:2]
                    bias = vecs[:, V_BADA + ADA_PE + a:V_BADA + ADA_PE + a + n]
                nc.vector.tensor_tensor(to, dots[:, 0:n, 2 - ways:2], bias.unsqueeze(2).to_broadcast([P, n, ways]),
                                        ALU.add).then_inc(dots_read, 1)
                dve.wait_ge(dots_read, k + 1 + i)

            def add_squares(which, w, c):
                n = 7 * SUMS.index(which) + c
                a, b = 2 * T - w, 2 * T
                dve.wait_ge(sq_made, 8 * SUMS.index(which) + c + 1)
                if c:
                    dve.wait_ge(ssq_made, n)
                    nc.vector.tensor_tensor(ssq[:, a:b], ssq[:, a:b], ta[:, c % 2, a:b], ALU.add).then_inc(ssq_made, 1)
                else:
                    nc.vector.tensor_copy(ssq[:, a:b], ta[:, 0, a:b]).then_inc(ssq_made, 1)

            def invert(which, a, b):
                dve.wait_ge(rms_made, which + 1)
                nc.vector.reciprocal(rstd[:, a:b], rstd[:, a:b]).then_inc(rstd_made, 1)
                dve.wait_ge(rstd_made, which + 1)

            def normed(which, s, c, sc):
                if c >= 2:
                    dve.wait_ge(ul_made, 8 * which + c - 1)
                nc.vector.scalar_tensor_tensor(tb[:, c % 2, T:2 * T], h[:, s, c], scale[:, sc, c, s:s + 1],
                                               rstd[:, s * T:s * T + T], ALU.mult, ALU.mult).then_inc(uf_made, 1)

            def u_lo(which, s, c, shift):
                dve.wait_ge(uh_made, 8 * which + c + 1)
                nc.vector.scalar_tensor_tensor(ul[:, s, c], tb[:, c % 2, T:2 * T], mod[:, 8 * shift + c, s:s + 1],
                                               uh[:, s, c].bitcast(F32), ALU.add, ALU.subtract).then_inc(ul_made, 1)

            both, lat = slice(0, 2), slice(1, 2)
            for c in range(KC - 1):
                add_squares(0, 2 * T, c)
            invert(0, 0, 2 * T)
            for c in range(KC):
                nc.vector.tensor_tensor(t_first[:, :, c], h[:, :, c], rstd[:].rearrange("p (a t) -> p a t", t=T),
                                        ALU.mult).then_inc(tf_made, 1)
                if c == 1:
                    dve.wait_ge(csil_ps, 1)
                if c in (1, 4):
                    dot(c // 3, c // 3, 2, terms=junk0)
            dot(2, 2, 2, terms=junk0)
            dot(3, 3, 2, terms=junk0)
            dve.wait_ge(small_in, 32)
            add_bias(0, 4, 2)
            lo(UP1)
            dve.wait_ge(ada0_done, ADA_GROUPS)
            bias = vecs[:, V_BADA:V_BADA + ADA_PE].unsqueeze(2).to_broadcast([P, ADA_PE, 2])
            link(nc.vector.tensor_tensor(mod[:, 0:ADA_PE], ps[:, 2, 0:2 * ADA_PE].rearrange(
                "p (a t) -> p a t", t=2), bias, ALU.add))
            gain(0, 1, V_N1)
            assert links[0] == MOD_FIRST
            dve.wait_ge(tf_made, KC)
            for c in range(KC + 1):
                if c < KC:
                    if c >= 2:
                        dve.wait_ge(ul_made, c - 1)
                    nc.vector.tensor_scalar(tb[:, c % 2, T:2 * T], t_first[:, 1, c], scale[:, 0, c, 1:2],
                                            mod[:, c, 1:2], ALU.mult, ALU.add).then_inc(uf_made, 1)
                if c:
                    dve.wait_ge(uh_made, c)
                    nc.vector.tensor_tensor(ul[:, :, c - 1], tb[:, (c - 1) % 2].rearrange("p (a t) -> p a t", t=T),
                                            uh[:, :, c - 1].bitcast(F32), ALU.subtract).then_inc(ul_made, 1)
                if c == 1:
                    lo(UP1 + 1)

            def up_body(first, g0, j0, i, per, w, ah, al, js, after=None):
                for s in range(2):
                    for e in range(2):
                        lo(first + 2 * s + e + 2, i=i, per=per)
                    g = g0 + s
                    dve.wait_ge(act_made, acts(g) + 2 * i)
                    nc.vector.tensor_tensor(tb[:, s, 0:w], ta[:, s, 0:w], ps[:, 2 * s + 1, 0:w],
                                            ALU.mult).then_inc(bank_read, 1)
                    dve.wait_ge(bank_read, g + 1 + 2 * i)
                    j = js + j0 + s
                    at_j = j0 + s + 2 * i
                    hj = ah[:, bass.ds(at_j, 1)] if per else ah[:, at_j:at_j + 1]
                    lj = al[:, bass.ds(at_j, 1)] if per else al[:, at_j:at_j + 1]
                    f = tb[:, s, 0:w].unsqueeze(1)
                    nc.vector.tensor_copy(hj, f).then_inc(acth_made, 1)
                    dve.wait_ge(acth_made, j + 1 + 2 * i)
                    nc.vector.tensor_tensor(lj, f, hj.bitcast(F32), ALU.subtract).then_inc(actl_made, 1)
                    if after:
                        after(s)

            ah, al = (x[:].rearrange("p f a t -> p f (a t)") for x in (act_h, act_l))
            def dots_beside(a, k, ways, i=0, per=0):
                def after(s):
                    dot(a + 2 * s, 2 * s, ways, i, per)
                    dot(a + 2 * s + 1, 2 * s + 1, ways, i, per)
                    if s:
                        add_bias(a, 4, ways, i, per, k)
                return after

            up_body(UP1, G_UP1, 0, 0, 0, 512, ah, al, 0, dots_beside(4, 1, 2))
            with dve.Fori(0, 5) as i:
                up_body(UP1 + 4, G_UP1 + 2, 2, i, 4, 512, ah, al, 0, dots_beside(8, 2, 2, i, 4))
            with dve.Fori(0, 5) as i:
                up_body(UP1 + 24, G_UP1 + 12, 12, i, 4, 512, ah, al, 0, dots_beside(28, 7, 1, i, 4))
            def first_gates_and_bounds():
                half(0, 2)
                gain(1, 4, V_NM)
                l0, l1 = vecs[:, V_LB:V_LB + 16], vecs[:, V_LB + 16:V_LB + 32]
                link(nc.vector.tensor_tensor(lbt[:, 0], l0, l1, ALU.max))
                nc.vector.tensor_tensor(lbt[:, 1], l0, lbt[:, 0], ALU.subtract)
                nc.vector.tensor_tensor(lbt[:, 2], l1, lbt[:, 0], ALU.subtract).then_inc(logits_made, 1)
                dve.wait_ge(exp_made, 1)
                link(nc.vector.tensor_tensor(lbt[:, 3], lbt[:, 1], lbt[:, 2], ALU.add))
                link(nc.vector.reciprocal(lbt[:, 0], lbt[:, 3]))
                link(nc.vector.tensor_tensor(lbt[:, 4], lbt[:, 1], lbt[:, 0], ALU.mult))
                link(nc.vector.tensor_scalar(lbt[:, 5], lbt[:, 4], -1.0, 1.0, ALU.mult, ALU.add))

            def down_body(first, units, after, g0, gates, which, halves):
                units = list(units)
                w = T * (halves.stop - halves.start)
                ks = ahead(units, after)
                for e in range(len(units)):
                    c, k0, k = units[e]
                    if which == 1 and e == len(units) - 1:
                        dve.wait_ge(lat_ps, 1)
                        add_product(c, bank(g0 + c), gates, 1, 0).then_inc(lat_added, 1)
                        add_squares(which, 2 * T, c - 1)
                        lo(first + e + 2, ks[e])
                        return
                    if e < len(ks):
                        lo(first + e + 2, ks[e])
                    if which == 1 and e == 1:
                        first_gates_and_bounds()
                    if which == 1 and e == len(units) - 2:
                        for a in ada_beside(c):
                            dot(a - ADA_PE, a - ADA_FIRST - ADA_UP, 1)
                    if k0 + k == FC:
                        down_epilogue(c, first + e, g0, gates, which, halves, w)
                        if g0 == G_DOWN1:
                            for a in ada_beside(c):
                                dot(a - ADA_PE, a - ADA_FIRST - ADA_UP, 1)

            def add_product(c, bk, gates, s, j):
                return nc.vector.scalar_tensor_tensor(h[:, s, c], ps[:, bk, j * T:j * T + T],
                                                      half_gate[:, gates, c, s:s + 1], h[:, s, c], ALU.mult, ALU.add)

            def down_epilogue(c, n, g0, gates, which, halves, w):
                dve.wait_ge(unit_done, n + 1)
                for s in range(halves.start, halves.stop):
                    x = add_product(c, bank(g0 + c), gates, s, s - halves.start)
                x.then_inc(bank_read, 1)
                if c:
                    add_squares(which, w, c - 1)

            down_body(DOWN1, down_units(), [8, 8], G_DOWN1, 0, 1, both)
            invert(1, T, 2 * T)
            for c in range(KC + 1):
                if c < KC:
                    normed(1, 1, c, 1)
                if c:
                    u_lo(1, 1, c - 1, 3)
                if c == 3:
                    dve.wait_ge(unit_done, GLU)
                    add_product(KC - 1, bank(G_DOWN1 + KC - 1) + 1, 0, 0, 0).then_inc(bank_read, 1)
            add_bias(ADA_FIRST + ADA_UP - ADA_PE, ADA - ADA_FIRST - ADA_UP, 1, k=12)
            gain(2, 7, V_N2, 1)
            half(1, 8, 1)
            invert(2, 0, T)
            dve.wait_ge(ready, 4)

            steps = [(c, tap) for c0 in range(0, KC, 2) for tap in range(TAPS) for c in (c0, c0 + 1)]
            done = [0]

            def convolve(count):
                for _ in range(count):
                    if done[0] == len(steps):
                        return
                    c, tap = steps[done[0]]
                    src = glu[:, c, tap:tap + T]
                    w = wdw[:, tap, c:c + 1]
                    if tap == 0:
                        dve.wait_ge(bank_read, G_GLU + c + 1)
                        dve.wait_ge(ul_made, 16 + c + 1)
                        x = nc.vector.tensor_scalar(hb[:, c], src, w, col(V_BDW + c), ALU.mult, ALU.add)
                    else:
                        dve.wait_ge(conv_step, done[0] - 1)
                        x = nc.vector.scalar_tensor_tensor(hb[:, c], src, w, hb[:, c], ALU.mult, ALU.add)
                    x.then_inc(conv_step, 1)
                    done[0] += 1

            for c in range(KC):
                if c < 7:
                    lo(GLU + 2 * c + 2)
                    lo(GLU + 2 * c + 3)
                normed(2, 0, c, 1)
                g = G_GLU + c
                dve.wait_ge(act_made, acts(g))
                nc.vector.tensor_tensor(glu[:, c, PAD:PAD + T], ps[:, bank(g), 0:T], ta[:, c % 2, 0:T],
                                        ALU.mult).then_inc(bank_read, 1)
                u_lo(2, 0, c, 3)
                if c:
                    convolve(GLU_STEPS)

            for c in range(2):
                convolve(V_STEPS[c])
                dve.wait_ge(unit_done, VV + 4 * c + 4)
                for b in (2, 3):
                    x = nc.vector.tensor_copy(v[:, b, 512 * c:512 * c + 512], ps[:, (4 - 4 * c) + b])
                x.then_inc(bank_read, 1)

            convolve(Z_FIRST)
            for j in range(16):
                way, hd = divmod(j, HEADS)
                gr, hl = divmod(hd, HG)
                g = G_Z + j
                lb, oml = lbt[:, 4, j:j + 1], lbt[:, 5, j:j + 1]
                dve.wait_ge(act_made, acts(g))
                f = kdec[:, way, hd]
                nc.vector.tensor_scalar(f, ta[:, j % 2, 0:T], oml, lb, ALU.mult, ALU.add).then_inc(z_step, 1)
                fl = tot1[gr][:, 1 - way, hl]
                nc.vector.tensor_scalar(fl, ta[:, j % 2, T:2 * T], oml, lb, ALU.mult, ALU.add).then_inc(bank_read, 1)
                dve.wait_ge(z_step, 3 * j + 1)
                if way == 0:
                    dst, src = dec[:, 0, j % 2, T - 2::-1], f[:, T - 1:0:-1]
                else:
                    dst, src = dec[:, 1, j % 2, 1:T], f[:, 0:T - 1]
                nc.vector.tensor_tensor_scan(dst, src, src, 1.0, ALU.mult, ALU.bypass).then_inc(z_step, 1)
                dve.wait_ge(bank_read, g + 1)
                nc.vector.tensor_scalar(K[:, way, hd], fl, -1.0, 1.0, ALU.mult, ALU.add)
                dve.wait_ge(z_step, 3 * j + 2)
                nc.vector.scalar_tensor_tensor(f, f, -1.0, dec[:, way, j % 2], ALU.add, ALU.mult).then_inc(z_step, 1)
                if j >= 14:
                    lo(QQ + j - 14)
                convolve(Z_STEPS[j])
            assert done[0] == KC * TAPS

            per_token = hb[:].rearrange("p c t -> p t c")
            bcast = lambda x: x.unsqueeze(1).to_broadcast([P, KC, T])
            dve.wait_ge(conv_step, KC * TAPS)
            for j in range(8):
                lo(QQ + j + 2)
                g = G_Q + j
                dve.wait_ge(act_made, acts(g))
                nc.vector.tensor_tensor(q[:, j], ps[:, bank(g), 0:T], ta[:, j % 2, 0:T], ALU.mult).then_inc(bank_read, 1)
                if j == 0:
                    nc.vector.tensor_reduce(ssq[:, 0:T], per_token, AX.X, ALU.add).then_inc(ln_dve, 1)
                if j == 3:
                    dve.wait_ge(ln_ps, 1)
                    nc.vector.tensor_scalar(rstd[:, 0:T], ps[:, 6, 0:T], 1.0 / D, None, ALU.mult).then_inc(ln_dve, 1)
                    dve.wait_ge(ln_dve, 2)
                    nc.vector.tensor_tensor(hb[:], hb[:], bcast(rstd[:, 0:T]), ALU.subtract).then_inc(ln_dve, 1)
                if j == 4:
                    dve.wait_ge(ln_act, 1)
                    nc.vector.tensor_reduce(ssq[:, T:2 * T], lnsq[:].rearrange("p c t -> p t c"), AX.X,
                                            ALU.add).then_inc(ln_dve, 1)
                if j == 6:
                    dve.wait_ge(ln_act, 2)
                    nc.vector.reciprocal(rstd[:, T:2 * T], rstd[:, T:2 * T]).then_inc(ln_dve, 1)
                    dve.wait_ge(ln_dve, 5)
                    nc.vector.tensor_tensor(hb[:], hb[:], bcast(rstd[:, T:2 * T]), ALU.mult).then_inc(ln_dve, 1)

            dve.wait_ge(bank_read, G_GO)
            dve.wait_ge(turned, HEADS)
            for gr in range(2):
                qv = q[:, HG * gr:HG * gr + HG].rearrange("p h t -> p (h t)").unsqueeze(1).to_broadcast([P, 2, HG * T])
                nc.vector.tensor_tensor(Q[:, :, HG * gr:HG * gr + HG].rearrange("p a h t -> p a (h t)"),
                                        tot1[gr][:].rearrange("p a h t -> p a (h t)"), qv,
                                        ALU.mult).then_inc(q_first, 1)
            nc.vector.tensor_copy(lbt[:, 0], lbt[:, 1]).then_inc(ln_dve, 1)
            dve.wait_ge(ln_dve, 7)
            nc.vector.tensor_copy(lbt[:, 0], lbt[:, 1]).then_inc(ln_dve, 1)

            def level_dve(gr, level):
                m = 1 << (level - 1)
                dve.wait_ge(level_ps[gr], level + 1)
                if level <= 7:
                    if level == 1:
                        dve.wait_ge(masks_made, 1)
                        dve.wait_ge(a_act[gr], 1)
                    else:
                        dve.wait_ge(a_dve[gr], level - 1)
                    diag = bass.AP(A[gr], 0, [[HG * 2 * T, P], [2 * T, HG], [T + P, 2], [1, P]])
                    x = ps[:, 4 + 2 * gr:6 + 2 * gr].rearrange("p a (h b t) -> p (a h) b t", h=2, b=2)
                    mk = bass.AP(masks, (level - 1) * P, [[7 * P, P], [0, HG], [0, 2], [1, P]])
                    nc.vector.copy_predicated(diag, mask=mk, data=x).then_inc(a_dve[gr], 1)
                    if level > 1:
                        dve.wait_ge(tot_up[gr], level - 1)
                        dve.wait_ge(q_up[gr], level - 1)
                    x = q_pairs(gr, m)
                    nc.vector.tensor_tensor(x, x, tot_pairs(gr, m, swap=False), ALU.mult).then_inc(q_up[gr], 1)
                else:
                    dve.wait_ge(tot_up[gr], 7)
                    dve.wait_ge(q_up[gr], 7)
                    x = q_pairs(gr, m)
                    nc.vector.tensor_tensor(x, x, tot_pairs(gr, m, swap=False), ALU.mult).then_inc(q_up[gr], 1)

            def z_dve(s):
                if s == 0:
                    for gr in range(2):
                        dve.wait_ge(k_up[gr], 1)
                        dve.wait_ge(tot_up[gr], 1)
                        dve.wait_ge(q_up[gr], 1)
                if s < KC:
                    if s >= 2:
                        dve.wait_ge(zl_made, s - 1)
                    nc.vector.tensor_scalar(tb[:, s % 2, T:2 * T], hb[:, s], col(V_LNG + s), col(V_LNB + s),
                                            ALU.mult, ALU.add).then_inc(chain, 1)
                    links[0] += 1
                if 1 <= s <= KC:
                    dve.wait_ge(zh_made, s)
                    nc.vector.tensor_tensor(zl[:, s - 1], tb[:, (s - 1) % 2, T:2 * T], zh[:, s - 1].bitcast(F32),
                                            ALU.subtract).then_inc(zl_made, 1)
                if s < KC:
                    dve.wait_ge(chain, links[0])
                    dve.wait_ge(zs_made, s + 1)
                    nc.vector.tensor_tensor(tb[:, s % 2, T:2 * T], tb[:, s % 2, T:2 * T], tb[:, s % 2, 0:T],
                                            ALU.mult).then_inc(zf_made, 1)

            queue = [(gr, level) for level in range(9) for gr in range(2)]

            def scan_step():
                if queue:
                    gr, level = queue.pop(0)
                    if level:
                        level_dve(gr, level)

            for j in range(8):
                lo(GO + j + 2)
                g = G_GO + j
                dve.wait_ge(act_made, acts(g))
                nc.vector.tensor_tensor(gout[:, j], ps[:, bank(g), 0:T], ta[:, j % 2, 0:T], ALU.mult).then_inc(bank_read, 1)
                for _ in range(scan_steps(GO + j)):
                    scan_step()
                if j >= 4:
                    z_dve(j - 4)
            for j in range(8):
                lo(GA + j + 2)
                g = G_GA + j
                dve.wait_ge(act_made, acts(g))
                nc.vector.tensor_copy(ga[:, j], ta[:, j % 2, 0:T]).then_inc(bank_read, 1)
                scan_step()
                z_dve(j + 4)

            def o_dve(p):
                dve.wait_ge(orms_made, p + 1)
                if p >= 2:
                    dve.wait_ge(ozl_made, p - 1)
                f = onorm[:, 2 * (p % 2):2 * (p % 2) + 2]
                link(nc.vector.reciprocal(o_pair(orms, p), o_pair(orms, p)))
                link(nc.vector.tensor_tensor(o_pair(onorm, p), ps[:, 4 + p], o_pair(orms, p), ALU.mult))
                nc.vector.scalar_tensor_tensor(f, f, col(V_HN), gout[:, 2 * p:2 * p + 2],
                                               ALU.mult, ALU.mult).then_inc(of_made, 1)

            def o_lo(p):
                dve.wait_ge(ozh_made, p + 1)
                nc.vector.tensor_tensor(ozl[:, 2 * p:2 * p + 2], onorm[:, 2 * (p % 2):2 * (p % 2) + 2],
                                        ozh[:, 2 * p:2 * p + 2].bitcast(F32), ALU.subtract).then_inc(ozl_made, 1)

            for c in range(KC):
                lo(PB + 2 * c + 2)
                if c == 5:
                    lo(PB + 2 * c + 3)
                if 0 <= c - 2 < 4:
                    o_dve(c - 2)
                if c != 5:
                    lo(PB + 2 * c + 3)
                g = G_PB + c
                dve.wait_ge(act_made, acts(g))
                nc.vector.tensor_tensor(yb[:, c], ps[:, g % 2, T:2 * T], ta[:, c % 2, 0:T], ALU.mult).then_inc(bank_read, 1)
                while queue:
                    scan_step()
                if 0 <= c - 3 < 4:
                    o_lo(c - 3)
            for c in range(KC):
                g = G_PA + c
                dve.wait_ge(unit_done, PA + c + 1)
                nc.vector.tensor_tensor(tb[:, c % 2, 0:T], ps[:, bank(g), 0:T], ga[:, c], ALU.mult).then_inc(bank_read, 1)
                dve.wait_ge(bank_read, g + 1)
                nc.vector.tensor_tensor(tb[:, c % 2, 0:T], tb[:, c % 2, 0:T], yb[:, c], ALU.add).then_inc(yf_made, 1)
                lo(PA + c + 2)
                dve.wait_ge(yh_made, c + 1)
                nc.vector.tensor_tensor(yl[:, c], tb[:, c % 2, 0:T], yh[:, c].bitcast(F32),
                                        ALU.subtract).then_inc(yl_made, 1)
            for c in range(KC):
                g = G_WO + c
                dve.wait_ge(unit_done, WO + c + 1)
                nc.vector.scalar_tensor_tensor(h[:, 1, c], ps[:, bank(g), 0:T], mod[:, 40 + c, 1:2], h[:, 1, c],
                                               ALU.mult, ALU.add).then_inc(bank_read, 1)
                lo(WO + c + 2)
                if c:
                    add_squares(3, T, c - 1)
            invert(3, T, 2 * T)
            for c in range(KC + 1):
                if c < KC:
                    normed(3, 1, c, 2)
                if c:
                    u_lo(3, 1, c - 1, 6)
            with dve.Fori(0, 11) as i:
                up_body(UP2, G_UP2, 0, i, 4, T, act2_h, act2_l, 22)
            down_body(DOWN2, down_units(), [], G_DOWN2, 1, 4, lat)
            invert(4, T, 2 * T)
            for c in range(KC):
                nc.vector.scalar_tensor_tensor(h[:, 1, c], h[:, 1, c], col(V_NF + c), rstd[:, T:2 * T],
                                               ALU.mult, ALU.mult).then_inc(out_made, 1)

        @block.tensor
        def _(pe):
            def three(out, w_hi, w_lo, x_hi, x_lo, start, stop):
                nc.tensor.matmul(out, w_hi, x_hi, start=start, stop=False)
                nc.tensor.matmul(out, w_hi, x_lo, start=False, stop=False)
                return nc.tensor.matmul(out, w_lo, x_hi, start=False, stop=stop)

            def unit(n, out, xs, k0=0, k=8, start=True, stop=True, i=0, per=0, ready_at=None, signal=unit_done):
                lo_wait(pe, n, i, per)
                for j in range(k):
                    if ready_at:
                        pe.wait_ge(ready_at[0], ready_at[1](k0 + j))
                    x = three(out, wh[:, n % 4, j], wl[:, n % 4, j], *xs(k0 + j),
                              start=start and j == 0, stop=stop and j == k - 1)
                if signal is not None:
                    x.then_inc(signal, 1)

            def free(g, i=0, per=0):
                if g >= 2:
                    pe.wait_ge(bank_read, g - 1 + per * i)

            def out512(b):
                return ps[:, b].rearrange("p (a t) -> p a t", a=2)

            u_both = lambda k: (uh[:, :, k], ul[:, :, k])
            u_lat = lambda k: (uh[:, 1, k], ul[:, 1, k])

            def statistics(which, a, b, bk=7):
                n = SUMS.index(which) if which != 2 else SUMS.index(1)
                pe.wait_ge(ssq_made, 7 * n + 7)
                nc.tensor.matmul(ps[:, bk, a:b], ones[:], ssq[:, a:b], start=True, stop=False)
                if which == 2:
                    pe.wait_ge(con_square, 1)
                else:
                    pe.wait_ge(sq_made, 8 * n + 8)
                nc.tensor.matmul(ps[:, bk, a:b], ones[:], ta[:, 1, a:b], start=False, stop=True).then_inc(stat_made, 1)

            pe.wait_ge(ready, 1)
            pe.wait_ge(c_row_made, 1)
            for n in range(4):
                x = nc.tensor.matmul(ps[:, 4 + n], ones[0:1], c_row[0:1].rearrange("p x n -> p (x n)")[
                    :, 512 * n:512 * n + 512], start=True, stop=True)
            x.then_inc(csil_ps, 1)

            def columns(g):
                pe.wait_ge(mrow_made, g + 1)
                for e in range(4):
                    a = 4 * g + e
                    x = nc.tensor.matmul(ps[:, 2, 2 * a:2 * a + 2], mrow[0:2, g, P * e:P * e + P], ident0[0:2],
                                         start=True, stop=True)
                x.then_inc(ada0_done, 1)

            pe.wait_ge(cvec_in, 32)
            pe.wait_ge(csil_made, 1)
            for g in range(ADA_GROUPS):
                if g == 2:
                    pe.wait_ge(mrow_made, 1)
                for k in range(KC):
                    if k % 4 == 0:
                        pe.wait_ge(ada0_in[2 * g + k // 4], 16)
                    if g == 0 and k == 4:
                        statistics(0, 0, 2 * T, 3)
                    x = nc.tensor.matmul(ps[0:2, g % 2], csil[:, k], ada0[:, g, k], start=(k == 0), stop=(k == KC - 1))
                x.then_inc(ada0_ps, 1)
                if g:
                    columns(g - 1)
            columns(2)

            def up_body(first, g0, i, per, w, xs, ready_at=None):
                for s in range(2):
                    g = g0 + s
                    free(g, i, 2)
                    for e in range(2):
                        b = 2 * s + e
                        unit(first + b, out512(b) if w == 512 else ps[:, b, 0:w], xs, i=i, per=per,
                             ready_at=ready_at if b == 0 else None)

            up_body(UP1, G_UP1, 0, 0, 512, u_both, (ul_made, lambda k: k + 1))
            with pe.Fori(0, 10) as i:
                up_body(UP1 + 4, G_UP1 + 2, i, 4, 512, u_both)

            def down_body(first, units, g0, js, xs, view):
                for n, (c, k0, k) in enumerate(units, first):
                    if k0 == 0:
                        free(g0 + c)
                    if c == 0:
                        pe.wait_ge(actl_made, js + k0 + k)
                    unit(n, view(bank(g0 + c)), xs, k0, k, start=(k0 == 0), stop=(k0 + k == FC))

            units = list(down_units())
            down_body(DOWN1, units[:-3], G_DOWN1, 0, lambda k: (act_h[:, k], act_l[:, k]), out512)
            bk = bank(G_DOWN1 + KC - 1)
            free(G_DOWN1 + KC - 1)
            for s in (1, 0):
                for n, (c, k0, k) in enumerate(units[-3:], GLU - 3):
                    if s == 0 and n == GLU - 1:
                        statistics(1, T, 2 * T, 1)
                    unit(n, ps[:, bk + 1 - s, 0:T], lambda j: (act_h[:, j, s], act_l[:, j, s]), k0, k,
                         start=(k0 == 0), stop=(k0 + k == FC), signal=unit_done if s == 0 else lat_ps if n == GLU - 1 else None)
            for c in range(KC):
                g = G_GLU + c
                free(g)
                unit(GLU + 2 * c, ps[:, bank(g), 0:T], u_lat, ready_at=(ul_made, lambda k: 8 + k + 1) if c == 0 else None)
                if c == 0:
                    pe.wait_ge(dot_made, ADA - ADA_PE)
                    statistics(2, 0, T, 5)
                unit(GLU + 2 * c + 1, ps[:, bank(g) + 1, 0:T], u_lat)
            for c in range(2):
                pe.wait_ge(bank_read, G_GLU if c == 0 else G_V)
                for j in range(4):
                    n = VV + 4 * c + j
                    lo_wait(pe, n)
                    w_hi = wh[:, n % 4].rearrange("p k c -> p (k c)")
                    w_lo = wl[:, n % 4].rearrange("p k c -> p (k c)")
                    for e in range(2):
                        k = 2 * j + e
                        if c == 0:
                            pe.wait_ge(ul_made, 16 + k + 1)
                        for b in range(4):
                            uhb = uh[:, b // 2, k, P * (b % 2):P * (b % 2) + P]
                            ulb = ul[:, b // 2, k, P * (b % 2):P * (b % 2) + P]
                            x = three(ps[:, (4 - 4 * c) + b], uhb, ulb, w_hi[:, 512 * e:512 * e + 512],
                                      w_lo[:, 512 * e:512 * e + 512], start=(k == 0), stop=(k == KC - 1))
                    x.then_inc(unit_done, 1)
            for j in range(16):
                g = G_Z + j
                if j == 0:
                    pe.wait_ge(act_made, acts(G_V + 1))
                elif j == 1:
                    pe.wait_ge(bank_read, G_Z)
                else:
                    free(g)
                unit(ZZ + j, out512(bank(g)), u_both)
            pe.wait_ge(ident_in, 16)

            def states(j):
                pe.wait_ge(turned_read, j + 1)
                if j:
                    pe.wait_ge(state_made, j)
                for way in range(2):
                    for b in range(2):
                        x = nc.tensor.matmul(ps[:, 5, way * P:way * P + P],
                                             tb[:, j % 2, (2 * way + b) * P:(2 * way + b) * P + P],
                                             v[:, b, P * j:P * j + P], start=(b == 0), stop=(b == 1))
                x.then_inc(state_ps, 1)

            for j in range(8):
                g = G_Q + j
                free(g)
                unit(QQ + j, ps[:, bank(g), 0:T], u_lat)
                if j == 0:
                    pe.wait_ge(z_step, 48)
                else:
                    pe.wait_ge(turned_read, j)
                for way in range(2):
                    for b in range(2):
                        x = nc.tensor.transpose(ps[:, 4, (2 * way + b) * P:(2 * way + b) * P + P],
                                                kdec[:, way, j, P * b:P * b + P], ident[:])
                x.then_inc(turned, 1)
                if j:
                    states(j - 1)
                if j == 2:
                    pe.wait_ge(ln_dve, 1)
                    nc.tensor.matmul(ps[:, 6, 0:T], ones[:], ssq[:, 0:T], start=True, stop=True).then_inc(ln_ps, 1)
                if j == 5:
                    pe.wait_ge(ln_dve, 4)
                    nc.tensor.matmul(ps[:, 7, 0:T], ones[:], ssq[:, T:2 * T], start=True, stop=True).then_inc(ln_ps, 1)
            def level_mm(gr, level):
                m = 1 << max(level - 1, 0)
                if level == 0:
                    pe.wait_ge(q_first, gr + 1)
                    if gr == 0:
                        pe.wait_ge(state_made, HEADS)
                else:
                    if level == 1:
                        pe.wait_ge(a_act[gr], 1)
                    else:
                        pe.wait_ge(a_dve[gr], level - 1)
                        pe.wait_ge(q_up[gr], level - 1)
                    if level < 8:
                        pe.wait_ge(khat_made[gr], level)
                    else:
                        pe.wait_ge(k_up[gr], 7)
                for hl in range(HG):
                    hd = HG * gr + hl
                    for b in range(2):
                        out = ps[:, 4 + 2 * gr + hl // 2, (hl % 2) * T + b * P:(hl % 2) * T + b * P + P]
                        if level == 0:
                            for way in range(2):
                                x = nc.tensor.matmul(out, K[:, way, hd, P * b:P * b + P], q[:, hd, P * b:P * b + P],
                                                     start=(way == 0), stop=(way == 1))
                        elif level < 8:
                            x = nc.tensor.matmul(out, khat[:, gr, hl, P * b:P * b + P], operand(Q, hd, b, m), start=True, stop=True)
                        else:
                            x = nc.tensor.matmul(out, K[:, b, hd, P * b:P * b + P],
                                                 Q[:, 1 - b, hd, P * (1 - b):P * (1 - b) + P], start=True, stop=True)
                x.then_inc(level_ps[gr], 1)

            queue = [(gr, level) for level in range(9) for gr in range(2)]
            for first, g0 in ((GO, G_GO), (GA, G_GA)):
                for j in range(8):
                    free(g0 + j)
                    unit(first + j, ps[:, bank(g0 + j), 0:T], u_lat)
                    if first == GO and j == 0:
                        states(7)
                        continue
                    for _ in range(scan_steps(first + j)):
                        level_mm(*queue.pop(0))

            def o_mm(p):
                gr = p // 2
                pe.wait_ge(a_act[gr], 2)
                pe.wait_ge(q_up[gr], 8)
                for hd in (2 * p, 2 * p + 1):
                    out = ps[:, 4 + p, (hd % 2) * T:(hd % 2) * T + T]
                    for s in range(2):
                        nc.tensor.matmul(out, v[:, 2 + s, P * hd:P * hd + P], A[gr][:, hd % HG, s], start=(s == 0),
                                         stop=False)
                    nc.tensor.matmul(out, state[:, hd, 0], Q[:, 1, hd], start=False, stop=False)
                    x = nc.tensor.matmul(out, state[:, hd, 1], Q[:, 0, hd], start=False, stop=True)
                x.then_inc(o_ps, 1)

            def o_statistics(p):
                pe.wait_ge(osq_made, p + 1)
                if p >= 2:
                    pe.wait_ge(orms_made, p - 1)
                nc.tensor.matmul(ps[:, 2 + p % 2], ones[:], o_pair(osq, p), start=True, stop=True).then_inc(ostat_ps, 1)

            for c in range(KC):
                g = G_PB + c
                free(g)
                unit(PB + 2 * c, ps[:, g % 2, 0:T], u_lat)
                unit(PB + 2 * c + 1, ps[:, g % 2, T:2 * T], lambda k: (zh[:, k], zl[:, k]),
                     ready_at=(zl_made, lambda k: k + 1) if c == 0 else None)
                while queue:
                    level_mm(*queue.pop(0))
                for f, lag in ((o_statistics, 1), (o_mm, 0)):
                    if 0 <= c - lag < 4:
                        f(c - lag)
            for c in range(KC):
                g = G_PA + c
                free(g)
                unit(PA + c, ps[:, bank(g), 0:T], lambda k: (ozh[:, k], ozl[:, k]),
                     ready_at=(ozl_made, lambda k: k // 2 + 1) if c == 0 else None)
            for c in range(KC):
                g = G_WO + c
                free(g)
                unit(WO + c, ps[:, bank(g), 0:T], lambda k: (yh[:, k], yl[:, k]), 
                     ready_at=(yl_made, lambda k: k + 1) if c == 0 else None)
            statistics(3, T, 2 * T)
            up_body(UP2, G_UP2, 0, 0, T, u_lat, (ul_made, lambda k: 24 + k + 1))
            with pe.Fori(0, 10) as i:
                up_body(UP2 + 4, G_UP2 + 2, i, 4, T, u_lat)
            down_body(DOWN2, down_units(), G_DOWN2, 22, lambda k: (act2_h[:, k], act2_l[:, k]),
                      lambda b: ps[:, b, 0:T])
            statistics(4, T, 2 * T)


def _units(w):
    k, n = w.shape
    return np.ascontiguousarray(w.reshape(k // P, P, n // P, P).transpose(2, 1, 0, 3))


def _columns(x):
    return x.reshape(-1, P).T


def kernel(**inputs):
    import concourse.bacc as _bacc
    from concourse.bass_utils import run_bass_kernel_spmd as _run

    a = {k: np.asarray(x) for k, x in inputs.items()}
    nc = _bacc.Bacc("TRN2", target_bir_lowering=False, num_devices=1)

    def tokens(x):
        return x.reshape(T, KC, P).transpose(2, 1, 0)

    def pairs(w):
        u = _units(w)
        return u.reshape(2, FC, P, KC, P).transpose(1, 0, 2, 3, 4).reshape(2 * FC, P, KC, P)

    w_in = a["w_in"][0]
    level = np.arange(P)
    masks = np.zeros((P, 7, P), np.float32)
    for i in range(7):
        m = 1 << i
        same = (level[:, None] // (2 * m)) == (level[None, :] // (2 * m))
        masks[:, i] = same & ((level[:, None] // m) != (level[None, :] // m))
    arrays = {
        "x": tokens(a["x"][0]),
        "ctx": tokens(a["ctx"][0]),
        "cvec": np.stack([_columns(a["c_ctx"]), _columns(a["c"][0])], axis=2),
        "vecs": np.concatenate(
            [_columns(a[n].reshape(-1)) for n in ("norm_ffn1", "norm_mix", "norm_ffn2", "final_norm", "b_ada",
                                                  "b_gate", "lb_logits", "hgrn_norm", "b_dw", "conv_ln_g",
                                                  "conv_ln_b")], axis=1),
        "wdw": a["w_dw"][0].reshape(TAPS, KC, P).transpose(2, 0, 1),
        "masks": masks,
        "ident": np.eye(P, dtype=np.float32),
        "c_rows": np.stack([a["c_ctx"], a["c"][0]])[None],
        "ident0": np.eye(2, dtype=np.float32),
        "ada0": a["w_ada"][0][:, :ADA_PE * P].reshape(KC, P, ADA_GROUPS, 4 * P).transpose(1, 2, 0, 3),
        "ada": a["w_ada"][0][:, ADA_PE * P:].T.reshape(ADA - ADA_PE, P, D),
        "up1": pairs(a["w_ffn1_up"][0]),
        "down1": _units(a["w_ffn1_down"][0]),
        "w_in": _units(w_in),
        "w_v": w_in[:, 3 * D:4 * D].reshape(4, 2, P, 2, 512).transpose(3, 0, 2, 1, 4),
        "gate": _units(a["w_gate"][0]),
        "proj_a": _units(a["w_proj_a"][0]),
        "proj_b": _units(a["w_proj_b"][0]),
        "w_o": _units(a["w_o"][0]),
        "up2": pairs(a["w_ffn2_up"][0]),
        "down2": _units(a["w_ffn2_down"][0]),
    }
    arrays = {f"{k}_dram": np.ascontiguousarray(x) for k, x in arrays.items()}
    d = {k[:-5]: nc.dram_tensor(k, x.shape, mybir.dt.from_np(x.dtype), kind="ExternalInput").ap()
         for k, x in arrays.items()}
    d["out"] = nc.dram_tensor("out_dram", (KC, P, T), F32, kind="ExternalOutput").ap()
    layer(nc, d)
    r = _run(nc, [arrays], core_ids=[0])
    return r.results[0]["out_dram"].transpose(2, 0, 1).reshape(1, T, D)
```
